# Optimizing a Trainium2 kernel written in Bass

```python
import jax
import jax.numpy as jnp
from jax import lax
import numpy as np

D_MODEL = 1024
BATCH = 1
SEQ = 128
DEPTH = 2
DEC_BATCH = 1
DEC_SEQ = 1024
PAST_LEN = 128

GRID_W = 64
HEAD_DIM = 64
ATT_HEADS = 8
ATT_KV_HEADS = 2
ATT_GROUP = ATT_HEADS // ATT_KV_HEADS
ATT_WIDTH = ATT_HEADS * HEAD_DIM
KV_WIDTH = ATT_KV_HEADS * HEAD_DIM
M_HEADS = 4
M_DIM = 64
M_WIDTH = M_HEADS * M_DIM
G_GROUPS = 4
G_WIDTH = D_MODEL - ATT_WIDTH - M_WIDTH
CHUNK = 128
Q_BLOCK = 128
D_FF = 4 * D_MODEL
ROPE_BASE = 10000.0
EPS = 1e-6
DEEPNORM_ALPHA = (2 * DEPTH) ** 0.25
DEEPNORM_BETA = (8 * DEPTH) ** -0.25
PROJ_SIZES = (ATT_WIDTH, KV_WIDTH, KV_WIDTH, M_WIDTH, M_WIDTH, M_WIDTH, M_WIDTH, 4 * M_HEADS, G_WIDTH, G_WIDTH)
PROJ_WIDTH = ATT_WIDTH + 2 * KV_WIDTH + 4 * M_WIDTH + 4 * M_HEADS + 2 * G_WIDTH

kernel_name = "hybrid_diffusion_prefix_step"

def layer_norm(x, g, b):
    xf = x.astype(jnp.float32)
    mu = jnp.mean(xf, axis=-1, keepdims=True)
    var = jnp.mean(jnp.square(xf - mu), axis=-1, keepdims=True)
    y = (xf - mu) * lax.rsqrt(var + EPS) * g.astype(jnp.float32) + b.astype(jnp.float32)
    return y.astype(x.dtype)

def rms_norm(x, g):
    xf = x.astype(jnp.float32)
    y = xf * lax.rsqrt(jnp.mean(jnp.square(xf), axis=-1, keepdims=True) + EPS) * g.astype(jnp.float32)
    return y.astype(x.dtype)

def rope_1d(x, ang):
    cos = jnp.cos(ang)[None, :, None, :]
    sin = jnp.sin(ang)[None, :, None, :]
    xa, xb = jnp.split(x.astype(jnp.float32), 2, axis=-1)
    return jnp.concatenate([xa * cos - xb * sin, xa * sin + xb * cos], axis=-1).astype(x.dtype)

def axial_rope(x, rows):
    r, cidx = jnp.meshgrid(jnp.arange(rows, dtype=jnp.float32), jnp.arange(GRID_W, dtype=jnp.float32), indexing='ij')
    n_freq = HEAD_DIM // 4
    inv = ROPE_BASE ** (-jnp.arange(n_freq, dtype=jnp.float32) / n_freq)
    ang_r = r.reshape(-1)[:, None] * inv[None, :]
    ang_c = cidx.reshape(-1)[:, None] * inv[None, :]
    half = HEAD_DIM // 2
    return jnp.concatenate([rope_1d(x[..., :half], ang_r), rope_1d(x[..., half:], ang_c)], axis=-1)

def blocked_attention(q, k, v):
    B, T = q.shape[0], q.shape[1]
    nb = T // Q_BLOCK
    qb = q.reshape(B, nb, Q_BLOCK, ATT_KV_HEADS, ATT_GROUP, HEAD_DIM).transpose(1, 0, 2, 3, 4, 5)
    scale = HEAD_DIM ** -0.5

    def one_block(qblk):
        s = jnp.einsum('bqkgd,bskd->bkgqs', qblk, k).astype(jnp.float32) * scale
        p = jax.nn.softmax(s, axis=-1).astype(v.dtype)
        return jnp.einsum('bkgqs,bskd->bqkgd', p, v)

    o = lax.map(one_block, qb)
    return o.transpose(1, 0, 2, 3, 4, 5).reshape(B, T, ATT_WIDTH)

def mlstm_scan(q, k, v, ig, lf, state):
    B, T, H, D = q.shape
    nc = T // CHUNK
    to_c = lambda a: a.reshape(B, nc, CHUNK, H, D).transpose(1, 0, 3, 2, 4)
    to_cg = lambda a: a.reshape(B, nc, CHUNK, H).transpose(1, 0, 3, 2)
    mask = jnp.tril(jnp.ones((CHUNK, CHUNK), dtype=bool))

    def step(carry, inp):
        C, n, m = carry
        qc, kc, vc, ic, fc = inp
        b = jnp.cumsum(fc, axis=-1)
        logw = jnp.where(mask, b[..., :, None] - b[..., None, :] + ic[..., None, :], -jnp.inf)
        m_t = jnp.maximum(b + m[..., None], jnp.max(logw, axis=-1))
        w = jnp.exp(logw - m_t[..., None])
        s = jnp.einsum('bhtd,bhsd->bhts', qc, kc) * w
        inter = jnp.exp(b + m[..., None] - m_t)
        num = jnp.einsum('bhts,bhse->bhte', s, vc) + inter[..., None] * jnp.einsum('bhtd,bhde->bhte', qc, C)
        den = jnp.sum(s, axis=-1) + inter * jnp.einsum('bhtd,bhd->bht', qc, n)
        h = num / jnp.maximum(jnp.abs(den), jnp.exp(-m_t))[..., None]
        m_new = m_t[..., -1]
        decay = jnp.exp(b[..., -1] + m - m_new)
        wk = jnp.exp(b[..., -1:] - b + ic - m_new[..., None])
        C_new = decay[..., None, None] * C + jnp.einsum('bhs,bhsd,bhse->bhde', wk, kc, vc)
        n_new = decay[..., None] * n + jnp.einsum('bhs,bhsd->bhd', wk, kc)
        return (C_new, n_new, m_new), h

    state = tuple(s.astype(jnp.float32) for s in state)
    final, hs = lax.scan(step, state, (to_c(q), to_c(k), to_c(v), to_cg(ig), to_cg(lf)))
    return hs.transpose(1, 0, 3, 2, 4).reshape(B, T, H, D), final

def mlstm_bidir(q, k, v, o_pre, gates, state_f, state_b):
    B, T = q.shape[0], q.shape[1]
    flip = lambda a: jnp.flip(a, axis=1)
    h_f, st_f = mlstm_scan(q, k, v, gates[:, :, 0], jax.nn.log_sigmoid(gates[:, :, 1]), state_f)
    h_b, st_b = mlstm_scan(flip(q), flip(k), flip(v), flip(gates[:, :, 2]),
                           flip(jax.nn.log_sigmoid(gates[:, :, 3])), state_b)
    h = (h_f + flip(h_b)).reshape(B, T, M_WIDTH)
    return jax.nn.sigmoid(o_pre.astype(jnp.float32)) * h, st_f, st_b

def gmlp_spatial(u, v, ln_g, ln_b, ws, bs):
    B, T, _ = v.shape
    vn = layer_norm(v, ln_g, ln_b)
    vr = vn.reshape(B, T // CHUNK, CHUNK, G_GROUPS, G_WIDTH // G_GROUPS)
    s = jnp.einsum('gts,bcsgd->bctgd', ws, vr) + bs.T[None, None, :, :, None]
    return u * s.reshape(B, T, G_WIDTH)

def modulation(cv, w_mod, b_mod):
    return (jax.nn.silu(cv) @ w_mod + b_mod)[:, None, :]

def trunk_layer(x, mod, p, ctx=None):
    (w_in, q_g, k_g, gate_b, gln_g, gln_b, g_ws, g_bs, w_out, ln1_g, ln1_b, w_ff1, w_ff2, ln2_g, ln2_b) = p
    sh1, sc1, g1, sh2, sc2, g2 = jnp.split(mod, 6, axis=-1)
    B, T, _ = x.shape
    h = x * (1 + sc1) + sh1
    z = h @ w_in
    splits = np.cumsum(PROJ_SIZES)[:-1].tolist()
    qa, ka, va, qm, km, vm, om, gm, ug, vg = jnp.split(z, splits, axis=-1)
    qa = rms_norm(qa.reshape(B, T, ATT_HEADS, HEAD_DIM), q_g)
    ka = rms_norm(ka.reshape(B, T, ATT_KV_HEADS, HEAD_DIM), k_g)
    va = va.reshape(B, T, ATT_KV_HEADS, HEAD_DIM)
    qm = qm.reshape(B, T, M_HEADS, M_DIM).astype(jnp.float32)
    km = km.reshape(B, T, M_HEADS, M_DIM).astype(jnp.float32) * (M_DIM ** -0.5)
    vm = vm.reshape(B, T, M_HEADS, M_DIM).astype(jnp.float32)
    gates = gm.reshape(B, T, 4, M_HEADS).astype(jnp.float32) + gate_b.astype(jnp.float32)
    if ctx is None:
        q_att, k_all, v_all = qa, ka, va
        zero = (jnp.zeros((B, M_HEADS, M_DIM, M_DIM), jnp.float32),
                jnp.zeros((B, M_HEADS, M_DIM), jnp.float32),
                jnp.zeros((B, M_HEADS), jnp.float32))
        st_f, st_b = zero, zero
    else:
        k_c, v_c, st_f, st_b = ctx
        rows = T // GRID_W
        q_att = axial_rope(qa, rows)
        k_all = jnp.concatenate([k_c.astype(x.dtype), axial_rope(ka, rows)], axis=1)
        v_all = jnp.concatenate([v_c.astype(x.dtype), va], axis=1)
    att = blocked_attention(q_att, k_all, v_all)
    m_out, st_f_new, st_b_new = mlstm_bidir(qm, km, vm, om, gates, st_f, st_b)
    g_out = gmlp_spatial(ug, vg, gln_g, gln_b, g_ws, g_bs)
    y = jnp.concatenate([att, m_out.astype(x.dtype), g_out], axis=-1) @ w_out
    x = layer_norm(DEEPNORM_ALPHA * x + g1 * y, ln1_g, ln1_b)
    h2 = x * (1 + sc2) + sh2
    f = jnp.square(jax.nn.relu(h2 @ w_ff1)) @ w_ff2
    x = layer_norm(DEEPNORM_ALPHA * x + g2 * f, ln2_g, ln2_b)
    if ctx is None:
        return x, (ka, va, st_f_new, st_b_new)
    return x, None

def setup_inputs(seed: int = 0) -> dict:
    key = jax.random.key(seed)
    ks = jax.random.split(key, 32)
    nrm = lambda k, shape, s: jax.random.normal(k, shape, jnp.float32) * s
    D = D_MODEL
    gate_off = jnp.array([0.0, 3.0, 0.0, 3.0], jnp.float32)[None, :, None]
    return {
        "x_prompt": nrm(ks[0], (BATCH, SEQ, D), 1.0),
        "x_sample": nrm(ks[1], (DEC_BATCH, DEC_SEQ, D), 1.0),
        "c": nrm(ks[2], (DEC_BATCH, D), 1.0),
        "cache_attn_k": nrm(ks[3], (DEC_BATCH, DEPTH, PAST_LEN, ATT_KV_HEADS, HEAD_DIM), 1.0),
        "cache_attn_v": nrm(ks[4], (DEC_BATCH, DEPTH, PAST_LEN, ATT_KV_HEADS, HEAD_DIM), 1.0),
        "state_mlstm_C": nrm(ks[5], (DEC_BATCH, DEPTH, 2, M_HEADS, M_DIM, M_DIM), 0.1),
        "state_mlstm_n": nrm(ks[6], (DEC_BATCH, DEPTH, 2, M_HEADS, M_DIM), 0.1),
        "state_mlstm_m": nrm(ks[7], (DEC_BATCH, DEPTH, 2, M_HEADS), 0.5),
        "c_ctx": nrm(ks[8], (D,), 1.0),
        "w_mod": nrm(ks[9], (DEPTH, D, 6 * D), 0.5 * D ** -0.5),
        "b_mod": nrm(ks[10], (DEPTH, 6 * D), 0.1),
        "w_in": nrm(ks[11], (DEPTH, D, PROJ_WIDTH), D ** -0.5),
        "q_norm_g": 1.0 + nrm(ks[12], (DEPTH, HEAD_DIM), 0.1),
        "k_norm_g": 1.0 + nrm(ks[13], (DEPTH, HEAD_DIM), 0.1),
        "mlstm_gate_b": gate_off + nrm(ks[14], (DEPTH, 4, M_HEADS), 0.3),
        "gmlp_ln_g": 1.0 + nrm(ks[15], (DEPTH, G_WIDTH), 0.1),
        "gmlp_ln_b": nrm(ks[16], (DEPTH, G_WIDTH), 0.02),
        "gmlp_ws": nrm(ks[17], (DEPTH, G_GROUPS, CHUNK, CHUNK), CHUNK ** -0.5),
        "gmlp_bs": 1.0 + nrm(ks[18], (DEPTH, G_GROUPS, CHUNK), 0.1),
        "w_out": nrm(ks[19], (DEPTH, D, D), DEEPNORM_BETA * D ** -0.5),
        "ln1_g": 1.0 + nrm(ks[20], (DEPTH, D), 0.1),
        "ln1_b": nrm(ks[21], (DEPTH, D), 0.02),
        "w_ff1": nrm(ks[22], (DEPTH, D, D_FF), D ** -0.5),
        "w_ff2": nrm(ks[23], (DEPTH, D_FF, D), DEEPNORM_BETA * D_FF ** -0.5),
        "ln2_g": 1.0 + nrm(ks[24], (DEPTH, D), 0.1),
        "ln2_b": nrm(ks[25], (DEPTH, D), 0.02),
    }

def reference(x_prompt, x_sample, c, cache_attn_k, cache_attn_v, state_mlstm_C, state_mlstm_n, state_mlstm_m,
              c_ctx, w_mod, b_mod, w_in, q_norm_g, k_norm_g, mlstm_gate_b, gmlp_ln_g, gmlp_ln_b, gmlp_ws, gmlp_bs,
              w_out, ln1_g, ln1_b, w_ff1, w_ff2, ln2_g, ln2_b):
    xp, xs = x_prompt, x_sample
    ks_, vs_, Cs_, ns_, ms_ = [], [], [], [], []
    for l in range(DEPTH):
        p = (w_in[l], q_norm_g[l], k_norm_g[l], mlstm_gate_b[l], gmlp_ln_g[l], gmlp_ln_b[l], gmlp_ws[l],
             gmlp_bs[l], w_out[l], ln1_g[l], ln1_b[l], w_ff1[l], w_ff2[l], ln2_g[l], ln2_b[l])
        mod_ctx = modulation(c_ctx[None, :], w_mod[l], b_mod[l])
        xp, (k_l, v_l, sf, sb) = trunk_layer(xp, mod_ctx, p)
        ks_.append(k_l)
        vs_.append(v_l)
        Cs_.append(jnp.stack([sf[0], sb[0]], axis=1))
        ns_.append(jnp.stack([sf[1], sb[1]], axis=1))
        ms_.append(jnp.stack([sf[2], sb[2]], axis=1))
        mod_lat = modulation(c, w_mod[l], b_mod[l])
        ctx = (cache_attn_k[:, l], cache_attn_v[:, l],
               (state_mlstm_C[:, l, 0], state_mlstm_n[:, l, 0], state_mlstm_m[:, l, 0]),
               (state_mlstm_C[:, l, 1], state_mlstm_n[:, l, 1], state_mlstm_m[:, l, 1]))
        xs, _ = trunk_layer(xs, mod_lat, p, ctx)
    new_attn_k = jnp.stack(ks_, axis=1)
    new_attn_v = jnp.stack(vs_, axis=1)
    new_mlstm_C = jnp.stack(Cs_, axis=1)
    new_mlstm_n = jnp.stack(ns_, axis=1)
    new_mlstm_m = jnp.stack(ms_, axis=1)
    return (xp, xs, new_attn_k, new_attn_v, new_mlstm_C, new_mlstm_n, new_mlstm_m)


_drawn_inputs = setup_inputs


def setup_inputs(seed=0):
    import zlib

    import numpy as np

    out = dict(_drawn_inputs(seed))
    spreads = {}
    factors = {'cache_attn_k': 8.0,
     'cache_attn_v': 8.0,
     'state_mlstm_C': 8.0,
     'state_mlstm_n': 8.0,
     'state_mlstm_m': 8.0,
     'q_norm_g': 8.0,
     'gmlp_ln_g': 3.964,
     'gmlp_ln_b': 8.0,
     'gmlp_bs': 4.636}
    for name, (base, spread) in spreads.items():
        noise = np.random.default_rng([zlib.crc32(name.encode()), seed]).standard_normal(out[name].shape)
        drawn = base * np.exp(spread * noise) if base else spread * noise
        out[name] = jnp.asarray(drawn.astype(out[name].dtype))
    for name, factor in factors.items():
        out[name] = (out[name] * factor).astype(out[name].dtype)
    return out
```

```python
from contextlib import ExitStack

import numpy as np

import concourse.bass as bass
from concourse import mybir

ALU = mybir.AluOpType
ACT = mybir.ActivationFunctionType
AX = mybir.AxisListType
F32 = mybir.dt.float32
F32R = mybir.dt.float32r

P = 128
D = 1024
KT = D // P
SEQ = 128
DEC_SEQ = 1024
NS = DEC_SEQ // P
NT = NS + 1
TOK = NT * P
GRP = 3 * P
NL = 2
HD = 64
HQ, HKV = 8, 2
HG = HQ // HKV
MH = 4
FF = 4 * D
HC = 4 * P
NFF = FF // HC
W = 512
EPS = 1e-6
M_SCALE = HD ** -0.5
ALPHA = (2 * NL) ** 0.25
NEG = -1e30

ZQM, ZKM, ZVM, ZOM, ZQ, ZK, ZV, ZVG, ZUG = 0, 256, 512, 768, 1024, 1536, 1664, 1792, 2048
ZW = 2304
SLOTS = 8
G_IN, G_OUT, G_FF = 5, 2, 2 * NFF
GROUPS = G_IN + G_OUT + G_FF
RAW = 4

ROWS = 36
VE = HD + 1
PV = 2 * VE
START = 8
NSLOT = 11

C_ID, C_MF, C_MB, C_BM, C_SEL, C_SELP = 0, 128, 256, 384, 514, 514 + 8 * 128
NCONST = C_SELP + 4 * 128


def constants():
    k = np.zeros((P, NCONST), np.float32)
    k[:, C_ID:C_ID + P] = np.eye(P)
    s, t = np.arange(P)[:, None], np.arange(P)[None]
    k[:, C_MF:C_MF + P] = np.where(s <= t, 0.0, NEG)
    k[:, C_MB:C_MB + P] = np.where(s >= t, 0.0, NEG)
    k[:HD, C_BM:C_BM + VE] = 1.0
    k[HD:, C_BM + VE:C_BM + PV] = 1.0
    for d in range(2):
        for h in range(MH):
            r = 32 * d + h
            k[r, C_SEL + (d * MH + h) * P:C_SEL + (d * MH + h + 1) * P] = 1.0
            o = C_SELP + (d * 2 + h // 2) * P + (h % 2) * HD
            k[r, o:o + HD] = 1.0
    return k


def rope_tables():
    n = HD // 4
    inv = (10000.0 ** (-np.arange(n, dtype=np.float32) / n)).astype(np.float32)
    pos = np.arange(DEC_SEQ)
    out = np.zeros((DEC_SEQ, 2, HD), np.float32)
    for i, p in enumerate((pos // 64, pos % 64)):
        ang = (p.astype(np.float32)[:, None] * inv[None]).astype(np.float32)
        c, s = np.cos(ang), np.sin(ang)
        o = i * HD // 2
        out[:, 0, o:o + n], out[:, 0, o + n:o + 2 * n] = c, c
        out[:, 1, o:o + n], out[:, 1, o + n:o + 2 * n] = -s, s
    out = out.reshape(NS, P, 2, HD).transpose(1, 0, 2, 3)
    return np.concatenate([out, out[:, 0:2]], 1)



def build(nc, x_in, cond, w_mod, b_mod, w_slots, consts, rope, cache_k, cache_v, state0, row_in,
          qk_g, gln, ws_t, bs_t, ln_gb, y_out, k_out, v_out, c_out, n_out, m_out):
    x1_dram = nc.dram_tensor("x1_dram", (NT, P, D), F32, kind="Internal").ap()
    mod_dram = nc.dram_tensor("mod_dram", (NL * 12, 2, W), F32, kind="Internal").ap()

    with ExitStack() as ctx:
        a_w = 16512
        a_b = a_w + (2 * SLOTS + RAW) * W * 4
        a_a = a_b + NT * ZW * 4
        a_m = a_a + 2 * KT * TOK * 4
        a_end = 229344

        def region(start, end):
            free = [start]

            def place(name, shape, dt=F32, rows=P):
                t = nc.alloc_sbuf_tensor_at(name, [rows, *shape], dt, offset=free[0])
                free[0] += (int(np.prod(shape)) * 4 + 31) // 32 * 32
                assert free[0] <= end, (name, free[0] - end)
                return t
            return place

        put = region(a_w, a_b)
        w_hi = put("w_hi", [SLOTS, W], F32R)
        w_lo = put("w_lo", [SLOTS, W], F32R)
        w_raw = put("w_raw", [RAW, W])
        put = region(a_b, a_a)
        modw = put("modw", [2, KT, W])
        modb = put("modb", [NL * 12, W], rows=2)
        put = region(a_b, a_a)
        xt = put("xt", [3, D])
        hf = put("hf", [3, D])
        put = region(a_b, a_a)
        z = put("z", [NT, ZW])
        put = region(a_b, a_a)
        xr = put("xr", [NT, D])
        hf2 = put("hf2", [3, D])
        lnb = put("lnb", [2, D])
        gate = put("gate", [2, D])
        lnt = put("lnt", [2, W])
        put = region(a_b, a_a)
        acc = put("acc", [NT, D])
        f_hi = put("f_hi", [HC // P, TOK], F32R)
        f_lo = put("f_lo", [HC // P, TOK], F32R)
        fr = put("fr", [2, GRP])
        fsq = put("fsq", [2, GRP])
        put = region(a_b + NT * D * 4, a_a)
        x1t = put("x1t", [3, D])
        lnb2 = put("lnb2", [2, D])
        gate2 = put("gate2", [2, D])
        put = region(a_a, a_m)
        modr = put("modr", [NL * 12, W], rows=2)
        put = region(a_a, a_m)
        hi = put("hi", [KT, TOK], F32R)
        lo = put("lo", [KT, TOK], F32R)
        put = region(a_a, a_m)
        r_r = put("r_r", [TOK], rows=ROWS)
        r_d = put("r_d", [TOK], rows=ROWS)
        r_b = put("r_b", [TOK], rows=ROWS)
        r_m = put("r_m", [TOK], rows=ROWS)
        cs = put("cs", [NSLOT, 2, 2, PV])
        cols = put("cols", [NT, 4, ROWS])
        selc = put("selc", [12, P])
        bmask = put("bmask", [PV])
        kw = put("kw", [2, 256])
        vext = put("vext", [MH, VE])
        qs = put("qs", [256])
        ks = put("ks", [256])
        qT = put("qT", [2, P])
        kT = put("kT", [2, P])
        qbd = put("qbd", [2, 2, P])
        wt = put("wt", [2, MH, P])
        hn = put("hn", [2, MH, VE])
        hh = put("hh", [2, MH, HD])
        og = put("og", [256])
        dec = put("dec", [8, 2, 2])
        mrow = put("mrow", [5, NT], rows=ROWS)
        den = put("den", [2, 2, MH])
        put = region(a_a, a_m)
        wst = put("wst", [4, P])
        glnb = put("glnb", [2, 256])
        vn = put("vn", [NT, 256])
        gs = put("gs", [3, 256])
        bst = put("bst", [4])
        put = region(a_a, a_m)
        p_hi = put("p_hi", [NT, HG, P], F32R)
        p_lo = put("p_lo", [NT, HG, P], F32R)
        kst = put("kst", [HKV, 10 * P], F32R)
        vst = put("vst", [HKV, 10, P], F32R)
        q_hi = put("q_hi", [HG, P], F32R)
        q_lo = put("q_lo", [HG, P], F32R)
        pr = put("pr", [2, NT * P])
        o_s = put("o_s", [HG * P])
        rp = put("rp", [2, 2, HD])
        put = region(a_m, a_end)
        ident = put("ident", [P])
        idr = put("idr", [P], F32R)
        mkr = put("mkr", [2, P], F32R)
        maskt = put("maskt", [2, P])
        ri = put("ri", [TOK], rows=ROWS)
        rf = put("rf", [TOK], rows=ROWS)
        modc = put("modc", [64])
        mod64 = put("mod64", [P], rows=64)
        sc = put("sc", [KT, 2])
        sce = put("sce", [KT, 2])
        condt = put("condt", [KT, 2])
        rcon = put("rcon", [3], rows=ROWS)
        st6 = put("st6", [NT, 2, 6])
        mv = put("mv", [NT, 2])
        rs = put("rs", [NT])
        half = put("half", [NT * 10])
        nm = put("nm", [2])
        rsum = put("rsum", [HQ])
        rinv = put("rinv", [HG])
        ss = put("ss", [NT, 10])
        put = region(a_m + 5 * 512, a_m + 5 * 512 + 2 * TOK * 4)
        qd = put("qd", [HQ, 2, HD])
        kvt = put("kvt", [2, P])
        gq = put("gq", [2, HD])
        qn = put("qn", [HQ * HD])
        ps = ctx.enter_context(nc.psum_tensor("ps", [P, 8, 512], F32))

        def sem(name):
            return ctx.enter_context(nc.semaphore(name))

        names = """passed x_copied const_ld mod_b_ld mod_st mod_ready silu_e mod_ps mod_row phase_end
            w_hi_done w_lo_done w_used
            mc_ld mc_ps xT_ps hf_done hi_done h_done row_ld
            z_ps z_done g_ps
            act_row dve_row abs_row pow_in pow_out rt_ps ml_ld ml_zero
            u_v u_kw u_ps u_done m_st m_tp m_qk m_D m_S m_w m_sw m_num m_og m_fin st_out
            gm_ld gm_vn gm_ps
            at_ld v_hi v_rdy kd_done kd_ps k_hi k_lo kv_out
            qd_done q_ps q_hi_done q_lo_done s_ps mx_done ex_done t_ps p_hi_done p_lo_done
            o_ps o_cp ot_ps ot_cp oy_done
            yT_ps y_hi y_lo o_out xr_half ln_ld xr_done x1_st
            h_ps r_done fhi_done flo_done f_ps f_acc acc_zero x1_used y_rdy ln_st""".split()
        S = dict((n, sem(n)) for n in names)
        w_ld = [sem(f"w_ld{j}") for j in range(RAW)]
        mod_w_ld = [sem(f"mod_w_ld{j}") for j in range(2)]
        xt_ld = [sem(f"xt_ld{j}") for j in range(3)]
        x1_ld = [sem(f"x1_ld{j}") for j in range(3)]
        rp_ld = [sem(f"rp_ld{j}") for j in range(2)]

        NB = 13

        def own(eng):
            eng.sem_inc(S["passed"], 1)

        def phase(eng, L, b):
            own(eng)
            eng.drain().then_inc(S["phase_end"], 1)
            eng.wait_ge(S["phase_end"], 4 * NB * L + 4 * (b + 2))
            own(eng)

        def slot(L, g, j):
            return L * (GROUPS * SLOTS) + g * SLOTS + j

        def split_hi(act, L, g, prev):
            for j in range(SLOTS):
                act.wait_ge(w_ld[j % RAW], 16 * (L * (GROUPS * 2) + 2 * g + j // RAW + 1))
                if prev and j < SLOTS - 1:
                    act.wait_ge(S["w_used"], START + (SLOTS - 1) * (L * GROUPS + g - 1) + j + 1)
                elif prev:
                    act.wait_ge(*prev)
                act.copy(w_hi[:, j, :], w_raw[:, j % RAW, :]).then_inc(S["w_hi_done"], 1)

        def split_lo(dve, L, g):
            for j in range(SLOTS):
                dve.wait_ge(S["w_hi_done"], slot(L, g, j) + 1)
                dve.tensor_tensor(w_lo[:, j, :], w_raw[:, j % RAW, :], w_hi[:, j, :].bitcast(F32),
                                  ALU.subtract).then_inc(S["w_lo_done"], 1)

        def col(L, which, kind, kt, g):
            c = which * 32 + (kind * 2 + kt // 4) * 8 + g * 4 + kt % 4
            return modc[:, c:c + 1]

        block = ctx.enter_context(nc.Block())

        @block.sync
        def _(sp):
            sp.dma_start(y_out, x_in).then_inc(S["x_copied"], 16)
            sp.dma_start(ident[:], consts[:, C_ID:C_ID + P]).then_inc(S["const_ld"], 16)
            sp.dma_start(maskt[:].rearrange("p a b -> p (a b)"), consts[:, C_MF:C_MF + 2 * P]).then_inc(S["const_ld"], 16)
            sp.dma_start(condt[:], cond).then_inc(S["const_ld"], 16)
            for n in range(2):
                sp.dma_start(modw[:, n], w_mod[n]).then_inc(mod_w_ld[n], 16)
            for j in range(RAW):
                sp.dma_start(w_raw[:, j, :], w_slots[j]).then_inc(w_ld[j], 16)
            with sp.Fori(0, NL * 12 // 2 - 1) as i:
                for u in range(2):
                    sp.wait_ge(S["mod_ps"], 2 * i + u + 1)
                    sp.dma_start(modw[:, u], w_mod[2 * i + u + 2]).then_inc(mod_w_ld[u], 16)
            with sp.Fori(0, (NL * GROUPS + 1) * SLOTS // RAW - 1) as i:
                for j in range(RAW):
                    sp.wait_ge(S["w_lo_done"], RAW * i + j + 1)
                    sp.dma_start(w_raw[:, j, :], w_slots[RAW * i + RAW + j]).then_inc(w_ld[j], 16)

        @block.gpsimd
        def _(pool):
            pool.memset(half[:], -0.5)
            pool.sem_inc(S["h_done"], START)
            pool.dma_start(modb[:], b_mod).then_inc(S["mod_b_ld"], 16)
            pool.wait_ge(S["mod_row"], START + NL * 12)
            pool.dma_start(mod_dram.rearrange("n g f -> g n f"), modr[:]).then_inc(S["mod_st"], 16)
            pool.wait_ge(S["mod_st"], 16)
            pool.wait_ge(S["x_copied"], 16)
            phase(pool, 0, -1)

            def rstd(L, k, ap, n):
                pool.wait_ge(S["pow_in"], 4 * L + k + 1)
                pool.tensor_tensor(ap, ap, half[:, 0:n], ALU.pow).then_inc(S["pow_out"], 1)

            def lo_of(t, src, count):
                pool.wait_ge(S["hi_done"], count + 1)
                pool.tensor_tensor(lo[:, :, bass.ds(t * P, P)], src.rearrange("p (k c) -> p k c", c=P),
                                   hi[:, :, bass.ds(t * P, P)].bitcast(F32), ALU.subtract).then_inc(S["h_done"], 1)

            with pool.Fori(0, NL) as L:
                for k in range(2):
                    pool.dma_start(mod64[32 * k:32 * k + 32, :],
                                   mod_dram[bass.ds(L * 12 + 6 * k, 4)].rearrange("n g (q f) -> (n g q) f", f=P)
                                   ).then_inc(S["mc_ld"], 16)
                pool.dma_start(rcon[:], row_in[L]).then_inc(S["row_ld"], 16)
                for u in range(3):
                    pool.dma_start(xt[:, u], y_out[u]).then_inc(xt_ld[u], 16)
                with pool.Fori(0, 2) as i:
                    for u in range(3):
                        pool.wait_ge(S["xT_ps"], 2 * NT * L + 3 * i + u + 1)
                        own(pool)
                        pool.dma_start(xt[:, u], y_out[3 * i + u + 3]).then_inc(xt_ld[u], 16)
                        lo_of(3 * i + u, hf[:, u], 2 * NT * L + 3 * i + u)
                for u in range(3):
                    lo_of(6 + u, hf[:, u], 2 * NT * L + 6 + u)
                phase(pool, L, 0)
                phase(pool, L, 1)
                pool.dma_start(selc[:], consts[:, C_SEL:C_SEL + 12 * P].rearrange("p (a b) -> p a b", b=P)).then_inc(S["ml_ld"], 16)
                pool.dma_start(bmask[:], consts[:, C_BM:C_BM + PV]).then_inc(S["ml_ld"], 16)
                pool.dma_start(cs[:, 0], state0[L]).then_inc(S["ml_ld"], 16)
                pool.memset(cs[:, 9], 0.0)
                pool.memset(qbd[:], 0.0)
                pool.memset(vext[:], 1.0).then_inc(S["ml_zero"], 1)
                pool.wait_ge(S["ml_ld"], 48 * L + 48)
                phase(pool, L, 2)
                phase(pool, L, 3)
                for d in range(2):
                    for h in range(MH):
                        part, o = (h % 2) * HD, (h % 2) * VE
                        pool.dma_start(c_out[L, d, h], cs[part:part + HD, 10, d, h // 2, o:o + HD]).then_inc(S["st_out"], 16)
                        pool.dma_start(n_out[L, d, h], cs[part:part + HD, 10, d, h // 2, o + HD:o + VE]).then_inc(S["st_out"], 16)
                    pool.dma_start(m_out[L, d], mrow[32 * d:32 * d + MH, 3, NS:NT]).then_inc(S["st_out"], 16)
                pool.wait_ge(S["st_out"], 16 * 18 * (L + 1))
                phase(pool, L, 4)
                pool.dma_start(wst[:], ws_t[L]).then_inc(S["gm_ld"], 16)
                pool.dma_start(bst[:], bs_t[L]).then_inc(S["gm_ld"], 16)
                pool.dma_start(glnb[:], gln[L]).then_inc(S["gm_ld"], 16)
                rstd(L, 0, rs[:], NT)
                phase(pool, L, 5)
                pool.dma_start(kvt[:, 0], cache_k[L]).then_inc(S["at_ld"], 16)
                pool.dma_start(kvt[:, 1], cache_v[L]).then_inc(S["at_ld"], 16)
                pool.dma_start(gq[:], qk_g[L]).then_inc(S["at_ld"], 16)
                for u in range(2):
                    pool.dma_start(rp[:, u], rope[:, u]).then_inc(rp_ld[u], 16)
                rstd(L, 1, ss[:].rearrange("p a b -> p (a b)"), NT * 10)
                with pool.Fori(0, 4) as i:
                    for u in range(2):
                        pool.wait_ge(S["kd_done"], START + 10 * L + 2 * i + u + 1)
                        own(pool)
                        pool.dma_start(rp[:, u], rope[:, 2 * i + u + 2]).then_inc(rp_ld[u], 16)
                pool.wait_ge(S["kd_done"], START + 10 * L + 10)
                own(pool)
                pool.dma_start(k_out[L], qn[:, 0:P]).then_inc(S["kv_out"], 16)
                pool.dma_start(v_out[L], z[:, NS, ZV:ZV + P]).then_inc(S["kv_out"], 16)
                pool.wait_ge(S["kv_out"], 32 * L + 32)
                phase(pool, L, 6)
                with pool.Fori(0, 3) as i:
                    for u in range(2):
                        pool.wait_ge(S["qd_done"], NT * L + 2 * i + u + 1)
                        own(pool)
                        pool.dma_start(rp[:, u], rope[:, 2 * i + u + 2]).then_inc(rp_ld[u], 16)
                phase(pool, L, 7)
                phase(pool, L, 8)
                pool.dma_start(xr[:], y_out.rearrange("t p d -> p t d")).then_inc(S["ln_ld"], 16)
                for g in range(2):
                    for n in range(2):
                        pool.dma_start(gate[:, g, n * W:(n + 1) * W],
                                       mod_dram[L * 12 + 4 + n, g].partition_broadcast(P)).then_inc(S["ln_ld"], 16)
                for k in range(2):
                    pool.dma_start(lnb[:, k], ln_gb[L, k].partition_broadcast(P)).then_inc(S["ln_ld"], 16)
                rstd(L, 2, rs[:], NT)
                with pool.Fori(0, NT) as t:
                    pool.wait_ge(S["xr_done"], NT * L + t + 1)
                    own(pool)
                    pool.dma_start(x1_dram[t], xr[:, t]).then_inc(S["x1_st"], 16)
                pool.wait_ge(S["x1_st"], 16 * NT * (L + 1))
                phase(pool, L, 9)
                for t in range(NT):
                    lo_of(t, hf2[:, t % 3], 2 * NT * L + NT + t)
                phase(pool, L, 10)
                pool.memset(acc[:], 0.0).then_inc(S["acc_zero"], 1)
                phase(pool, L, 11)
                for u in range(3):
                    pool.dma_start(x1t[:, u], x1_dram[u]).then_inc(x1_ld[u], 16)
                for g in range(2):
                    for n in range(2):
                        pool.dma_start(gate2[:, g, n * W:(n + 1) * W],
                                       mod_dram[L * 12 + 10 + n, g].partition_broadcast(P)).then_inc(S["ln_ld"], 16)
                for k in range(2):
                    pool.dma_start(lnb2[:, k], ln_gb[L, 2 + k].partition_broadcast(P)).then_inc(S["ln_ld"], 16)
                with pool.Fori(0, 2) as i:
                    for u in range(3):
                        pool.wait_ge(S["x1_used"], NT * L + 3 * i + u + 1)
                        own(pool)
                        pool.dma_start(x1t[:, u], x1_dram[3 * i + u + 3]).then_inc(x1_ld[u], 16)
                rstd(L, 3, rs[:], NT)
                with pool.Fori(0, NT) as t:
                    pool.wait_ge(S["y_rdy"], NT * L + t + 1)
                    own(pool)
                    pool.dma_start(y_out[t], acc[:, t]).then_inc(S["ln_st"], 16)
                pool.wait_ge(S["ln_st"], 16 * NT * (L + 1))
                phase(pool, L, 12)

        @block.scalar
        def _(act):
            for n in ("z_done", "ex_done", "r_done", "m_w", "o_cp"):
                act.sem_inc(S[n], START)
            act.wait_ge(S["const_ld"], 48)
            act.activation(sce[:], condt[:], ACT.Exp, scale=-1.0).then_inc(S["silu_e"], 1)
            act.copy(idr[:], ident[:])
            act.copy(mkr[:], maskt[:])
            split_hi(act, 0, 0, None)
            phase(act, 0, -1)

            def hi_of(t, src, count):
                act.wait_ge(S["hf_done"], START + count + 1)
                act.copy(hi[:, :, bass.ds(t * P, P)], src.rearrange("p (k c) -> p k c", c=P)).then_inc(S["hi_done"], 1)

            def z_tile(L, c, t, dst, src):
                act.wait_ge(S["z_ps"], START + 45 * L + 9 * c + t + 1)
                act.copy(dst, src).then_inc(S["z_done"], 1)

            def states_v(L, c, n):
                act.wait_ge(S["u_ps"], START + NT * L + n)
                act.copy(vext[:, :, 0:HD], z[:, c, ZVM:ZVM + 256].rearrange("p (h e) -> p h e", e=HD)).then_inc(S["u_v"], 1)

            def mlstm(L, c, n):
                act.wait_ge(S["m_tp"], START + NT * L + n)
                act.copy(qs[:], z[:, c, ZQM:ZQM + 256])
                act.activation(ks[:], z[:, c, ZKM:ZKM + 256], ACT.Copy, scale=M_SCALE)
                act.wait_ge(S["m_num"], START + NT * L + n)
                act.copy(vext[:, :, 0:HD], z[:, c, ZVM:ZVM + 256].rearrange("p (h e) -> p h e", e=HD)).then_inc(S["m_st"], 1)
                act.wait_ge(S["m_fin"], START + NT * L + n)
                act.activation(og[:], z[:, c, ZOM:ZOM + 256], ACT.Exp, scale=-1.0).then_inc(S["m_og"], 1)
                act.wait_ge(S["m_D"], NT * L + n + 1)
                for d in range(2):
                    for h in range(MH):
                        ins = act.activation(wt[:, d, h], ps[:, 2 + d, h * P:(h + 1) * P], ACT.Exp,
                                             bias=cols[:, c, 0, 32 * d + h:32 * d + h + 1])
                ins.then_inc(S["m_w"], 1)

            with act.Fori(0, NL) as L:
                with act.Fori(0, 3) as i:
                    for u in range(3):
                        hi_of(3 * i + u, hf[:, u], 2 * NT * L + 3 * i + u)
                phase(act, L, 0)
                act.wait_ge(S["row_ld"], 16 * L + 16)
                for g in range(3):
                    act.wait_ge(S["g_ps"], 3 * L + g + 1)
                    act.activation(ri[:, g * GRP:(g + 1) * GRP], ps[0:ROWS, 4 + g, 0:GRP], ACT.Identity, bias=rcon[:, 0:1])
                    act.activation(rf[:, g * GRP:(g + 1) * GRP], ps[64:64 + ROWS, 4 + g, 0:GRP], ACT.Identity, bias=rcon[:, 1:2])
                for t in range(NT - 1):
                    z_tile(L, 0, t, z[:, t, ZUG:ZUG + 256], ps[:, t % 3, 0:256])
                split_hi(act, L, 1, (S["z_ps"], START + 45 * L + 9))
                z_tile(L, 0, NT - 1, z[:, NT - 1, ZUG:ZUG + 256], ps[:, 2, 0:256])
                with act.Fori(0, 4) as c:
                    for t in range(NT - 1):
                        z_tile(L, c + 1, t, z[:, t, bass.ds(c * W, W)], ps[:, t % 3, :])
                    split_hi(act, L, c + 2, (S["z_ps"], START + 45 * L + 9 * c + 18))
                    z_tile(L, c + 1, NT - 1, z[:, NT - 1, bass.ds(c * W, W)], ps[:, 2, :])
                phase(act, L, 1)
                act.wait_ge(S["abs_row"], L + 1)
                act.activation(r_b[:], r_b[:], ACT.Exp, scale=-1.0)
                act.drain()
                act.activation(r_b[:], r_b[:], ACT.Ln, bias=1.0).then_inc(S["act_row"], 1)
                act.wait_ge(S["dve_row"], L + 1)
                act.activation(rf[:], rf[:], ACT.Exp)
                act.activation(r_r[:], r_r[:], ACT.Exp)
                act.activation(r_d[:], r_d[:], ACT.Exp, scale=-1.0)
                act.activation(mrow[:, 4], mrow[:, 4], ACT.Exp).then_inc(S["act_row"], 1)
                phase(act, L, 2)
                with act.Fori(0, NS) as c:
                    states_v(L, c, c)
                states_v(L, NS, NS)
                phase(act, L, 3)
                with act.Fori(0, NS) as c:
                    mlstm(L, c, c)
                mlstm(L, NS, NS)
                phase(act, L, 4)
                phase(act, L, 5)
                act.wait_ge(S["at_ld"], 48 * L + 48)
                for v in range(HKV):
                    c = v * HD
                    act.copy(vst[:, v, 0:NS, 0:HD], z[:, 0:NS, ZV + c:ZV + c + HD])
                    act.copy(vst[:, v, 8, 0:HD], kvt[:, 1, c:c + HD])
                    ins = act.copy(vst[:, v, 9, 0:HD], z[:, NS, ZV + c:ZV + c + HD])
                ins.then_inc(S["v_hi"], 1)

                def keys_hi(tile, n):
                    act.wait_ge(S["kd_ps"], START + 10 * L + n + 1)
                    act.wait_ge(S["k_lo"], START + 10 * L + n)
                    act.copy(kst[0:HD, :, bass.ds(tile * P, P)], ps[0:HD, 0, 0:2 * P].rearrange("p (a b) -> p a b", b=P))
                    act.copy(q_hi[HD:P, 0:2], ps[HD:P, 0, 0:2 * P].rearrange("p (a b) -> p a b", b=P)).then_inc(S["k_hi"], 1)

                with act.Fori(0, NS) as t:
                    keys_hi(t, t)
                keys_hi(8, 8)
                keys_hi(9, 9)
                phase(act, L, 6)

                def att(cur, prev, t):
                    for n in range(HQ):
                        hs = 72 * L + HQ * t + n
                        if n % HG == 0 and cur:
                            act.wait_ge(S["q_ps"], 18 * L + 2 * t + n // HG + 1)
                            act.wait_ge(S["s_ps"], START + hs)
                            act.copy(q_hi[:], ps[:, 7, :].rearrange("p (a b) -> p a b", b=P)).then_inc(S["q_hi_done"], 1)
                        if cur:
                            nk = cur
                            act.wait_ge(S["mx_done"], START + hs + 1)
                            act.wait_ge(S["t_ps"], START + hs - 1)
                            if n % HG == 0:
                                act.wait_ge(S["oy_done"], START + 18 * L + 2 * t + n // HG - 1)
                            if nk == NT:
                                o_, i_ = pr[:, n % 2].rearrange("p (a b) -> p a b", b=GRP), ps[:, 0:3, 0:GRP]
                            else:
                                o_, i_ = pr[:, n % 2, 0:P], ps[:, 0, 0:P]
                            act.activation(o_, i_, ACT.Exp, bias=nm[:, n % 2:n % 2 + 1],
                                           accum_out=rsum[:, n:n + 1])
                            act.drain().then_inc(S["ex_done"], 1)
                        what = cur if n else prev
                        if what and (n or prev):
                            m = (n - 1) % HG
                            act.wait_ge(S["t_ps"], START + hs)
                            act.wait_ge(S["o_ps"], START + 18 * L + 2 * t + (n + 3) // HG - 1)
                            if what == NT:
                                act.copy(p_hi[:, :, m].rearrange("p (a b) c -> p a b c", b=3),
                                         ps[:, 3:6, 0:GRP].rearrange("p a (b c) -> p a b c", c=P)).then_inc(S["p_hi_done"], 1)
                            else:
                                act.copy(p_hi[:, 0, m], ps[:, 3, 0:P]).then_inc(S["p_hi_done"], 1)
                        if n % HG == 1 and (cur if n > 1 else prev):
                            act.wait_ge(S["oy_done"], START + 18 * L + 2 * t + n // HG - 1)
                            act.wait_ge(S["o_ps"], START + 18 * L + 2 * t + n // HG)
                            act.copy(o_s[:], ps[:, 6, :]).then_inc(S["o_cp"], 1)
                        if n % HG == 2 and (cur if n > 2 else prev):
                            act.wait_ge(S["ot_ps"], 18 * L + 2 * t + n // HG)
                            act.copy(o_s[:, 0:256].rearrange("p (a b) -> p a b", b=HD),
                                     ps[:, 7, :].rearrange("p (a b) -> p a b", b=P)[:, :, 0:HD]).then_inc(S["ot_cp"], 1)

                att(NT, None, 0)
                with act.Fori(1, NS) as t:
                    att(NT, NT, t)
                att(1, NT, NS)
                att(None, 1, NT)
                phase(act, L, 7)
                for t in range(NT):
                    act.wait_ge(S["yT_ps"], NT * L + t + 1)
                    for k in range(2):
                        ins = act.copy(hi[:, 4 * k:4 * k + 4, t * P:(t + 1) * P],
                                       ps[:, 2 * (t % 3) + k, :].rearrange("p (a b) -> p a b", b=P))
                    ins.then_inc(S["y_hi"], 1)
                phase(act, L, 8)
                split_hi(act, L, 6, (S["o_out"], START + 18 * L + 9))
                split_hi(act, L, 7, (S["o_out"], START + 18 * L + 18))
                phase(act, L, 9)
                for t in range(NT):
                    hi_of(t, hf2[:, t % 3], 2 * NT * L + NT + t)
                phase(act, L, 10)

                def hidden(i, b):
                    n = 12 * (NFF * L + i) + b
                    act.wait_ge(S["h_ps"], START + n + 1)
                    act.wait_ge(S["flo_done"], START + n - 1)
                    act.activation(fr[:, b % 2], ps[:, b % 3, 0:GRP], ACT.Relu).then_inc(S["r_done"], 1)
                    act.drain()
                    act.activation(f_hi[:, b // 3, (b % 3) * GRP:(b % 3 + 1) * GRP], fr[:, b % 2],
                                   ACT.Square).then_inc(S["fhi_done"], 1)

                with act.Fori(0, NFF) as i:
                    for b in range(11):
                        hidden(i, b)
                    split_hi(act, L, 2 * i + 8, (S["h_ps"], START + 12 * (NFF * L + i) + 12))
                    hidden(i, 11)
                    split_hi(act, L, 2 * i + 9, (S["f_ps"], START + 18 * (NFF * L + i) + 18))
                phase(act, L, 11)
                phase(act, L, 12)

        @block.vector
        def _(dve):
            for n in ("mod_row", "hf_done", "u_done", "m_qk", "m_sw", "m_fin", "gm_vn", "kd_done", "k_lo",
                      "mx_done", "p_lo_done", "oy_done", "q_lo_done", "y_lo", "xr_half", "flo_done", "f_acc"):
                dve.sem_inc(S[n], START)
            dve.wait_ge(S["silu_e"], 1)
            dve.tensor_scalar(sce[:], sce[:], 1.0, None, ALU.add)
            dve.drain()
            dve.reciprocal(sce[:], sce[:])
            dve.drain()
            dve.tensor_tensor(sc[:], sce[:], condt[:], ALU.mult).then_inc(S["mod_ready"], 1)
            dve.wait_ge(S["mod_b_ld"], 16)
            own(dve)
            with dve.Fori(0, NL * 12 // 2) as i:
                for u in range(2):
                    dve.wait_ge(S["mod_ps"], 2 * i + u + 1)
                    dve.tensor_tensor(modr[:, 2 * i + u], ps[0:2, u, :], modb[:, 2 * i + u], ALU.add).then_inc(S["mod_row"], 1)
            split_lo(dve, 0, 0)
            phase(dve, 0, -1)

            def modulate(L, n, which, dst, u, g):
                dve.wait_ge(S["xT_ps"], 2 * NT * L + n + 1)
                dve.wait_ge(S["h_done"], START + 2 * NT * L + n - 2)
                for kt in range(KT):
                    ins = dve.tensor_scalar(dst[:, u, kt * P:(kt + 1) * P],
                                            ps[:, 2 * u + kt // 4, (kt % 4) * P:(kt % 4 + 1) * P],
                                            col(L, which, 1, kt, g), col(L, which, 0, kt, g), ALU.mult, ALU.add)
                ins.then_inc(S["hf_done"], 1)

            def b2(ap, n):
                return ap.unsqueeze(len(ap.shape)).broadcast_to([*ap.shape, n])

            def spread(ap, n):
                return ap.unsqueeze(1).broadcast_to([ap.shape[0], n, *ap.shape[1:]])

            def layer_norm(L, k, x, gb, done):
                with dve.Fori(0, NT) as t:
                    for j in range(2):
                        dve.bn_stats(st6[:, t, j], x[:, t, j * W:(j + 1) * W])
                dve.drain()
                for t in range(NT):
                    dve.bn_aggr(mv[:, t], st6[:, t].rearrange("p a b -> p (a b)"))
                dve.drain()
                dve.tensor_scalar(rs[:], mv[:, :, 1], EPS, None, ALU.add).then_inc(S["pow_in"], 1)
                dve.wait_ge(S["pow_out"], 4 * L + k + 1)
                own(dve)
                with dve.Fori(0, NT) as t:
                    dve.tensor_scalar(x[:, t], x[:, t], mv[:, t, 0:1], rs[:, bass.ds(t, 1)], ALU.subtract, ALU.mult)
                    dve.drain()
                    dve.tensor_tensor(x[:, t], x[:, t], gb[:, 0], ALU.mult)
                    dve.drain()
                    dve.tensor_tensor(x[:, t], x[:, t], gb[:, 1], ALU.add).then_inc(done, 1)

            with dve.Fori(0, NL) as L:
                dve.wait_ge(S["mc_ps"], L + 1)
                for k in range(2):
                    dve.tensor_copy(modc[:, 32 * k:32 * k + 16], ps[:, 7, 32 * k:32 * k + 16])
                    dve.tensor_scalar(modc[:, 32 * k + 16:32 * k + 32], ps[:, 7, 32 * k + 16:32 * k + 32], 1.0, None, ALU.add)
                dve.drain()
                with dve.Fori(0, 2) as i:
                    for u in range(3):
                        modulate(L, 3 * i + u, 0, hf, u, 1)
                for u in range(3):
                    modulate(L, 6 + u, 0, hf, u, int(u < 2))
                phase(dve, L, 0)
                with dve.Fori(0, 5) as c:
                    split_lo(dve, L, c + 1)
                phase(dve, L, 1)
                dve.scalar_tensor_tensor(r_b[:], rf[:], -1.0, rf[:], ALU.mult, ALU.max).then_inc(S["abs_row"], 1)
                dve.memset(r_r[:], 1.0)
                dve.memset(r_d[:], 0.0)
                dve.memset(r_m[:], 0.0)
                dve.memset(mrow[:], 0.0)
                dve.drain()
                dve.memset(r_r[:, 0:TOK:P], 0.0)
                dve.wait_ge(S["act_row"], 2 * L + 1)
                dve.scalar_tensor_tensor(rf[:], rf[:], 0.0, r_b[:], ALU.min, ALU.subtract)
                dve.drain()
                F, Bk = slice(0, MH), slice(32, 32 + MH)
                dve.tensor_tensor_scan(r_b[F], r_r[F], rf[F], 0.0, ALU.mult, ALU.add)
                dve.tensor_tensor_scan(r_b[Bk, ::-1], r_r[Bk], rf[Bk, ::-1], 0.0, ALU.mult, ALU.add)
                dve.drain()
                dve.tensor_copy(r_d[F, P:DEC_SEQ:P], r_b[F, P - 1:DEC_SEQ - P:P])
                dve.tensor_copy(r_d[Bk, P - 1:DEC_SEQ - P:P], r_b[Bk, P:DEC_SEQ:P])
                dve.tensor_tensor(ri[:], ri[:], r_b[:], ALU.subtract)
                dve.drain()
                N = DEC_SEQ
                dve.tensor_tensor_scan(r_m[F, 0:N], r_d[F, 0:N], ri[F, 0:N], rcon[F, 2:3], ALU.add, ALU.max)
                dve.tensor_tensor_scan(r_m[F, N:TOK], r_d[F, N:TOK], ri[F, N:TOK], 0.0, ALU.add, ALU.max)
                dve.tensor_tensor_scan(r_m[Bk, N - 1::-1], r_d[Bk, N - 1::-1], ri[Bk, N - 1::-1], rcon[Bk, 2:3], ALU.add, ALU.max)
                dve.tensor_tensor_scan(r_m[Bk, TOK - 1:N - 1:-1], r_d[Bk, TOK - 1:N - 1:-1], ri[Bk, TOK - 1:N - 1:-1],
                                       0.0, ALU.add, ALU.max)
                dve.drain()
                dve.tensor_copy(mrow[F, 0], r_b[F, P - 1:TOK:P])
                dve.tensor_copy(mrow[Bk, 0], r_b[Bk, 0:TOK:P])
                dve.tensor_copy(mrow[F, 1], r_m[F, P - 1:TOK:P])
                dve.tensor_copy(mrow[Bk, 1], r_m[Bk, 0:TOK:P])
                dve.tensor_copy(mrow[F, 2, 0:1], rcon[F, 2:3])
                dve.tensor_copy(mrow[Bk, 2, NS - 1:NS], rcon[Bk, 2:3])
                dve.drain()
                dve.tensor_tensor(mrow[:, 3], mrow[:, 0], mrow[:, 1], ALU.add)
                dve.drain()
                dve.tensor_copy(mrow[F, 2, 1:NS], mrow[F, 3, 0:NS - 1])
                dve.tensor_copy(mrow[Bk, 2, 0:NS - 1], mrow[Bk, 3, 1:NS])
                dve.drain()
                dve.tensor_tensor(mrow[:, 4], mrow[:, 2], mrow[:, 1], ALU.subtract)
                v3 = lambda r: r[:].rearrange("p (c t) -> p c t", t=P)
                dve.tensor_tensor(v3(rf), v3(ri), b2(mrow[:, 1], P), ALU.subtract)
                dve.tensor_tensor(v3(r_r), b2(mrow[:, 2], P), v3(r_m), ALU.subtract)
                dve.tensor_tensor(r_d[:], r_b[:], r_m[:], ALU.add).then_inc(S["dve_row"], 1)
                dve.drain()
                dve.tensor_scalar(r_m[:], r_m[:], -1.0, None, ALU.mult)
                dve.wait_ge(S["rt_ps"], L + 1)
                dve.tensor_copy(cols[:].rearrange("p (a b) c d -> p a (b c d)", b=3), ps[:, 0:3, 0:12 * ROWS])
                for p_ in range(2):
                    dve.tensor_copy(dec[:, :, 0, p_], ps[:, 3, p_ * NT:p_ * NT + NS])
                    dve.tensor_copy(dec[:, :, 1, p_], ps[:, 3, (2 + p_) * NT:(2 + p_) * NT + NS][:, ::-1])
                phase(dve, L, 2)

                def states(c, n, s_f, s_b):
                    dve.wait_ge(S["u_ps"], START + NT * L + n)
                    for d in range(2):
                        ins = dve.scalar_tensor_tensor(kw[:, d].rearrange("p (h e) -> p h e", e=HD),
                                                       z[:, c, ZKM:ZKM + 256].rearrange("p (h e) -> p h e", e=HD), M_SCALE,
                                                       b2(cols[:, c, 1, 32 * d:32 * d + MH], HD), ALU.mult, ALU.mult)
                    ins.then_inc(S["u_kw"], 1)
                    dve.wait_ge(S["u_ps"], START + NT * L + n + 1)
                    for d, s_ in enumerate((s_f, s_b)):
                        ins = dve.tensor_tensor(cs[:, s_, d], ps[:, d, 0:2 * PV].rearrange("p (a b) -> p a b", b=PV),
                                                spread(bmask[:], 2), ALU.mult)
                    ins.then_inc(S["u_done"], 1)

                with dve.Fori(0, NS) as c:
                    states(c, c, c + 1, 8 - c)
                states(NS, NS, 10, 10)
                dve.drain()
                tmp = hn[:].rearrange("p a b c -> p (a b c)")
                flat = lambda ap: ap.rearrange("p a b c -> p (a b) c")
                with dve.Fori(0, NS) as i:
                    dve.tensor_tensor(tmp.rearrange("p (a b) -> p a b", b=PV), flat(cs[:, i]),
                                      b2(dec[:, i].rearrange("p a b -> p (a b)"), PV), ALU.mult)
                    dve.drain()
                    dve.tensor_tensor(flat(cs[:, i + 1]), flat(cs[:, i + 1]), tmp.rearrange("p (a b) -> p a b", b=PV), ALU.add)
                    dve.drain()
                phase(dve, L, 3)

                def mlstm(c, n):
                    dve.wait_ge(S["m_tp"], START + NT * L + n + 1)
                    dve.wait_ge(S["m_num"], START + NT * L + n)
                    for p_ in range(2):
                        a = slice(HD * p_, HD * p_ + HD)
                        dve.tensor_copy(qbd[a, :, p_, :], ps[a, 0, 0:2 * P].rearrange("p (a b) -> p a b", b=P))
                    dve.tensor_copy(qT[:], ps[:, 0, 0:2 * P].rearrange("p (a b) -> p a b", b=P))
                    dve.tensor_copy(kT[:], ps[:, 0, 2 * P:4 * P].rearrange("p (a b) -> p a b", b=P)).then_inc(S["m_qk"], 1)
                    dve.wait_ge(S["m_og"], NT * L + n + 1)
                    dve.tensor_scalar(og[:], og[:], 1.0, None, ALU.add)
                    dve.drain()
                    dve.reciprocal(og[:], og[:])
                    dve.wait_ge(S["m_S"], NT * L + n + 1)
                    dve.wait_ge(S["m_w"], START + NT * L + n + 1)
                    for d in range(2):
                        ins = dve.tensor_tensor(wt[:, d].rearrange("p a b -> p (a b)"), ps[:, 1, :],
                                                wt[:, d].rearrange("p a b -> p (a b)"), ALU.mult)
                    ins.then_inc(S["m_sw"], 1)
                    dve.wait_ge(S["m_num"], START + NT * L + n + 1)
                    v = lambda b: ps[:, b, 0:2 * PV].rearrange("p (a b) -> p a b", b=VE)
                    for d in range(2):
                        dve.tensor_tensor(hn[:, d], v(6 + d), b2(cols[:, c, 2, 32 * d:32 * d + MH], VE), ALU.mult)
                    dve.drain()
                    for d in range(2):
                        dve.tensor_tensor(hn[:, d], hn[:, d], v(4 + d), ALU.add)
                    dve.drain()
                    dve.scalar_tensor_tensor(den[:, 0], hn[:, :, :, HD], -1.0, hn[:, :, :, HD], ALU.mult, ALU.max)
                    dve.drain()
                    for d in range(2):
                        dve.tensor_tensor(den[:, 0, d], den[:, 0, d], cols[:, c, 3, 32 * d:32 * d + MH], ALU.max)
                    dve.drain()
                    dve.reciprocal(den[:, 1], den[:, 0])
                    dve.drain()
                    for d in range(2):
                        dve.tensor_tensor(hh[:, d], hn[:, d, :, 0:HD], b2(den[:, 1, d], HD), ALU.mult)
                    dve.drain()
                    dve.tensor_tensor(hh[:, 0], hh[:, 0], hh[:, 1], ALU.add)
                    dve.drain()
                    dve.tensor_tensor(z[:, c, ZOM:ZOM + 256], hh[:, 0].rearrange("p a b -> p (a b)"), og[:],
                                      ALU.mult).then_inc(S["m_fin"], 1)

                with dve.Fori(0, NS) as c:
                    mlstm(c, c)
                mlstm(NS, NS)
                phase(dve, L, 4)
                with dve.Fori(0, NT) as t:
                    dve.bn_stats(st6[:, t, 0], z[:, t, ZVG:ZVG + 256])
                dve.drain()
                for t in range(NT):
                    dve.bn_aggr(mv[:, t], st6[:, t, 0])
                dve.drain()
                dve.tensor_scalar(rs[:], mv[:, :, 1], EPS, None, ALU.add).then_inc(S["pow_in"], 1)
                dve.wait_ge(S["pow_out"], 4 * L + 1)
                dve.wait_ge(S["gm_ld"], 48 * L + 48)
                own(dve)
                with dve.Fori(0, NT) as t:
                    dve.tensor_scalar(vn[:, t], z[:, t, ZVG:ZVG + 256], mv[:, t, 0:1], rs[:, bass.ds(t, 1)], ALU.subtract, ALU.mult)
                    dve.drain()
                    dve.tensor_tensor(vn[:, t], vn[:, t], glnb[:, 0], ALU.mult)
                    dve.drain()
                    dve.tensor_tensor(vn[:, t], vn[:, t], glnb[:, 1], ALU.add).then_inc(S["gm_vn"], 1)
                with dve.Fori(0, 3) as i:
                    for u in range(3):
                        dve.wait_ge(S["gm_ps"], NT * L + 3 * i + u + 1)
                        dve.tensor_tensor(gs[:, u].rearrange("p (a b) -> p a b", b=HD),
                                          ps[:, u, 0:256].rearrange("p (a b) -> p a b", b=HD), b2(bst[:], HD), ALU.add)
                        dve.drain()
                        ug = z[:, 3 * i + u, ZUG:ZUG + 256]
                        dve.tensor_tensor(ug, ug, gs[:, u], ALU.mult).then_inc(S["gm_vn"], 1)
                phase(dve, L, 5)

                with dve.Fori(0, NT) as t:
                    dve.tensor_tensor(pr[:, 0, 0:640], z[:, t, ZQ:ZQ + 640], z[:, t, ZQ:ZQ + 640], ALU.mult)
                    dve.drain()
                    dve.tensor_reduce(ss[:, t], pr[:, 0, 0:640].rearrange("p (a b) -> p a b", b=HD), AX.X, ALU.add)
                    dve.drain()
                dve.tensor_scalar(ss[:], ss[:], 1.0 / HD, EPS, ALU.mult, ALU.add).then_inc(S["pow_in"], 1)
                dve.wait_ge(S["at_ld"], 48 * L + 48)
                dve.wait_ge(S["v_hi"], L + 1)
                for v in range(HKV):
                    c = v * HD
                    for o_, i_ in ((vst[:, v, 0:NS], z[:, 0:NS, ZV + c:ZV + c + HD]), (vst[:, v, 8], kvt[:, 1, c:c + HD]),
                                   (vst[:, v, 9], z[:, NS, ZV + c:ZV + c + HD])):
                        o_h, o_l = (o_[:, :, 0:HD], o_[:, :, HD:P]) if len(o_.shape) == 3 else (o_[:, 0:HD], o_[:, HD:P])
                        dve.tensor_tensor(o_l, i_, o_h.bitcast(F32), ALU.subtract)
                dve.wait_ge(S["pow_out"], 4 * L + 2)
                own(dve)

                def normed(t, nh, c0, k0, which, extra):
                    o_ = qn[:, 0:nh * HD].rearrange("p (a b) -> p a b", b=HD)
                    dve.tensor_tensor(o_, z[:, t, c0:c0 + nh * HD].rearrange("p (a b) -> p a b", b=HD),
                                      b2(ss[:, t, k0:k0 + nh], HD), ALU.mult)
                    dve.drain()
                    dve.scalar_tensor_tensor(o_, o_, extra, spread(gq[:, which], nh), ALU.mult, ALU.mult)
                    dve.drain()

                def rotated(u, nh):
                    o_ = qn[:, 0:nh * HD].rearrange("p (a b) -> p a b", b=HD)
                    dve.tensor_tensor(qd[:, 0:nh, 0], o_, spread(rp[:, u, 0], nh), ALU.mult)
                    for r in range(2):
                        h_ = HD // 2
                        q4 = o_[:, :, r * h_:(r + 1) * h_].rearrange("p a (b c) -> p a b c", b=2)
                        d4 = qd[:, 0:nh, 1, r * h_:(r + 1) * h_].rearrange("p a (b c) -> p a b c", b=2)
                        s4 = rp[:, u, 1, r * h_:(r + 1) * h_].rearrange("p (b c) -> p b c", b=2)
                        dve.tensor_tensor(d4, q4[:, :, ::-1, :], spread(s4, nh), ALU.mult)
                    dve.drain()
                    dve.tensor_tensor(qd[:, 0:nh, 0], qd[:, 0:nh, 0], qd[:, 0:nh, 1], ALU.add)
                    dve.drain()
                    return dve.tensor_copy(qd[:, 0:nh, 1], qd[:, 0:nh, 0])

                def keys_lo(tile, n):
                    dve.wait_ge(S["k_hi"], 10 * L + n + 1)
                    dve.tensor_tensor(kst[HD:P, :, bass.ds(tile * P, P)], ps[HD:P, 0, 0:2 * P].rearrange("p (a b) -> p a b", b=P),
                                      q_hi[HD:P, 0:2].bitcast(F32), ALU.subtract).then_inc(S["k_lo"], 1)

                with dve.Fori(0, 4) as i:
                    for u in range(2):
                        t = 2 * i + u
                        dve.wait_ge(S["kd_ps"], START + 10 * L + t)
                        normed(t, HKV, ZK, HQ, 1, 1.0)
                        dve.wait_ge(rp_ld[u], 16 * (8 * L + i + 1))
                        rotated(u, HKV).then_inc(S["kd_done"], 1)
                        keys_lo(t, t)
                dve.wait_ge(S["kd_ps"], START + 10 * L + 8)
                dve.tensor_copy(qd[:, 0:HKV], kvt[:, 0].rearrange("p (a b) -> p a b", b=HD).unsqueeze(2)
                                .broadcast_to([P, HKV, 2, HD])).then_inc(S["kd_done"], 1)
                keys_lo(8, 8)
                dve.wait_ge(S["kd_ps"], START + 10 * L + 9)
                normed(NS, HKV, ZK, HQ, 1, 1.0)
                dve.tensor_copy(qd[:, 0:HKV], qn[:, 0:P].rearrange("p (a b) -> p a b", b=HD).unsqueeze(2)
                                .broadcast_to([P, HKV, 2, HD])).then_inc(S["kd_done"], 1)
                keys_lo(9, 9)
                phase(dve, L, 6)

                def att(cur, prev, t, prep):
                    for n in range(HQ):
                        hs = 72 * L + HQ * t + n
                        if cur:
                            if n % HG == 0:
                                dve.wait_ge(S["q_hi_done"], 18 * L + 2 * t + n // HG + 1)
                                dve.tensor_tensor(q_lo[:], ps[:, 7, :].rearrange("p (a b) -> p a b", b=P),
                                                  q_hi[:].bitcast(F32), ALU.subtract).then_inc(S["q_lo_done"], 1)
                            dve.wait_ge(S["s_ps"], START + hs + 1)
                            dve.wait_ge(S["ex_done"], START + hs - 1)
                            i_ = ps[:, 0:3, 0:GRP] if cur == NT else ps[:, 0:1, 0:P]
                            dve.tensor_reduce(nm[:, n % 2:n % 2 + 1], i_, AX.XY, ALU.max, negate=True).then_inc(S["mx_done"], 1)
                        what = cur if n > 1 else prev
                        if what:
                            m = (n - 2) % HG
                            dve.wait_ge(S["p_hi_done"], hs - 1)
                            if what == NT:
                                dve.tensor_tensor(p_lo[:, :, m].rearrange("p (a b) c -> p a b c", b=3),
                                                  ps[:, 3:6, 0:GRP].rearrange("p a (b c) -> p a b c", c=P),
                                                  p_hi[:, :, m].rearrange("p (a b) c -> p a b c", b=3).bitcast(F32),
                                                  ALU.subtract).then_inc(S["p_lo_done"], 1)
                            else:
                                dve.tensor_tensor(p_lo[:, 0, m], ps[:, 3, 0:P], p_hi[:, 0, m].bitcast(F32),
                                                  ALU.subtract).then_inc(S["p_lo_done"], 1)
                        if n % HG == 3 and (cur if n > 3 else prev):
                            g = (n // HG + 1) % 2
                            tt = t if n > 3 else t - 1
                            dve.reciprocal(rinv[:], rsum[:, g * HG:(g + 1) * HG])
                            dve.wait_ge(S["ot_cp"], 18 * L + 2 * t + n // HG)
                            o3 = z[:, tt, ZQ + g * 256:ZQ + g * 256 + 256].rearrange("p (a b) -> p a b", b=HD)
                            dve.tensor_tensor(o3, o_s[:, 0:256].rearrange("p (a b) -> p a b", b=HD),
                                              ps[:, 7, :].rearrange("p (a b) -> p a b", b=P)[:, :, HD:P], ALU.add)
                            dve.drain()
                            dve.tensor_tensor(o3, o3, b2(rinv[:], HD), ALU.mult).then_inc(S["oy_done"], 1)
                        if n == 5 and prep:
                            prep()

                normed(0, HQ, ZQ, 0, 0, HD ** -0.5)
                dve.wait_ge(rp_ld[0], 16 * (8 * L + 5))
                rotated(0, HQ).then_inc(S["qd_done"], 1)

                def prep_next(t, u, k):
                    def go():
                        dve.wait_ge(S["q_ps"], 18 * L + 2 * t)
                        queries(t, u, k)
                    return go

                def queries(t, u, k):
                    normed(t, HQ, ZQ, 0, 0, HD ** -0.5)
                    if u is None:
                        q3 = qn[:].rearrange("p (a b) -> p a b", b=HD)
                        dve.tensor_copy(qd[:, :, 0], q3)
                        dve.tensor_copy(qd[:, :, 1], q3).then_inc(S["qd_done"], 1)
                    else:
                        dve.wait_ge(rp_ld[u], k)
                        rotated(u, HQ).then_inc(S["qd_done"], 1)

                att(NT, None, 0, prep_next(1, 1, 16 * (8 * L + 5)))
                with dve.Fori(0, 3) as i:
                    att(NT, NT, 2 * i + 1, prep_next(2 * i + 2, 0, 16 * (8 * L + i + 6)))
                    att(NT, NT, 2 * i + 2, prep_next(2 * i + 3, 1, 16 * (8 * L + i + 6)))
                att(NT, NT, 7, prep_next(8, None, None))
                att(1, NT, NS, None)
                att(None, 1, NT, None)
                phase(dve, L, 7)
                for t in range(NT):
                    dve.wait_ge(S["y_hi"], NT * L + t + 1)
                    for k in range(2):
                        r = (slice(None), slice(4 * k, 4 * k + 4), slice(t * P, (t + 1) * P))
                        ins = dve.tensor_tensor(lo[r], ps[:, 2 * (t % 3) + k, :].rearrange("p (a b) -> p a b", b=P),
                                                hi[r].bitcast(F32), ALU.subtract)
                    ins.then_inc(S["y_lo"], 1)
                phase(dve, L, 8)

                def residual(n, t):
                    k = 18 * L + 9 * n + t
                    g = int(t < NS)
                    dve.wait_ge(S["o_out"], START + k + 1)
                    dve.tensor_tensor(lnt[:, (n + t) % 2], ps[:, t % 3, :], gate[:, g, bass.ds(n * W, W)], ALU.mult)
                    dve.drain()
                    r = xr[:, t, bass.ds(n * W, W)]
                    dve.scalar_tensor_tensor(r, r, ALPHA, lnt[:, (n + t) % 2], ALU.mult, ALU.add).then_inc(S["xr_half"], 1)

                dve.wait_ge(S["ln_ld"], 16 * (13 * L + 7))
                own(dve)
                for n in range(2):
                    for t in range(NT - 1):
                        residual(n, t)
                    split_lo(dve, L, 6 + n)
                    residual(n, NT - 1)
                dve.drain()
                layer_norm(L, 2, xr, lnb, S["xr_done"])
                phase(dve, L, 9)
                for t in range(NT):
                    modulate(L, NT + t, 1, hf2, t % 3, int(t < NS))
                phase(dve, L, 10)

                def hidden(i, b):
                    n = 12 * (NFF * L + i) + b
                    dve.wait_ge(S["r_done"], START + n + 1)
                    dve.tensor_tensor(fsq[:, b % 2], fr[:, b % 2], fr[:, b % 2], ALU.mult)
                    dve.drain()
                    r = (slice(None), b // 3, slice((b % 3) * GRP, (b % 3 + 1) * GRP))
                    dve.wait_ge(S["fhi_done"], n + 1)
                    dve.tensor_tensor(f_lo[r], fsq[:, b % 2], f_hi[r].bitcast(F32), ALU.subtract).then_inc(S["flo_done"], 1)

                def summed(i, b):
                    n = 18 * (NFF * L + i) + b
                    dve.wait_ge(S["f_ps"], START + n + 1)
                    a = acc[:, b // 2, (b % 2) * W:(b % 2 + 1) * W]
                    dve.tensor_tensor(a, a, ps[:, 3 + b % 3, :], ALU.add).then_inc(S["f_acc"], 1)

                dve.wait_ge(S["acc_zero"], L + 1)
                own(dve)
                with dve.Fori(0, NFF) as i:
                    for b in range(11):
                        hidden(i, b)
                    split_lo(dve, L, 2 * i + 8)
                    hidden(i, 11)
                    for b in range(17):
                        summed(i, b)
                    split_lo(dve, L, 2 * i + 9)
                    summed(i, 17)
                    dve.drain()
                phase(dve, L, 11)
                dve.wait_ge(S["ln_ld"], 16 * (13 * L + 13))
                own(dve)

                def residual2(n, k, u, g):
                    a = acc[:, n]
                    dve.tensor_tensor(a, a, gate2[:, g], ALU.mult)
                    dve.drain()
                    dve.wait_ge(x1_ld[u], 16 * (3 * L + k + 1))
                    dve.scalar_tensor_tensor(a, x1t[:, u], ALPHA, a, ALU.mult, ALU.add).then_inc(S["x1_used"], 1)

                with dve.Fori(0, 2) as i:
                    for u in range(3):
                        residual2(3 * i + u, i, u, 1)
                for u in range(3):
                    residual2(6 + u, 2, u, int(u < 2))
                dve.drain()
                layer_norm(L, 3, acc, lnb2, S["y_rdy"])
                phase(dve, L, 12)

        @block.tensor
        def _(pe):
            for n in ("mod_ps", "u_ps", "m_tp", "m_num", "z_ps", "f_ps", "h_ps", "o_out", "kd_ps", "s_ps", "t_ps", "o_ps", "w_used"):
                if n != "mod_ps":
                    pe.sem_inc(S[n], START)
            pe.wait_ge(S["const_ld"], 48)
            pe.wait_ge(S["mod_ready"], 1)
            own(pe)
            with pe.Fori(0, NL * 12 // 2) as i:
                for u in range(2):
                    pe.wait_ge(mod_w_ld[u], 16 * i + 16)
                    pe.wait_ge(S["mod_row"], START + 2 * i + u - 1)
                    for k in range(KT):
                        mm = pe.matmul(ps[0:2, u, :], sc[:, k, :], modw[:, u, k, :], start=(k == 0), stop=(k == KT - 1))
                    mm.then_inc(S["mod_ps"], 1)
            phase(pe, 0, -1)

            def product(out, a_hi, a_lo, b_hi, b_lo, first, last, used=None):
                mm = pe.matmul(out, a_hi, b_hi, start=first, stop=False)
                if used is not None:
                    mm.then_inc(used, 1)
                pe.matmul(out, a_hi, b_lo, start=False, stop=False)
                return pe.matmul(out, a_lo, b_hi, start=False, stop=last)

            def dense(L, g, t, bank, cols_, wait_w, last_tile, done):
                out = ps[:, bank, 0:cols_]
                a = slice(t * P, (t + 1) * P)
                for k in range(KT):
                    if wait_w:
                        pe.wait_ge(S["w_lo_done"], slot(L, g, k) + 1)
                    mm = product(out, hi[:, k, a], lo[:, k, a], w_hi[:, k, 0:cols_], w_lo[:, k, 0:cols_],
                                 k == 0, k == KT - 1, S["w_used"] if last_tile and k else None)
                mm.then_inc(done, 1)

            with pe.Fori(0, NL) as L:
                pe.wait_ge(S["mc_ld"], 32 * L + 32)
                own(pe)
                pe.transpose(ps[:, 7, 0:64], mod64[:, :], ident[0:64, 0:64]).then_inc(S["mc_ps"], 1)
                with pe.Fori(0, 3) as i:
                    for u in range(3):
                        pe.wait_ge(xt_ld[u], 16 * (3 * L + i + 1))
                        pe.wait_ge(S["hf_done"], START + 2 * NT * L + 3 * i + u - 2)
                        for k in range(KT):
                            mm = pe.transpose(ps[:, 2 * u + k // 4, (k % 4) * P:(k % 4 + 1) * P], xt[:, u, k * P:(k + 1) * P], ident[:])
                        mm.then_inc(S["xT_ps"], 1)
                phase(pe, L, 0)
                for g in range(3):
                    a = slice(g * GRP, (g + 1) * GRP)
                    for k in range(KT):
                        if g == 0:
                            pe.wait_ge(S["w_lo_done"], slot(L, 0, k) + 1)
                        mm = product(ps[:, 4 + g, 0:GRP], w_hi[:, k, 256:384], w_lo[:, k, 256:384], hi[:, k, a], lo[:, k, a],
                                     k == 0, k == KT - 1)
                    mm.then_inc(S["g_ps"], 1)
                for t in range(NT):
                    pe.wait_ge(S["z_done"], START + 45 * L + t - 2)
                    dense(L, 0, t, t % 3, 256, False, t == NT - 1, S["z_ps"])
                with pe.Fori(0, 4) as c:
                    for t in range(NT):
                        pe.wait_ge(S["z_done"], START + 45 * L + 9 * c + 9 + t - 2)
                        dense(L, c + 1, t, t % 3, W, t == 0, t == NT - 1, S["z_ps"])
                phase(pe, L, 1)
                pe.wait_ge(S["act_row"], 2 * L + 2)
                own(pe)
                for t in range(NT):
                    for q, r in enumerate((ri, rf, r_r, r_d)):
                        o = (t % 3) * 4 * ROWS + q * ROWS
                        pe.transpose(ps[:, t // 3, o:o + ROWS], r[:, t * P:(t + 1) * P], ident[0:ROWS, 0:ROWS])
                pe.wait_ge(S["ml_ld"], 48 * L + 48)
                for j in range(4):
                    mm = pe.matmul(ps[:, 3, j * NT:(j + 1) * NT], selc[0:ROWS, 8 + j], mrow[:, 4], start=True, stop=True)
                mm.then_inc(S["rt_ps"], 1)
                phase(pe, L, 2)

                def states(n):
                    pe.wait_ge(S["u_v"], NT * L + n + 1)
                    pe.wait_ge(S["u_kw"], NT * L + n + 1)
                    pe.wait_ge(S["u_done"], START + NT * L + n)
                    for d in range(2):
                        for p_ in range(2):
                            mm = pe.matmul(ps[:, d, p_ * PV:(p_ + 1) * PV], kw[:, d, p_ * P:(p_ + 1) * P],
                                           vext[:, 2 * p_:2 * p_ + 2, :].rearrange("p a b -> p (a b)"), start=True, stop=True)
                    mm.then_inc(S["u_ps"], 1)

                with pe.Fori(0, NS) as c:
                    states(c)
                states(NS)
                phase(pe, L, 3)

                def mlstm(c, n, s_f, s_b):
                    pe.wait_ge(S["m_w"], START + NT * L + n)
                    for d in range(2):
                        for h in range(MH):
                            pe.matmul(ps[:, 2 + d, h * P:(h + 1) * P], selc[0:ROWS, d * MH + h],
                                      r_m[:, bass.ds(c * P, P)], start=(h == 0), stop=False, skip_group_check=True)
                        mm = pe.matmul(ps[:, 2 + d, :], idr[:], mkr[:, d].unsqueeze(1).broadcast_to([P, MH, P]),
                                       start=False, stop=True, skip_group_check=True)
                    mm.then_inc(S["m_D"], 1)
                    pe.wait_ge(S["m_st"], NT * L + n + 1)
                    pe.wait_ge(S["m_qk"], START + NT * L + n)
                    for p_ in range(2):
                        pe.transpose(ps[:, 0, p_ * P:(p_ + 1) * P], qs[:, p_ * P:(p_ + 1) * P], ident[:])
                        mm = pe.transpose(ps[:, 0, (2 + p_) * P:(3 + p_) * P], ks[:, p_ * P:(p_ + 1) * P], ident[:])
                    mm.then_inc(S["m_tp"], 1)
                    pe.wait_ge(S["m_qk"], START + NT * L + n + 1)
                    pe.wait_ge(S["m_sw"], START + NT * L + n)
                    for p_ in range(2):
                        mm = pe.matmul(ps[:, 1, p_ * 256:(p_ + 1) * 256], kT[:, p_],
                                       qbd[:, p_].rearrange("p a b -> p (a b)"), start=True, stop=True)
                    mm.then_inc(S["m_S"], 1)
                    pe.wait_ge(S["m_fin"], START + NT * L + n)
                    for d, s_ in enumerate((s_f, s_b)):
                        for p_ in range(2):
                            pe.matmul(ps[:, 6 + d, p_ * PV:(p_ + 1) * PV], qT[:, p_], cs[:, s_, d, p_], start=True, stop=True)
                    pe.wait_ge(S["m_sw"], START + NT * L + n + 1)
                    for d in range(2):
                        for h in range(MH):
                            mm = pe.matmul(ps[:, 4 + d, h * VE:(h + 1) * VE], wt[:, d, h], vext[:, h], start=True, stop=True)
                    mm.then_inc(S["m_num"], 1)

                with pe.Fori(0, NS) as c:
                    mlstm(c, c, c, 7 - c)
                mlstm(NS, NS, 9, 9)
                phase(pe, L, 4)
                with pe.Fori(0, 3) as i:
                    for u in range(3):
                        pe.wait_ge(S["gm_vn"], START + 18 * L + 3 * i + u + 1)
                        for g in range(4):
                            mm = pe.matmul(ps[:, u, g * HD:(g + 1) * HD], wst[:, g], vn[:, 3 * i + u, g * HD:(g + 1) * HD],
                                           start=True, stop=True)
                        mm.then_inc(S["gm_ps"], 1)
                        if u == 2:
                            pe.wait_ge(S["gm_vn"], START + 18 * L + NT + 3 * i + 3)
                phase(pe, L, 5)

                def keys(n):
                    pe.wait_ge(S["kd_done"], START + 10 * L + n + 1)
                    pe.wait_ge(S["k_lo"], START + 10 * L + n)
                    for v in range(HKV):
                        mm = pe.transpose(ps[:, 0, v * P:(v + 1) * P], qd[:, v].rearrange("p a b -> p (a b)"), ident[:])
                    mm.then_inc(S["kd_ps"], 1)

                with pe.Fori(0, 10) as n:
                    keys(n)
                phase(pe, L, 6)

                def att(cur, prev, t):
                    for n in range(HQ):
                        hs = 72 * L + HQ * t + n
                        if cur and n % HG == 0:
                            g2 = 18 * L + 2 * t + n // HG
                            if n == 0:
                                pe.wait_ge(S["qd_done"], NT * L + t + 1)
                            pe.wait_ge(S["oy_done"], START + g2 - 1)
                            for h in range(HG):
                                mm = pe.transpose(ps[:, 7, h * P:(h + 1) * P], qd[:, n + h].rearrange("p a b -> p (a b)"), ident[:])
                            mm.then_inc(S["q_ps"], 1)
                            pe.wait_ge(S["q_lo_done"], START + g2 + 1)
                        if cur:
                            pe.wait_ge(S["ex_done"], START + hs)
                            k0 = 0 if cur == NT else 9 * P
                            for b in range(3 if cur == NT else 1):
                                w_ = GRP if cur == NT else P
                                rhs = kst[:, n // HG, k0 + b * w_:k0 + (b + 1) * w_]
                                pe.matmul(ps[:, b, 0:w_], q_hi[:, n % HG], rhs, start=True, stop=False)
                                mm = pe.matmul(ps[:, b, 0:w_], q_lo[:, n % HG], rhs, start=False, stop=True)
                            mm.then_inc(S["s_ps"], 1)
                        if n % HG == 2 and (cur if n > 2 else prev):
                            g2 = 18 * L + 2 * t + n // HG
                            pe.wait_ge(S["o_cp"], START + g2)
                            if cur:
                                pe.wait_ge(S["q_lo_done"], START + g2 + 1)
                            for h in range(HG):
                                mm = pe.transpose(ps[:, 7, h * P:(h + 1) * P], o_s[:, h * P:(h + 1) * P], ident[:])
                            mm.then_inc(S["ot_ps"], 1)
                        what = cur if n else prev
                        if what:
                            pe.wait_ge(S["ex_done"], START + hs)
                            pe.wait_ge(S["p_lo_done"], START + hs - 1)
                            m = (n - 1) % 2
                            for j in range(what):
                                mm = pe.transpose(ps[:, 3 + j // 3, (j % 3) * P:(j % 3 + 1) * P], pr[:, m, j * P:(j + 1) * P], ident[:])
                            mm.then_inc(S["t_ps"], 1)
                        if n % HG == 1 and (cur if n > 1 else prev):
                            what = prev if n == 1 else cur
                            pe.wait_ge(S["o_cp"], START + 18 * L + 2 * t + n // HG - 1)
                            g = (n // HG + 1) % 2
                            pe.wait_ge(S["p_lo_done"], START + hs - 1)
                            k0 = 0 if what == NT else 9
                            for j in range(what):
                                pe.matmul(ps[:, 6, :], vst[:, g, k0 + j], p_hi[:, j].rearrange("p a b -> p (a b)"), start=(j == 0), stop=False)
                                mm = pe.matmul(ps[:, 6, :], vst[:, g, k0 + j], p_lo[:, j].rearrange("p a b -> p (a b)"),
                                               start=False, stop=(j == what - 1))
                            mm.then_inc(S["o_ps"], 1)

                att(NT, None, 0)
                with pe.Fori(1, NS) as t:
                    att(NT, NT, t)
                att(1, NT, NS)
                att(None, 1, NT)
                phase(pe, L, 7)
                for t in range(NT):
                    pe.wait_ge(S["y_lo"], START + NT * L + t - 2)
                    for k in range(KT):
                        c = (ZQ + k * P) if k < 4 else (ZOM + (k - 4) * P) if k < 6 else (ZUG + (k - 6) * P)
                        mm = pe.transpose(ps[:, 2 * (t % 3) + k // 4, (k % 4) * P:(k % 4 + 1) * P], z[:, t, c:c + P], ident[:])
                    mm.then_inc(S["yT_ps"], 1)
                phase(pe, L, 8)
                with pe.Fori(0, 2) as n:
                    for t in range(NT):
                        pe.wait_ge(S["xr_half"], START + 18 * L + 9 * n + t - 2)
                        dense(L, n + 5, t, t % 3, W, t == 0, t == NT - 1, S["o_out"])
                phase(pe, L, 9)
                for t in range(NT):
                    pe.wait_ge(S["hf_done"], START + 2 * NT * L + NT + t - 2)
                    for k in range(KT):
                        mm = pe.transpose(ps[:, 2 * (t % 3) + k // 4, (k % 4) * P:(k % 4 + 1) * P], xr[:, t, k * P:(k + 1) * P], ident[:])
                    mm.then_inc(S["xT_ps"], 1)
                phase(pe, L, 10)
                with pe.Fori(0, NFF) as i:
                    for b in range(12):
                        n = 12 * (NFF * L + i) + b
                        m, g = b // 3, b % 3
                        a = slice(g * GRP, (g + 1) * GRP)
                        pe.wait_ge(S["r_done"], START + n - 2)
                        for k in range(KT):
                            if b == 0:
                                pe.wait_ge(S["w_lo_done"], slot(L, 2 * i + 7, k) + 1)
                            mm = product(ps[:, g, 0:GRP], w_hi[:, k, m * P:(m + 1) * P], w_lo[:, k, m * P:(m + 1) * P],
                                         hi[:, k, a], lo[:, k, a], k == 0, k == KT - 1, S["w_used"] if b == 11 and k else None)
                        mm.then_inc(S["h_ps"], 1)
                    for b in range(18):
                        n = 18 * (NFF * L + i) + b
                        t, hf_ = b // 2, b % 2
                        a = slice(t * P, (t + 1) * P)
                        if b in (0, 6, 12):
                            pe.wait_ge(S["flo_done"], START + 12 * (NFF * L + i) + 10 + b // 6)
                        pe.wait_ge(S["f_acc"], START + n - 2)
                        for m in range(4):
                            if t == 0:
                                pe.wait_ge(S["w_lo_done"], slot(L, 2 * i + 8, 4 * hf_ + m) + 1)
                            mm = product(ps[:, 3 + b % 3, :], f_hi[:, m, a], f_lo[:, m, a], w_hi[:, 4 * hf_ + m, :], w_lo[:, 4 * hf_ + m, :],
                                         m == 0, m == 3, S["w_used"] if t == NT - 1 and (m or hf_) else None)
                        mm.then_inc(S["f_ps"], 1)
                phase(pe, L, 11)
                phase(pe, L, 12)


_INS = ["x_in", "cond", "w_mod", "b_mod", "w_slots", "consts", "rope", "cache_k", "cache_v", "state0", "row_in",
        "qk_g", "gln", "ws_t", "bs_t", "ln_gb"]
_OUTS = [(NT, P, D), (NL, P, P), (NL, P, P), (NL, 2, MH, HD, HD), (NL, 2, MH, HD, 1), (NL, 2, MH, 1)]


def layout(x_prompt, x_sample, c, cache_attn_k, cache_attn_v, state_mlstm_C, state_mlstm_n, state_mlstm_m,
           c_ctx, w_mod, b_mod, w_in, q_norm_g, k_norm_g, mlstm_gate_b, gmlp_ln_g, gmlp_ln_b, gmlp_ws, gmlp_bs,
           w_out, ln1_g, ln1_b, w_ff1, w_ff2, ln2_g, ln2_b):
    f = np.float32
    a = {k: np.asarray(v) for k, v in locals().items() if k != "f"}
    out = {}
    out["x_in"] = np.concatenate([a["x_sample"].reshape(NS, P, D), a["x_prompt"].reshape(1, P, D)])
    out["cond"] = np.stack([a["c_ctx"].reshape(KT, P), a["c"].reshape(KT, P)], -1).transpose(1, 0, 2)
    out["w_mod"] = a["w_mod"].reshape(NL, KT, P, 12, W).transpose(0, 3, 2, 1, 4).reshape(NL * 12, P, KT, W)
    out["b_mod"] = np.broadcast_to(a["b_mod"].reshape(1, NL * 12, W), (2, NL * 12, W))
    o = np.cumsum([0, 512, 128, 128, 256, 256, 256, 256, 16, 256, 256])
    qa, ka, va, qm, km, vm, om, gm, ug, vg = (a["w_in"][:, :, o[i]:o[i + 1]] for i in range(10))
    first = np.zeros((NL, D, W), f)
    first[:, :, 0:256] = ug
    for kind, at in ((0, 256), (2, 256 + 32), (1, 256 + 64), (3, 256 + 96)):
        first[:, :, at:at + MH] = gm[:, :, kind * MH:(kind + 1) * MH]
    slots = np.zeros(((NL * GROUPS + 1) * SLOTS, P, W), f)
    for l in range(NL):
        groups = [first[l], np.concatenate([qm[l], km[l]], -1), np.concatenate([vm[l], om[l]], -1), qa[l],
                  np.concatenate([ka[l], va[l], vg[l]], -1), a["w_out"][l][:, :W], a["w_out"][l][:, W:]]
        groups = [g.reshape(KT, P, W) for g in groups]
        for i in range(NFF):
            groups.append(a["w_ff1"][l][:, i * HC:(i + 1) * HC].reshape(KT, P, W))
            w2 = a["w_ff2"][l][i * HC:(i + 1) * HC].reshape(HC // P, P, 2, W)
            groups.append(w2.transpose(2, 0, 1, 3).reshape(SLOTS, P, W))
        for g, v in enumerate(groups):
            s = (l * GROUPS + g) * SLOTS
            slots[s:s + SLOTS] = v
    out["w_slots"] = slots
    out["consts"] = constants()
    out["rope"] = rope_tables()
    out["cache_k"] = a["cache_attn_k"].reshape(NL, P, P)
    out["cache_v"] = a["cache_attn_v"].reshape(NL, P, P)
    s0 = np.zeros((NL, 2, HD, 2, 2, 2, VE), f)
    C, n = a["state_mlstm_C"][0], a["state_mlstm_n"][0]
    for h in range(MH):
        s0[:, h % 2, :, :, h // 2, h % 2, 0:HD] = C[:, :, h].transpose(0, 2, 1, 3)
        s0[:, h % 2, :, :, h // 2, h % 2, HD] = n[:, :, h].transpose(0, 2, 1)
    out["state0"] = s0.reshape(NL, P, 2, 2, PV)
    r = np.zeros((NL, ROWS, 3), f)
    gb, m = a["mlstm_gate_b"], a["state_mlstm_m"][0]
    for d in range(2):
        r[:, 32 * d:32 * d + MH, 0] = gb[:, 2 * d]
        r[:, 32 * d:32 * d + MH, 1] = gb[:, 2 * d + 1]
        r[:, 32 * d:32 * d + MH, 2] = m[:, d]
    out["row_in"] = r

    def rows(v):
        return np.broadcast_to(v[:, None], (NL, P, *v.shape[1:]))
    out["qk_g"] = rows(np.stack([a["q_norm_g"], a["k_norm_g"]], 1))
    out["gln"] = rows(np.stack([a["gmlp_ln_g"], a["gmlp_ln_b"]], 1))
    out["ws_t"] = a["gmlp_ws"].transpose(0, 3, 1, 2)
    out["bs_t"] = a["gmlp_bs"].transpose(0, 2, 1)
    out["ln_gb"] = np.stack([a["ln1_g"], a["ln1_b"], a["ln2_g"], a["ln2_b"]], 1)
    return {k: np.ascontiguousarray(out[k]) for k in _INS}


def program(nc, arrays):
    args = [nc.dram_tensor(f"in_{n}", v.shape, F32, kind="ExternalInput").ap() for n, v in arrays.items()]
    args += [nc.dram_tensor(f"out_{i}", s, F32, kind="ExternalOutput").ap() for i, s in enumerate(_OUTS)]
    build(nc, *args)


def kernel(**inputs):
    import concourse.bacc as bacc
    from concourse.bass_utils import run_bass_kernel_spmd
    arrays = layout(**inputs)
    nc = bacc.Bacc("TRN2", target_bir_lowering=False, num_devices=1)
    program(nc, arrays)
    r = run_bass_kernel_spmd(nc, [{f"in_{n}": v for n, v in arrays.items()}], core_ids=[0])
    y, k, v, c, n, m = (r.results[0][f"out_{i}"] for i in range(len(_OUTS)))
    return (y[NS:NT].reshape(1, SEQ, D), y[0:NS].reshape(1, DEC_SEQ, D),
            k.reshape(1, NL, SEQ, HKV, HD), v.reshape(1, NL, SEQ, HKV, HD),
            c.reshape(1, NL, 2, MH, HD, HD), n.reshape(1, NL, 2, MH, HD), m.reshape(1, NL, 2, MH))
```

```python
from contextlib import ExitStack

import numpy as np

import concourse.bass as bass
from concourse import mybir

ALU = mybir.AluOpType
ACT = mybir.ActivationFunctionType
AX = mybir.AxisListType
F32 = mybir.dt.float32
F32R = mybir.dt.float32r

P = 128
D = 1024
KT = D // P
SEQ = 128
DEC_SEQ = 1024
NS = DEC_SEQ // P
NT = NS + 1
TOK = NT * P
GRP = 3 * P
NL = 2
HD = 64
HQ, HKV = 8, 2
HG = HQ // HKV
MH = 4
FF = 4 * D
HC = 4 * P
NFF = FF // HC
W = 512
EPS = 1e-6
M_SCALE = HD ** -0.5
ALPHA = (2 * NL) ** 0.25
NEG = -1e30

ZQM, ZKM, ZVM, ZOM, ZQ, ZK, ZV, ZVG, ZUG = 0, 256, 512, 768, 1024, 1536, 1664, 1792, 2048
ZW = 2304
SLOTS = 8
G_IN, G_OUT, G_FF = 5, 2, 2 * NFF
GROUPS = G_IN + G_OUT + G_FF
RAW = 4

ROWS = 36
VE = HD + 1
PV = 2 * VE
NG = 2 * NT
N_E = 2 * (NS * NT + 1)
N_A = 2 * (NS * (NT - 1) + 1)
SCORES_AT = {2: 0, 3: 1, 4: 2, 5: 3}
START = 8
NSLOT = 11

C_ID, C_MF, C_MB, C_BM, C_SEL, C_SELP = 0, 128, 256, 384, 514, 514 + 8 * 128
NCONST = C_SELP + 4 * 128


def constants():
    k = np.zeros((P, NCONST), np.float32)
    k[:, C_ID:C_ID + P] = np.eye(P)
    s, t = np.arange(P)[:, None], np.arange(P)[None]
    k[:, C_MF:C_MF + P] = np.where(s <= t, 0.0, NEG)
    k[:, C_MB:C_MB + P] = np.where(s >= t, 0.0, NEG)
    k[:HD, C_BM:C_BM + VE] = 1.0
    k[HD:, C_BM + VE:C_BM + PV] = 1.0
    for d in range(2):
        for h in range(MH):
            r = 32 * d + h
            k[r, C_SEL + (d * MH + h) * P:C_SEL + (d * MH + h + 1) * P] = 1.0
            o = C_SELP + (d * 2 + h // 2) * P + (h % 2) * HD
            k[r, o:o + HD] = 1.0
    return k


def rope_tables():
    n = HD // 4
    inv = (10000.0 ** (-np.arange(n, dtype=np.float32) / n)).astype(np.float32)
    pos = np.arange(DEC_SEQ)
    out = np.zeros((DEC_SEQ, 2, HD), np.float32)
    for i, p in enumerate((pos // 64, pos % 64)):
        ang = (p.astype(np.float32)[:, None] * inv[None]).astype(np.float32)
        c, s = np.cos(ang), np.sin(ang)
        o = i * HD // 2
        out[:, 0, o:o + n], out[:, 0, o + n:o + 2 * n] = c, c
        out[:, 1, o:o + n], out[:, 1, o + n:o + 2 * n] = -s, s
    out = out.reshape(NS, P, 2, HD).transpose(1, 0, 2, 3)
    return np.concatenate([out, out[:, 0:2]], 1)



def build(nc, x_in, cond, w_mod, b_mod, w_slots, consts, rope, cache_k, cache_v, state0, row_in,
          qk_g, gln, ws_t, bs_t, ln_gb, y_out, k_out, v_out, c_out, n_out, m_out):
    x1_dram = nc.dram_tensor("x1_dram", (NT, P, D), F32, kind="Internal").ap()
    mod_dram = nc.dram_tensor("mod_dram", (NL * 12, 2, W), F32, kind="Internal").ap()

    with ExitStack() as ctx:
        a_w = 16512
        a_b = a_w + (2 * SLOTS + RAW) * W * 4
        a_a = a_b + NT * ZW * 4
        a_m = a_a + 2 * KT * TOK * 4
        a_end = 229344

        def region(start, end):
            free = [start]

            def place(name, shape, dt=F32, rows=P):
                t = nc.alloc_sbuf_tensor_at(name, [rows, *shape], dt, offset=free[0])
                free[0] += (int(np.prod(shape)) * 4 + 31) // 32 * 32
                assert free[0] <= end, (name, free[0] - end)
                return t
            return place

        put = region(a_w, a_b)
        w_hi = put("w_hi", [SLOTS, W], F32R)
        w_lo = put("w_lo", [SLOTS, W], F32R)
        w_raw = put("w_raw", [RAW, W])
        put = region(a_b, a_a)
        modw = put("modw", [2, KT, W])
        modb = put("modb", [NL * 12, W], rows=2)
        put = region(a_b, a_a)
        xt = put("xt", [3, D])
        hf = put("hf", [3, D])
        put = region(a_b, a_a)
        z = put("z", [NT, ZW])
        put = region(a_b, a_a)
        xr = put("xr", [NT, D])
        hf2 = put("hf2", [3, D])
        lnb = put("lnb", [2, D])
        gate = put("gate", [2, D])
        lnt = put("lnt", [2, W])
        put = region(a_b, a_a)
        acc = put("acc", [NT, D])
        f_hi = put("f_hi", [HC // P, TOK], F32R)
        f_lo = put("f_lo", [HC // P, TOK], F32R)
        fr = put("fr", [2, GRP])
        fsq = put("fsq", [2, GRP])
        put = region(a_b + NT * D * 4, a_a)
        x1t = put("x1t", [3, D])
        lnb2 = put("lnb2", [2, D])
        gate2 = put("gate2", [2, D])
        put = region(a_a, a_m)
        modr = put("modr", [NL * 12, W], rows=2)
        put = region(a_a, a_m)
        hi = put("hi", [KT, TOK], F32R)
        lo = put("lo", [KT, TOK], F32R)
        put = region(a_a, a_m)
        r_r = put("r_r", [TOK], rows=ROWS)
        r_d = put("r_d", [TOK], rows=ROWS)
        r_b = put("r_b", [TOK], rows=ROWS)
        r_m = put("r_m", [TOK], rows=ROWS)
        cs = put("cs", [NSLOT, 2, 2, PV])
        cols = put("cols", [NT, 4, ROWS])
        selc = put("selc", [12, P])
        bmask = put("bmask", [PV])
        kw = put("kw", [2, 256])
        vext = put("vext", [MH, VE])
        qs = put("qs", [256])
        ks = put("ks", [256])
        qT = put("qT", [2, P])
        kT = put("kT", [2, P])
        qbd = put("qbd", [2, 2, P])
        wt = put("wt", [2, MH, P])
        hn = put("hn", [2, MH, VE])
        hh = put("hh", [2, MH, HD])
        og = put("og", [256])
        dec = put("dec", [8, 2, 2])
        mrow = put("mrow", [5, NT], rows=ROWS)
        den = put("den", [2, 2, MH])
        put = region(a_a, a_m)
        wst = put("wst", [4, P])
        glnb = put("glnb", [2, 256])
        vn = put("vn", [NT, 256])
        gs = put("gs", [3, 256])
        bst = put("bst", [4])
        put = region(a_a, a_m)
        kst = put("kst", [HKV, 10 * P], F32R)
        vst = put("vst", [HKV, 10, P], F32R)
        q_hi = put("q_hi", [2, HG, P], F32R)
        q_lo = put("q_lo", [2, HG, P], F32R)
        pr = put("pr", [3, HG * P])
        p_hi = put("p_hi", [3, HG * P], F32R)
        p_lo = put("p_lo", [3, HG * P], F32R)
        psm = put("psm", [2, HG * P])
        dg = put("dg", [2, HG, P], F32R)
        one_r = put("one_r", [P], F32R)
        sq = put("sq", [3, 640])
        ones = put("ones", [P])
        o_s = put("o_s", [HG * P])
        rp = put("rp", [2, 2, HD])
        put = region(a_m, a_end)
        ident = put("ident", [P])
        idr = put("idr", [P], F32R)
        mkr = put("mkr", [2, P], F32R)
        maskt = put("maskt", [2, P])
        ri = put("ri", [TOK], rows=ROWS)
        rf = put("rf", [TOK], rows=ROWS)
        modc = put("modc", [64])
        mod64 = put("mod64", [P], rows=64)
        sc = put("sc", [KT, 2])
        sce = put("sce", [KT, 2])
        condt = put("condt", [KT, 2])
        rcon = put("rcon", [3], rows=ROWS)
        st6 = put("st6", [NT, 2, 6])
        mv = put("mv", [NT, 2])
        rs = put("rs", [NT])
        half = put("half", [NT * 10])
        nm = put("nm", [2, HG])
        rinv = put("rinv", [HG])
        ss = put("ss", [NT, 10])
        put = region(a_m + 5 * 512, a_m + 5 * 512 + 2 * TOK * 4)
        qd = put("qd", [HQ, 2, HD])
        kvt = put("kvt", [2, P])
        gq = put("gq", [2, HD])
        qn = put("qn", [HQ * HD])
        ps = ctx.enter_context(nc.psum_tensor("ps", [P, 8, 512], F32))

        def sem(name):
            return ctx.enter_context(nc.semaphore(name))

        names = """passed x_copied const_ld mod_b_ld mod_st mod_ready silu_e mod_ps mod_row phase_end
            w_hi_done w_lo_done w_used
            mc_ld mc_ps xT_ps hf_done hi_done h_done row_ld
            z_ps z_done g_ps
            act_row dve_row abs_row pow_in pow_out rt_ps ml_ld ml_zero
            u_v u_kw u_ps u_done m_st m_tp m_qk m_D m_S m_w m_sw m_num m_og m_fin st_out
            gm_ld gm_vn gm_ps
            at_ld v_hi v_rdy kd_done kd_ps k_hi k_lo kv_out
            qd_done q_ps q_hi_done q_lo_done s_ps mx_done dg_done st_ps ex_done p_hi_done p_lo_done sum_done pv_done
            o_cp ot_ps sm_ps rv_done ot_cp oy_done
            yT_ps y_hi y_lo o_out xr_half ln_ld xr_done x1_st
            h_ps r_done fhi_done flo_done f_ps f_acc acc_zero x1_used y_rdy ln_st""".split()
        S = dict((n, sem(n)) for n in names)
        w_ld = [sem(f"w_ld{j}") for j in range(RAW)]
        mod_w_ld = [sem(f"mod_w_ld{j}") for j in range(2)]
        xt_ld = [sem(f"xt_ld{j}") for j in range(3)]
        x1_ld = [sem(f"x1_ld{j}") for j in range(3)]
        rp_ld = [sem(f"rp_ld{j}") for j in range(2)]

        NB = 13

        def own(eng):
            eng.sem_inc(S["passed"], 1)

        def phase(eng, L, b):
            own(eng)
            eng.drain().then_inc(S["phase_end"], 1)
            eng.wait_ge(S["phase_end"], 4 * NB * L + 4 * (b + 2))
            own(eng)

        def counts(L, t, g):
            if isinstance(t, int) and t == NS:
                return NG * L + 2 * NS + g, N_E * L + 2 * NS * NT + g, N_A * L + 2 * NS * (NT - 1) + g
            return NG * L + 2 * t + g, N_E * L + 2 * NT * t + NT * g, N_A * L + 2 * (NT - 1) * t + (NT - 1) * g

        def walk(eng, L, step, by_two=False):
            step(0, 0, NT, 0, NT, (1, 1, 5))
            step(0, 1, NT, NT, NT, (1, 1, 5))
            if by_two:
                with eng.Fori(0, 3) as i:
                    for u in range(2):
                        for g in range(2):
                            step(2 * i + 1 + u, g, NT, NT, NT, (2 * i + 2 + u, u, i + 6))
            else:
                with eng.Fori(1, NS - 1) as t:
                    for g in range(2):
                        step(t, g, NT, NT, NT, None)
            step(NS - 1, 0, NT, NT, NT, (NS, None, 0))
            step(NS - 1, 1, NT, NT, 1, (NS, None, 0))
            step(NS, 0, 1, NT, 1, None)
            step(NS, 1, 1, 1, 0, None)

        def slot(L, g, j):
            return L * (GROUPS * SLOTS) + g * SLOTS + j

        def split_hi(act, L, g, prev):
            for j in range(SLOTS):
                act.wait_ge(w_ld[j % RAW], 16 * (L * (GROUPS * 2) + 2 * g + j // RAW + 1))
                if prev and j < SLOTS - 1:
                    act.wait_ge(S["w_used"], START + (SLOTS - 1) * (L * GROUPS + g - 1) + j + 1)
                elif prev:
                    act.wait_ge(*prev)
                act.copy(w_hi[:, j, :], w_raw[:, j % RAW, :]).then_inc(S["w_hi_done"], 1)

        def split_lo(dve, L, g):
            for j in range(SLOTS):
                dve.wait_ge(S["w_hi_done"], slot(L, g, j) + 1)
                dve.tensor_tensor(w_lo[:, j, :], w_raw[:, j % RAW, :], w_hi[:, j, :].bitcast(F32),
                                  ALU.subtract).then_inc(S["w_lo_done"], 1)

        def col(L, which, kind, kt, g):
            c = which * 32 + (kind * 2 + kt // 4) * 8 + g * 4 + kt % 4
            return modc[:, c:c + 1]

        block = ctx.enter_context(nc.Block())

        @block.sync
        def _(sp):
            sp.dma_start(y_out, x_in).then_inc(S["x_copied"], 16)
            sp.dma_start(ident[:], consts[:, C_ID:C_ID + P]).then_inc(S["const_ld"], 16)
            sp.dma_start(maskt[:].rearrange("p a b -> p (a b)"), consts[:, C_MF:C_MF + 2 * P]).then_inc(S["const_ld"], 16)
            sp.dma_start(condt[:], cond).then_inc(S["const_ld"], 16)
            for n in range(2):
                sp.dma_start(modw[:, n], w_mod[n]).then_inc(mod_w_ld[n], 16)
            for j in range(RAW):
                sp.dma_start(w_raw[:, j, :], w_slots[j]).then_inc(w_ld[j], 16)
            with sp.Fori(0, NL * 12 // 2 - 1) as i:
                for u in range(2):
                    sp.wait_ge(S["mod_ps"], 2 * i + u + 1)
                    sp.dma_start(modw[:, u], w_mod[2 * i + u + 2]).then_inc(mod_w_ld[u], 16)
            with sp.Fori(0, (NL * GROUPS + 1) * SLOTS // RAW - 1) as i:
                for j in range(RAW):
                    sp.wait_ge(S["w_lo_done"], RAW * i + j + 1)
                    sp.dma_start(w_raw[:, j, :], w_slots[RAW * i + RAW + j]).then_inc(w_ld[j], 16)

        @block.gpsimd
        def _(pool):
            pool.memset(half[:], -0.5)
            pool.sem_inc(S["h_done"], START)
            pool.sem_inc(S["sum_done"], START)
            pool.dma_start(modb[:], b_mod).then_inc(S["mod_b_ld"], 16)
            pool.wait_ge(S["mod_row"], START + NL * 12)
            pool.dma_start(mod_dram.rearrange("n g f -> g n f"), modr[:]).then_inc(S["mod_st"], 16)
            pool.wait_ge(S["mod_st"], 16)
            pool.wait_ge(S["x_copied"], 16)
            phase(pool, 0, -1)

            def rstd(L, k, ap, n):
                pool.wait_ge(S["pow_in"], 4 * L + k + 1)
                pool.tensor_tensor(ap, ap, half[:, 0:n], ALU.pow).then_inc(S["pow_out"], 1)

            def lo_of(t, src, count):
                pool.wait_ge(S["hi_done"], count + 1)
                pool.tensor_tensor(lo[:, :, bass.ds(t * P, P)], src.rearrange("p (k c) -> p k c", c=P),
                                   hi[:, :, bass.ds(t * P, P)].bitcast(F32), ALU.subtract).then_inc(S["h_done"], 1)

            with pool.Fori(0, NL) as L:
                for k in range(2):
                    pool.dma_start(mod64[32 * k:32 * k + 32, :],
                                   mod_dram[bass.ds(L * 12 + 6 * k, 4)].rearrange("n g (q f) -> (n g q) f", f=P)
                                   ).then_inc(S["mc_ld"], 16)
                pool.dma_start(rcon[:], row_in[L]).then_inc(S["row_ld"], 16)
                for u in range(3):
                    pool.dma_start(xt[:, u], y_out[u]).then_inc(xt_ld[u], 16)
                with pool.Fori(0, 2) as i:
                    for u in range(3):
                        pool.wait_ge(S["xT_ps"], 2 * NT * L + 3 * i + u + 1)
                        own(pool)
                        pool.dma_start(xt[:, u], y_out[3 * i + u + 3]).then_inc(xt_ld[u], 16)
                        lo_of(3 * i + u, hf[:, u], 2 * NT * L + 3 * i + u)
                for u in range(3):
                    lo_of(6 + u, hf[:, u], 2 * NT * L + 6 + u)
                phase(pool, L, 0)
                phase(pool, L, 1)
                pool.dma_start(selc[:], consts[:, C_SEL:C_SEL + 12 * P].rearrange("p (a b) -> p a b", b=P)).then_inc(S["ml_ld"], 16)
                pool.dma_start(bmask[:], consts[:, C_BM:C_BM + PV]).then_inc(S["ml_ld"], 16)
                pool.dma_start(cs[:, 0], state0[L]).then_inc(S["ml_ld"], 16)
                pool.memset(cs[:, 9], 0.0)
                pool.memset(qbd[:], 0.0)
                pool.memset(vext[:], 1.0).then_inc(S["ml_zero"], 1)
                pool.wait_ge(S["ml_ld"], 48 * L + 48)
                phase(pool, L, 2)
                phase(pool, L, 3)
                for d in range(2):
                    for h in range(MH):
                        part, o = (h % 2) * HD, (h % 2) * VE
                        pool.dma_start(c_out[L, d, h], cs[part:part + HD, 10, d, h // 2, o:o + HD]).then_inc(S["st_out"], 16)
                        pool.dma_start(n_out[L, d, h], cs[part:part + HD, 10, d, h // 2, o + HD:o + VE]).then_inc(S["st_out"], 16)
                    pool.dma_start(m_out[L, d], mrow[32 * d:32 * d + MH, 3, NS:NT]).then_inc(S["st_out"], 16)
                pool.wait_ge(S["st_out"], 16 * 18 * (L + 1))
                phase(pool, L, 4)
                pool.dma_start(wst[:], ws_t[L]).then_inc(S["gm_ld"], 16)
                pool.dma_start(bst[:], bs_t[L]).then_inc(S["gm_ld"], 16)
                pool.dma_start(glnb[:], gln[L]).then_inc(S["gm_ld"], 16)
                rstd(L, 0, rs[:], NT)
                phase(pool, L, 5)
                pool.memset(ones[:], 1.0)
                pool.drain()
                pool.tensor_copy(one_r[:], ones[:])
                pool.dma_start(kvt[:, 0], cache_k[L]).then_inc(S["at_ld"], 16)
                pool.dma_start(kvt[:, 1], cache_v[L]).then_inc(S["at_ld"], 16)
                pool.dma_start(gq[:], qk_g[L]).then_inc(S["at_ld"], 16)
                for u in range(2):
                    pool.dma_start(rp[:, u], rope[:, u]).then_inc(rp_ld[u], 16)
                rstd(L, 1, ss[:].rearrange("p a b -> p (a b)"), NT * 10)
                with pool.Fori(0, 4) as i:
                    for u in range(2):
                        pool.wait_ge(S["kd_done"], START + 10 * L + 2 * i + u + 1)
                        own(pool)
                        pool.dma_start(rp[:, u], rope[:, 2 * i + u + 2]).then_inc(rp_ld[u], 16)
                pool.wait_ge(S["kd_done"], START + 10 * L + 10)
                own(pool)
                pool.dma_start(k_out[L], qn[:, 0:P]).then_inc(S["kv_out"], 16)
                pool.dma_start(v_out[L], z[:, NS, ZV:ZV + P]).then_inc(S["kv_out"], 16)
                pool.wait_ge(S["kv_out"], 32 * L + 32)
                phase(pool, L, 6)
                def diagonal(G, g, h):
                    pool.wait_ge(S["mx_done"], START + HG * (G + 1) + h + 1)
                    n_ = 1 - g
                    pool.tensor_tensor(dg[:, n_, h], ident[:], nm[:, n_, h:h + 1].broadcast_to([P, P]),
                                       ALU.mult).then_inc(S["dg_done"], 1)

                def step(t, g, nk, pk, nn, prep):
                    G, E, A = counts(L, t, g)
                    pool.wait_ge(S["sm_ps"], START + G - 1)
                    if nk == 1:
                        pool.wait_ge(S["ex_done"], START + E + 1)
                        own(pool)
                        pool.tensor_copy(psm[:, g], pr[:, 0]).then_inc(S["sum_done"], 1)
                        for h in range(HG if nn else 0):
                            diagonal(G, g, h)
                    else:
                        for j in range(1, nk):
                            pool.wait_ge(S["ex_done"], START + E + j + 1)
                            if j > 1:
                                pool.wait_ge(S["sum_done"], START + A + j - 1)
                            pool.tensor_tensor(psm[:, g], pr[:, 0] if j == 1 else psm[:, g], pr[:, j % 3],
                                               ALU.add).then_inc(S["sum_done"], 1)
                            if j - 2 in SCORES_AT:
                                diagonal(G, g, SCORES_AT[j - 2])
                    if g == 1 and prep and prep[1] is not None:
                        pool.wait_ge(S["qd_done"], G + 3)
                        own(pool)
                        pool.dma_start(rp[:, prep[1]], rope[:, prep[0] + 2]).then_inc(rp_ld[prep[1]], 16)

                pool.wait_ge(S["qd_done"], NG * L + 2)
                own(pool)
                pool.dma_start(rp[:, 0], rope[:, 2]).then_inc(rp_ld[0], 16)
                for h in range(HG):
                    diagonal(NG * L - 1, 1, h)
                walk(pool, L, step, True)
                for u in range(2):
                    pool.wait_ge(rp_ld[u], 16 * (9 * L + 9))
                phase(pool, L, 7)
                phase(pool, L, 8)
                pool.dma_start(xr[:], y_out.rearrange("t p d -> p t d")).then_inc(S["ln_ld"], 16)
                for g in range(2):
                    for n in range(2):
                        pool.dma_start(gate[:, g, n * W:(n + 1) * W],
                                       mod_dram[L * 12 + 4 + n, g].partition_broadcast(P)).then_inc(S["ln_ld"], 16)
                for k in range(2):
                    pool.dma_start(lnb[:, k], ln_gb[L, k].partition_broadcast(P)).then_inc(S["ln_ld"], 16)
                rstd(L, 2, rs[:], NT)
                with pool.Fori(0, NT) as t:
                    pool.wait_ge(S["xr_done"], NT * L + t + 1)
                    own(pool)
                    pool.dma_start(x1_dram[t], xr[:, t]).then_inc(S["x1_st"], 16)
                pool.wait_ge(S["x1_st"], 16 * NT * (L + 1))
                phase(pool, L, 9)
                for t in range(NT):
                    lo_of(t, hf2[:, t % 3], 2 * NT * L + NT + t)
                phase(pool, L, 10)
                pool.memset(acc[:], 0.0).then_inc(S["acc_zero"], 1)
                phase(pool, L, 11)
                for u in range(3):
                    pool.dma_start(x1t[:, u], x1_dram[u]).then_inc(x1_ld[u], 16)
                for g in range(2):
                    for n in range(2):
                        pool.dma_start(gate2[:, g, n * W:(n + 1) * W],
                                       mod_dram[L * 12 + 10 + n, g].partition_broadcast(P)).then_inc(S["ln_ld"], 16)
                for k in range(2):
                    pool.dma_start(lnb2[:, k], ln_gb[L, 2 + k].partition_broadcast(P)).then_inc(S["ln_ld"], 16)
                with pool.Fori(0, 2) as i:
                    for u in range(3):
                        pool.wait_ge(S["x1_used"], NT * L + 3 * i + u + 1)
                        own(pool)
                        pool.dma_start(x1t[:, u], x1_dram[3 * i + u + 3]).then_inc(x1_ld[u], 16)
                rstd(L, 3, rs[:], NT)
                with pool.Fori(0, NT) as t:
                    pool.wait_ge(S["y_rdy"], NT * L + t + 1)
                    own(pool)
                    pool.dma_start(y_out[t], acc[:, t]).then_inc(S["ln_st"], 16)
                pool.wait_ge(S["ln_st"], 16 * NT * (L + 1))
                phase(pool, L, 12)

        @block.scalar
        def _(act):
            for n in ("z_done", "ex_done", "r_done", "m_w", "o_cp"):
                act.sem_inc(S[n], START)
            act.wait_ge(S["const_ld"], 48)
            act.activation(sce[:], condt[:], ACT.Exp, scale=-1.0).then_inc(S["silu_e"], 1)
            act.copy(idr[:], ident[:])
            act.copy(mkr[:], maskt[:])
            split_hi(act, 0, 0, None)
            phase(act, 0, -1)

            def hi_of(t, src, count):
                act.wait_ge(S["hf_done"], START + count + 1)
                act.copy(hi[:, :, bass.ds(t * P, P)], src.rearrange("p (k c) -> p k c", c=P)).then_inc(S["hi_done"], 1)

            def z_tile(L, c, t, dst, src):
                act.wait_ge(S["z_ps"], START + 45 * L + 9 * c + t + 1)
                act.copy(dst, src).then_inc(S["z_done"], 1)

            def states_v(L, c, n):
                act.wait_ge(S["u_ps"], START + NT * L + n)
                act.copy(vext[:, :, 0:HD], z[:, c, ZVM:ZVM + 256].rearrange("p (h e) -> p h e", e=HD)).then_inc(S["u_v"], 1)

            def mlstm(L, c, n):
                act.wait_ge(S["m_tp"], START + NT * L + n)
                act.copy(qs[:], z[:, c, ZQM:ZQM + 256])
                act.activation(ks[:], z[:, c, ZKM:ZKM + 256], ACT.Copy, scale=M_SCALE)
                act.wait_ge(S["m_num"], START + NT * L + n)
                act.copy(vext[:, :, 0:HD], z[:, c, ZVM:ZVM + 256].rearrange("p (h e) -> p h e", e=HD)).then_inc(S["m_st"], 1)
                act.wait_ge(S["m_fin"], START + NT * L + n)
                act.activation(og[:], z[:, c, ZOM:ZOM + 256], ACT.Exp, scale=-1.0).then_inc(S["m_og"], 1)
                act.wait_ge(S["m_D"], NT * L + n + 1)
                for d in range(2):
                    for h in range(MH):
                        ins = act.activation(wt[:, d, h], ps[:, 2 + d, h * P:(h + 1) * P], ACT.Exp,
                                             bias=cols[:, c, 0, 32 * d + h:32 * d + h + 1])
                ins.then_inc(S["m_w"], 1)

            with act.Fori(0, NL) as L:
                with act.Fori(0, 3) as i:
                    for u in range(3):
                        hi_of(3 * i + u, hf[:, u], 2 * NT * L + 3 * i + u)
                phase(act, L, 0)
                act.wait_ge(S["row_ld"], 16 * L + 16)
                for g in range(3):
                    act.wait_ge(S["g_ps"], 3 * L + g + 1)
                    act.activation(ri[:, g * GRP:(g + 1) * GRP], ps[0:ROWS, 4 + g, 0:GRP], ACT.Identity, bias=rcon[:, 0:1])
                    act.activation(rf[:, g * GRP:(g + 1) * GRP], ps[64:64 + ROWS, 4 + g, 0:GRP], ACT.Identity, bias=rcon[:, 1:2])
                for t in range(NT - 1):
                    z_tile(L, 0, t, z[:, t, ZUG:ZUG + 256], ps[:, t % 3, 0:256])
                split_hi(act, L, 1, (S["z_ps"], START + 45 * L + 9))
                z_tile(L, 0, NT - 1, z[:, NT - 1, ZUG:ZUG + 256], ps[:, 2, 0:256])
                with act.Fori(0, 4) as c:
                    for t in range(NT - 1):
                        z_tile(L, c + 1, t, z[:, t, bass.ds(c * W, W)], ps[:, t % 3, :])
                    split_hi(act, L, c + 2, (S["z_ps"], START + 45 * L + 9 * c + 18))
                    z_tile(L, c + 1, NT - 1, z[:, NT - 1, bass.ds(c * W, W)], ps[:, 2, :])
                phase(act, L, 1)
                act.wait_ge(S["abs_row"], L + 1)
                act.activation(r_b[:], r_b[:], ACT.Exp, scale=-1.0)
                act.drain()
                act.activation(r_b[:], r_b[:], ACT.Ln, bias=1.0).then_inc(S["act_row"], 1)
                act.wait_ge(S["dve_row"], L + 1)
                act.activation(rf[:], rf[:], ACT.Exp)
                act.activation(r_r[:], r_r[:], ACT.Exp)
                act.activation(r_d[:], r_d[:], ACT.Exp, scale=-1.0)
                act.activation(mrow[:, 4], mrow[:, 4], ACT.Exp).then_inc(S["act_row"], 1)
                phase(act, L, 2)
                with act.Fori(0, NS) as c:
                    states_v(L, c, c)
                states_v(L, NS, NS)
                phase(act, L, 3)
                with act.Fori(0, NS) as c:
                    mlstm(L, c, c)
                mlstm(L, NS, NS)
                phase(act, L, 4)
                phase(act, L, 5)
                act.wait_ge(S["at_ld"], 48 * L + 48)
                for v in range(HKV):
                    c = v * HD
                    act.copy(vst[:, v, 0:NS, 0:HD], z[:, 0:NS, ZV + c:ZV + c + HD])
                    act.copy(vst[:, v, 8, 0:HD], kvt[:, 1, c:c + HD])
                    ins = act.copy(vst[:, v, 9, 0:HD], z[:, NS, ZV + c:ZV + c + HD])
                ins.then_inc(S["v_hi"], 1)

                def keys_hi(tile, n):
                    act.wait_ge(S["kd_ps"], START + 10 * L + n + 1)
                    act.wait_ge(S["k_lo"], START + 10 * L + n)
                    act.copy(kst[0:HD, :, bass.ds(tile * P, P)], ps[0:HD, 0, 0:2 * P].rearrange("p (a b) -> p a b", b=P))
                    act.copy(q_hi[HD:P, 0, 0:2], ps[HD:P, 0, 0:2 * P].rearrange("p (a b) -> p a b", b=P)).then_inc(S["k_hi"], 1)

                with act.Fori(0, NS) as t:
                    keys_hi(t, t)
                keys_hi(8, 8)
                keys_hi(9, 9)
                phase(act, L, 6)

                def queries_hi(G, g):
                    act.wait_ge(S["q_ps"], G + 1)
                    act.copy(q_hi[:, g], ps[:, 7, :].rearrange("p (a b) -> p a b", b=P)).then_inc(S["q_hi_done"], 1)

                def exp_(E, A, j, fresh):
                    act.wait_ge(S["st_ps"], E + j + 1)
                    act.wait_ge(S["p_lo_done"], START + (E + j if fresh else E + j - 2))
                    act.wait_ge(S["sum_done"], START + A + (0 if fresh else j - 2 if j < 3 else max(j - 3, 1)))
                    act.activation(pr[:, j % 3], ps[:, 3 + j % 3, :], ACT.Exp).then_inc(S["ex_done"], 1)

                def hi_(e, j, fresh=False):
                    act.wait_ge(S["ex_done"], START + e + 1)
                    act.wait_ge(S["pv_done"], START + (e if fresh else e - 2))
                    act.copy(p_hi[:, j % 3], pr[:, j % 3]).then_inc(S["p_hi_done"], 1)

                def sums_out(G, E):
                    act.wait_ge(S["oy_done"], START + G)
                    act.wait_ge(S["pv_done"], START + E)
                    act.copy(o_s[:], ps[:, 6, :]).then_inc(S["o_cp"], 1)

                def turned_out(G):
                    act.wait_ge(S["ot_ps"], START + G + 1)
                    act.copy(o_s[:, 0:256].rearrange("p (a b) -> p a b", b=HD),
                             ps[:, 7, :].rearrange("p (a b) -> p a b", b=P)[:, :, 0:HD]).then_inc(S["ot_cp"], 1)

                def step(t, g, nk, pk, nn, prep):
                    G, E, A = counts(L, t, g)
                    for j in range(nk):
                        if pk == 1:
                            hi_(E - 1, 0)
                        exp_(E, A, j, pk == 1)
                        if (j or pk) and pk != 1:
                            hi_(E + j - 1, (j or pk) - 1)
                        if nn and j == min(1, nk - 1):
                            queries_hi(G + 1, 1 - g)
                        if pk and j == min(1, nk - 1):
                            sums_out(G - 1, E)
                        if pk and j == min(6, nk - 1):
                            turned_out(G - 1)

                queries_hi(NG * L, 0)
                walk(act, L, step)
                hi_(N_E * (L + 1) - 1, 0, True)
                sums_out(NG * (L + 1) - 1, N_E * (L + 1))
                turned_out(NG * (L + 1) - 1)
                phase(act, L, 7)
                for t in range(NT):
                    act.wait_ge(S["yT_ps"], NT * L + t + 1)
                    for k in range(2):
                        ins = act.copy(hi[:, 4 * k:4 * k + 4, t * P:(t + 1) * P],
                                       ps[:, 2 * (t % 3) + k, :].rearrange("p (a b) -> p a b", b=P))
                    ins.then_inc(S["y_hi"], 1)
                phase(act, L, 8)
                split_hi(act, L, 6, (S["o_out"], START + 18 * L + 9))
                split_hi(act, L, 7, (S["o_out"], START + 18 * L + 18))
                phase(act, L, 9)
                for t in range(NT):
                    hi_of(t, hf2[:, t % 3], 2 * NT * L + NT + t)
                phase(act, L, 10)

                def hidden(i, b):
                    n = 12 * (NFF * L + i) + b
                    act.wait_ge(S["h_ps"], START + n + 1)
                    act.wait_ge(S["flo_done"], START + n - 1)
                    act.activation(fr[:, b % 2], ps[:, b % 3, 0:GRP], ACT.Relu).then_inc(S["r_done"], 1)
                    act.drain()
                    act.activation(f_hi[:, b // 3, (b % 3) * GRP:(b % 3 + 1) * GRP], fr[:, b % 2],
                                   ACT.Square).then_inc(S["fhi_done"], 1)

                with act.Fori(0, NFF) as i:
                    for b in range(11):
                        hidden(i, b)
                    split_hi(act, L, 2 * i + 8, (S["h_ps"], START + 12 * (NFF * L + i) + 12))
                    hidden(i, 11)
                    split_hi(act, L, 2 * i + 9, (S["f_ps"], START + 18 * (NFF * L + i) + 18))
                phase(act, L, 11)
                phase(act, L, 12)

        @block.vector
        def _(dve):
            for n in ("mod_row", "hf_done", "u_done", "m_qk", "m_sw", "m_fin", "gm_vn", "kd_done", "k_lo",
                      "mx_done", "p_lo_done", "oy_done", "q_lo_done", "y_lo", "xr_half", "flo_done", "f_acc"):
                dve.sem_inc(S[n], START)
            dve.wait_ge(S["silu_e"], 1)
            dve.tensor_scalar(sce[:], sce[:], 1.0, None, ALU.add)
            dve.drain()
            dve.reciprocal(sce[:], sce[:])
            dve.drain()
            dve.tensor_tensor(sc[:], sce[:], condt[:], ALU.mult).then_inc(S["mod_ready"], 1)
            dve.wait_ge(S["mod_b_ld"], 16)
            own(dve)
            with dve.Fori(0, NL * 12 // 2) as i:
                for u in range(2):
                    dve.wait_ge(S["mod_ps"], 2 * i + u + 1)
                    dve.tensor_tensor(modr[:, 2 * i + u], ps[0:2, u, :], modb[:, 2 * i + u], ALU.add).then_inc(S["mod_row"], 1)
            split_lo(dve, 0, 0)
            phase(dve, 0, -1)

            def modulate(L, n, which, dst, u, g):
                dve.wait_ge(S["xT_ps"], 2 * NT * L + n + 1)
                dve.wait_ge(S["h_done"], START + 2 * NT * L + n - 2)
                for kt in range(KT):
                    ins = dve.tensor_scalar(dst[:, u, kt * P:(kt + 1) * P],
                                            ps[:, 2 * u + kt // 4, (kt % 4) * P:(kt % 4 + 1) * P],
                                            col(L, which, 1, kt, g), col(L, which, 0, kt, g), ALU.mult, ALU.add)
                ins.then_inc(S["hf_done"], 1)

            def b2(ap, n):
                return ap.unsqueeze(len(ap.shape)).broadcast_to([*ap.shape, n])

            def spread(ap, n):
                return ap.unsqueeze(1).broadcast_to([ap.shape[0], n, *ap.shape[1:]])

            def layer_norm(L, k, x, gb, done):
                with dve.Fori(0, NT) as t:
                    for j in range(2):
                        dve.bn_stats(st6[:, t, j], x[:, t, j * W:(j + 1) * W])
                dve.drain()
                for t in range(NT):
                    dve.bn_aggr(mv[:, t], st6[:, t].rearrange("p a b -> p (a b)"))
                dve.drain()
                dve.tensor_scalar(rs[:], mv[:, :, 1], EPS, None, ALU.add).then_inc(S["pow_in"], 1)
                dve.wait_ge(S["pow_out"], 4 * L + k + 1)
                own(dve)
                with dve.Fori(0, NT) as t:
                    dve.tensor_scalar(x[:, t], x[:, t], mv[:, t, 0:1], rs[:, bass.ds(t, 1)], ALU.subtract, ALU.mult)
                    dve.drain()
                    dve.tensor_tensor(x[:, t], x[:, t], gb[:, 0], ALU.mult)
                    dve.drain()
                    dve.tensor_tensor(x[:, t], x[:, t], gb[:, 1], ALU.add).then_inc(done, 1)

            with dve.Fori(0, NL) as L:
                dve.wait_ge(S["mc_ps"], L + 1)
                for k in range(2):
                    dve.tensor_copy(modc[:, 32 * k:32 * k + 16], ps[:, 7, 32 * k:32 * k + 16])
                    dve.tensor_scalar(modc[:, 32 * k + 16:32 * k + 32], ps[:, 7, 32 * k + 16:32 * k + 32], 1.0, None, ALU.add)
                dve.drain()
                with dve.Fori(0, 2) as i:
                    for u in range(3):
                        modulate(L, 3 * i + u, 0, hf, u, 1)
                for u in range(3):
                    modulate(L, 6 + u, 0, hf, u, int(u < 2))
                phase(dve, L, 0)
                with dve.Fori(0, 5) as c:
                    split_lo(dve, L, c + 1)
                phase(dve, L, 1)
                dve.scalar_tensor_tensor(r_b[:], rf[:], -1.0, rf[:], ALU.mult, ALU.max).then_inc(S["abs_row"], 1)
                dve.memset(r_r[:], 1.0)
                dve.memset(r_d[:], 0.0)
                dve.memset(r_m[:], 0.0)
                dve.memset(mrow[:], 0.0)
                dve.drain()
                dve.memset(r_r[:, 0:TOK:P], 0.0)
                dve.wait_ge(S["act_row"], 2 * L + 1)
                dve.scalar_tensor_tensor(rf[:], rf[:], 0.0, r_b[:], ALU.min, ALU.subtract)
                dve.drain()
                F, Bk = slice(0, MH), slice(32, 32 + MH)
                dve.tensor_tensor_scan(r_b[F], r_r[F], rf[F], 0.0, ALU.mult, ALU.add)
                dve.tensor_tensor_scan(r_b[Bk, ::-1], r_r[Bk], rf[Bk, ::-1], 0.0, ALU.mult, ALU.add)
                dve.drain()
                dve.tensor_copy(r_d[F, P:DEC_SEQ:P], r_b[F, P - 1:DEC_SEQ - P:P])
                dve.tensor_copy(r_d[Bk, P - 1:DEC_SEQ - P:P], r_b[Bk, P:DEC_SEQ:P])
                dve.tensor_tensor(ri[:], ri[:], r_b[:], ALU.subtract)
                dve.drain()
                N = DEC_SEQ
                dve.tensor_tensor_scan(r_m[F, 0:N], r_d[F, 0:N], ri[F, 0:N], rcon[F, 2:3], ALU.add, ALU.max)
                dve.tensor_tensor_scan(r_m[F, N:TOK], r_d[F, N:TOK], ri[F, N:TOK], 0.0, ALU.add, ALU.max)
                dve.tensor_tensor_scan(r_m[Bk, N - 1::-1], r_d[Bk, N - 1::-1], ri[Bk, N - 1::-1], rcon[Bk, 2:3], ALU.add, ALU.max)
                dve.tensor_tensor_scan(r_m[Bk, TOK - 1:N - 1:-1], r_d[Bk, TOK - 1:N - 1:-1], ri[Bk, TOK - 1:N - 1:-1],
                                       0.0, ALU.add, ALU.max)
                dve.drain()
                dve.tensor_copy(mrow[F, 0], r_b[F, P - 1:TOK:P])
                dve.tensor_copy(mrow[Bk, 0], r_b[Bk, 0:TOK:P])
                dve.tensor_copy(mrow[F, 1], r_m[F, P - 1:TOK:P])
                dve.tensor_copy(mrow[Bk, 1], r_m[Bk, 0:TOK:P])
                dve.tensor_copy(mrow[F, 2, 0:1], rcon[F, 2:3])
                dve.tensor_copy(mrow[Bk, 2, NS - 1:NS], rcon[Bk, 2:3])
                dve.drain()
                dve.tensor_tensor(mrow[:, 3], mrow[:, 0], mrow[:, 1], ALU.add)
                dve.drain()
                dve.tensor_copy(mrow[F, 2, 1:NS], mrow[F, 3, 0:NS - 1])
                dve.tensor_copy(mrow[Bk, 2, 0:NS - 1], mrow[Bk, 3, 1:NS])
                dve.drain()
                dve.tensor_tensor(mrow[:, 4], mrow[:, 2], mrow[:, 1], ALU.subtract)
                v3 = lambda r: r[:].rearrange("p (c t) -> p c t", t=P)
                dve.tensor_tensor(v3(rf), v3(ri), b2(mrow[:, 1], P), ALU.subtract)
                dve.tensor_tensor(v3(r_r), b2(mrow[:, 2], P), v3(r_m), ALU.subtract)
                dve.tensor_tensor(r_d[:], r_b[:], r_m[:], ALU.add).then_inc(S["dve_row"], 1)
                dve.drain()
                dve.tensor_scalar(r_m[:], r_m[:], -1.0, None, ALU.mult)
                dve.wait_ge(S["rt_ps"], L + 1)
                dve.tensor_copy(cols[:].rearrange("p (a b) c d -> p a (b c d)", b=3), ps[:, 0:3, 0:12 * ROWS])
                for p_ in range(2):
                    dve.tensor_copy(dec[:, :, 0, p_], ps[:, 3, p_ * NT:p_ * NT + NS])
                    dve.tensor_copy(dec[:, :, 1, p_], ps[:, 3, (2 + p_) * NT:(2 + p_) * NT + NS][:, ::-1])
                phase(dve, L, 2)

                def states(c, n, s_f, s_b):
                    dve.wait_ge(S["u_ps"], START + NT * L + n)
                    for d in range(2):
                        ins = dve.scalar_tensor_tensor(kw[:, d].rearrange("p (h e) -> p h e", e=HD),
                                                       z[:, c, ZKM:ZKM + 256].rearrange("p (h e) -> p h e", e=HD), M_SCALE,
                                                       b2(cols[:, c, 1, 32 * d:32 * d + MH], HD), ALU.mult, ALU.mult)
                    ins.then_inc(S["u_kw"], 1)
                    dve.wait_ge(S["u_ps"], START + NT * L + n + 1)
                    for d, s_ in enumerate((s_f, s_b)):
                        ins = dve.tensor_tensor(cs[:, s_, d], ps[:, d, 0:2 * PV].rearrange("p (a b) -> p a b", b=PV),
                                                spread(bmask[:], 2), ALU.mult)
                    ins.then_inc(S["u_done"], 1)

                with dve.Fori(0, NS) as c:
                    states(c, c, c + 1, 8 - c)
                states(NS, NS, 10, 10)
                dve.drain()
                tmp = hn[:].rearrange("p a b c -> p (a b c)")
                flat = lambda ap: ap.rearrange("p a b c -> p (a b) c")
                with dve.Fori(0, NS) as i:
                    dve.tensor_tensor(tmp.rearrange("p (a b) -> p a b", b=PV), flat(cs[:, i]),
                                      b2(dec[:, i].rearrange("p a b -> p (a b)"), PV), ALU.mult)
                    dve.drain()
                    dve.tensor_tensor(flat(cs[:, i + 1]), flat(cs[:, i + 1]), tmp.rearrange("p (a b) -> p a b", b=PV), ALU.add)
                    dve.drain()
                phase(dve, L, 3)

                def mlstm(c, n):
                    dve.wait_ge(S["m_tp"], START + NT * L + n + 1)
                    dve.wait_ge(S["m_num"], START + NT * L + n)
                    for p_ in range(2):
                        a = slice(HD * p_, HD * p_ + HD)
                        dve.tensor_copy(qbd[a, :, p_, :], ps[a, 0, 0:2 * P].rearrange("p (a b) -> p a b", b=P))
                    dve.tensor_copy(qT[:], ps[:, 0, 0:2 * P].rearrange("p (a b) -> p a b", b=P))
                    dve.tensor_copy(kT[:], ps[:, 0, 2 * P:4 * P].rearrange("p (a b) -> p a b", b=P)).then_inc(S["m_qk"], 1)
                    dve.wait_ge(S["m_og"], NT * L + n + 1)
                    dve.tensor_scalar(og[:], og[:], 1.0, None, ALU.add)
                    dve.drain()
                    dve.reciprocal(og[:], og[:])
                    dve.wait_ge(S["m_S"], NT * L + n + 1)
                    dve.wait_ge(S["m_w"], START + NT * L + n + 1)
                    for d in range(2):
                        ins = dve.tensor_tensor(wt[:, d].rearrange("p a b -> p (a b)"), ps[:, 1, :],
                                                wt[:, d].rearrange("p a b -> p (a b)"), ALU.mult)
                    ins.then_inc(S["m_sw"], 1)
                    dve.wait_ge(S["m_num"], START + NT * L + n + 1)
                    v = lambda b: ps[:, b, 0:2 * PV].rearrange("p (a b) -> p a b", b=VE)
                    for d in range(2):
                        dve.tensor_tensor(hn[:, d], v(6 + d), b2(cols[:, c, 2, 32 * d:32 * d + MH], VE), ALU.mult)
                    dve.drain()
                    for d in range(2):
                        dve.tensor_tensor(hn[:, d], hn[:, d], v(4 + d), ALU.add)
                    dve.drain()
                    dve.scalar_tensor_tensor(den[:, 0], hn[:, :, :, HD], -1.0, hn[:, :, :, HD], ALU.mult, ALU.max)
                    dve.drain()
                    for d in range(2):
                        dve.tensor_tensor(den[:, 0, d], den[:, 0, d], cols[:, c, 3, 32 * d:32 * d + MH], ALU.max)
                    dve.drain()
                    dve.reciprocal(den[:, 1], den[:, 0])
                    dve.drain()
                    for d in range(2):
                        dve.tensor_tensor(hh[:, d], hn[:, d, :, 0:HD], b2(den[:, 1, d], HD), ALU.mult)
                    dve.drain()
                    dve.tensor_tensor(hh[:, 0], hh[:, 0], hh[:, 1], ALU.add)
                    dve.drain()
                    dve.tensor_tensor(z[:, c, ZOM:ZOM + 256], hh[:, 0].rearrange("p a b -> p (a b)"), og[:],
                                      ALU.mult).then_inc(S["m_fin"], 1)

                with dve.Fori(0, NS) as c:
                    mlstm(c, c)
                mlstm(NS, NS)
                phase(dve, L, 4)
                with dve.Fori(0, NT) as t:
                    dve.bn_stats(st6[:, t, 0], z[:, t, ZVG:ZVG + 256])
                dve.drain()
                for t in range(NT):
                    dve.bn_aggr(mv[:, t], st6[:, t, 0])
                dve.drain()
                dve.tensor_scalar(rs[:], mv[:, :, 1], EPS, None, ALU.add).then_inc(S["pow_in"], 1)
                dve.wait_ge(S["pow_out"], 4 * L + 1)
                dve.wait_ge(S["gm_ld"], 48 * L + 48)
                own(dve)
                with dve.Fori(0, NT) as t:
                    dve.tensor_scalar(vn[:, t], z[:, t, ZVG:ZVG + 256], mv[:, t, 0:1], rs[:, bass.ds(t, 1)], ALU.subtract, ALU.mult)
                    dve.drain()
                    dve.tensor_tensor(vn[:, t], vn[:, t], glnb[:, 0], ALU.mult)
                    dve.drain()
                    dve.tensor_tensor(vn[:, t], vn[:, t], glnb[:, 1], ALU.add).then_inc(S["gm_vn"], 1)
                with dve.Fori(0, 3) as i:
                    for u in range(3):
                        dve.wait_ge(S["gm_ps"], NT * L + 3 * i + u + 1)
                        dve.tensor_tensor(gs[:, u].rearrange("p (a b) -> p a b", b=HD),
                                          ps[:, u, 0:256].rearrange("p (a b) -> p a b", b=HD), b2(bst[:], HD), ALU.add)
                        dve.drain()
                        ug = z[:, 3 * i + u, ZUG:ZUG + 256]
                        dve.tensor_tensor(ug, ug, gs[:, u], ALU.mult).then_inc(S["gm_vn"], 1)
                phase(dve, L, 5)

                with dve.Fori(0, 3) as i:
                    for u in range(3):
                        x_ = z[:, 3 * i + u, ZQ:ZQ + 640]
                        dve.tensor_tensor(sq[:, u], x_, x_, ALU.mult)
                    dve.drain()
                    for u in range(3):
                        dve.tensor_reduce(ss[:, 3 * i + u], sq[:, u].rearrange("p (a b) -> p a b", b=HD), AX.X, ALU.add)
                    dve.drain()
                dve.tensor_scalar(ss[:], ss[:], 1.0 / HD, EPS, ALU.mult, ALU.add).then_inc(S["pow_in"], 1)
                dve.wait_ge(S["at_ld"], 48 * L + 48)
                dve.wait_ge(S["v_hi"], L + 1)
                for v in range(HKV):
                    c = v * HD
                    for o_, i_ in ((vst[:, v, 0:NS], z[:, 0:NS, ZV + c:ZV + c + HD]), (vst[:, v, 8], kvt[:, 1, c:c + HD]),
                                   (vst[:, v, 9], z[:, NS, ZV + c:ZV + c + HD])):
                        o_h, o_l = (o_[:, :, 0:HD], o_[:, :, HD:P]) if len(o_.shape) == 3 else (o_[:, 0:HD], o_[:, HD:P])
                        dve.tensor_tensor(o_l, i_, o_h.bitcast(F32), ALU.subtract)
                dve.wait_ge(S["pow_out"], 4 * L + 2)
                own(dve)

                def normed(t, nh, c0, k0, which, extra):
                    o_ = qn[:, 0:nh * HD].rearrange("p (a b) -> p a b", b=HD)
                    dve.tensor_tensor(o_, z[:, t, c0:c0 + nh * HD].rearrange("p (a b) -> p a b", b=HD),
                                      b2(ss[:, t, k0:k0 + nh], HD), ALU.mult)
                    dve.drain()
                    dve.scalar_tensor_tensor(o_, o_, extra, spread(gq[:, which], nh), ALU.mult, ALU.mult)
                    dve.drain()

                def rotated(u, nh, a=0):
                    o_ = qn[:, 0:nh * HD].rearrange("p (a b) -> p a b", b=HD)
                    dve.tensor_tensor(qd[:, a:a + nh, 0], o_, spread(rp[:, u, 0], nh), ALU.mult)
                    for r in range(2):
                        h_ = HD // 2
                        q4 = o_[:, :, r * h_:(r + 1) * h_].rearrange("p a (b c) -> p a b c", b=2)
                        d4 = qd[:, a:a + nh, 1, r * h_:(r + 1) * h_].rearrange("p a (b c) -> p a b c", b=2)
                        s4 = rp[:, u, 1, r * h_:(r + 1) * h_].rearrange("p (b c) -> p b c", b=2)
                        dve.tensor_tensor(d4, q4[:, :, ::-1, :], spread(s4, nh), ALU.mult)
                    dve.drain()
                    dve.tensor_tensor(qd[:, a:a + nh, 0], qd[:, a:a + nh, 0], qd[:, a:a + nh, 1], ALU.add)
                    dve.drain()
                    return dve.tensor_copy(qd[:, a:a + nh, 1], qd[:, a:a + nh, 0])

                def keys_lo(tile, n):
                    dve.wait_ge(S["k_hi"], 10 * L + n + 1)
                    dve.tensor_tensor(kst[HD:P, :, bass.ds(tile * P, P)], ps[HD:P, 0, 0:2 * P].rearrange("p (a b) -> p a b", b=P),
                                      q_hi[HD:P, 0, 0:2].bitcast(F32), ALU.subtract).then_inc(S["k_lo"], 1)

                with dve.Fori(0, 4) as i:
                    for u in range(2):
                        t = 2 * i + u
                        dve.wait_ge(S["kd_ps"], START + 10 * L + t)
                        normed(t, HKV, ZK, HQ, 1, 1.0)
                        dve.wait_ge(rp_ld[u], 16 * (9 * L + i + 1))
                        rotated(u, HKV).then_inc(S["kd_done"], 1)
                        keys_lo(t, t)
                dve.wait_ge(S["kd_ps"], START + 10 * L + 8)
                dve.tensor_copy(qd[:, 0:HKV], kvt[:, 0].rearrange("p (a b) -> p a b", b=HD).unsqueeze(2)
                                .broadcast_to([P, HKV, 2, HD])).then_inc(S["kd_done"], 1)
                keys_lo(8, 8)
                dve.wait_ge(S["kd_ps"], START + 10 * L + 9)
                normed(NS, HKV, ZK, HQ, 1, 1.0)
                dve.tensor_copy(qd[:, 0:HKV], qn[:, 0:P].rearrange("p (a b) -> p a b", b=HD).unsqueeze(2)
                                .broadcast_to([P, HKV, 2, HD])).then_inc(S["kd_done"], 1)
                keys_lo(9, 9)
                phase(dve, L, 6)

                def queries(t, g, u, k, part=2):
                    o = g * HG
                    if part != 1:
                        normed(t, HG, ZQ + o * HD, o, 0, HD ** -0.5)
                    if part and u is None:
                        dve.tensor_copy(qd[:, o:o + HG], qn[:, 0:HG * HD].rearrange("p (a b) -> p a b", b=HD).unsqueeze(2)
                                        .broadcast_to([P, HG, 2, HD])).then_inc(S["qd_done"], 1)
                    elif part:
                        dve.wait_ge(rp_ld[u], k)
                        rotated(u, HG, o).then_inc(S["qd_done"], 1)

                def queries_lo(G, g):
                    dve.wait_ge(S["q_hi_done"], G + 1)
                    dve.tensor_tensor(q_lo[:, g], ps[:, 7, :].rearrange("p (a b) -> p a b", b=P),
                                      q_hi[:, g].bitcast(F32), ALU.subtract).then_inc(S["q_lo_done"], 1)

                def maximum(G, g, h, nk):
                    dve.wait_ge(S["s_ps"], START + HG * G + h + 1)
                    i_ = ps[:, 0:3, 0:GRP] if nk == NT else ps[:, 0:1, 0:P]
                    dve.tensor_reduce(nm[:, g, h:h + 1], i_, AX.XY, ALU.max, negate=True).then_inc(S["mx_done"], 1)

                def lo_(e, j):
                    dve.wait_ge(S["p_hi_done"], e + 1)
                    dve.tensor_tensor(p_lo[:, j % 3], pr[:, j % 3], p_hi[:, j % 3].bitcast(F32),
                                      ALU.subtract).then_inc(S["p_lo_done"], 1)

                def reciprocals(G):
                    dve.wait_ge(S["sm_ps"], START + G + 1)
                    dve.reciprocal(rinv[:], ps[:, 2, GRP:GRP + HG]).then_inc(S["rv_done"], 1)

                def outputs(t, g, G):
                    dve.wait_ge(S["ot_cp"], G + 1)
                    o3 = z[:, t, ZQ + g * 256:ZQ + g * 256 + 256].rearrange("p (a b) -> p a b", b=HD)
                    dve.tensor_tensor(o3, o_s[:, 0:256].rearrange("p (a b) -> p a b", b=HD),
                                      ps[:, 7, :].rearrange("p (a b) -> p a b", b=P)[:, :, HD:P], ALU.add)
                    dve.drain()
                    dve.tensor_tensor(o3, o3, b2(rinv[:], HD), ALU.mult).then_inc(S["oy_done"], 1)

                def step(t, g, nk, pk, nn, prep):
                    G, E, A = counts(L, t, g)
                    for j in range(nk):
                        for key, h in SCORES_AT.items():
                            if nn and nk == NT and j == key + 1:
                                maximum(G + 1, 1 - g, h, nn)
                        if j or pk:
                            lo_(E + j - 1, (j or pk) - 1)
                        if nn and j == min(1, nk - 1):
                            queries_lo(G + 1, 1 - g)
                        if prep and j in (0, 2):
                            queries(prep[0], g, prep[1], 16 * (9 * L + prep[2]), j // 2)
                        if pk and j == min(1, nk - 1):
                            reciprocals(G - 1)
                        if nn and nk == 1:
                            for h in range(HG):
                                maximum(G + 1, 1 - g, h, nn)
                        if pk and j == min(6, nk - 1):
                            outputs(t if g else t - 1, 1 - g, G - 1)

                for g in range(2):
                    queries(0, g, 0, 16 * (9 * L + 5))
                queries_lo(NG * L, 0)
                for h in range(HG):
                    maximum(NG * L, 0, h, NT)
                walk(dve, L, step, True)
                lo_(N_E * (L + 1) - 1, 0)
                reciprocals(NG * (L + 1) - 1)
                outputs(NS, 1, NG * (L + 1) - 1)
                phase(dve, L, 7)
                for t in range(NT):
                    dve.wait_ge(S["y_hi"], NT * L + t + 1)
                    for k in range(2):
                        r = (slice(None), slice(4 * k, 4 * k + 4), slice(t * P, (t + 1) * P))
                        ins = dve.tensor_tensor(lo[r], ps[:, 2 * (t % 3) + k, :].rearrange("p (a b) -> p a b", b=P),
                                                hi[r].bitcast(F32), ALU.subtract)
                    ins.then_inc(S["y_lo"], 1)
                phase(dve, L, 8)

                def residual(n, t):
                    k = 18 * L + 9 * n + t
                    g = int(t < NS)
                    dve.wait_ge(S["o_out"], START + k + 1)
                    dve.tensor_tensor(lnt[:, (n + t) % 2], ps[:, t % 3, :], gate[:, g, bass.ds(n * W, W)], ALU.mult)
                    dve.drain()
                    r = xr[:, t, bass.ds(n * W, W)]
                    dve.scalar_tensor_tensor(r, r, ALPHA, lnt[:, (n + t) % 2], ALU.mult, ALU.add).then_inc(S["xr_half"], 1)

                dve.wait_ge(S["ln_ld"], 16 * (13 * L + 7))
                own(dve)
                for n in range(2):
                    for t in range(NT - 1):
                        residual(n, t)
                    split_lo(dve, L, 6 + n)
                    residual(n, NT - 1)
                dve.drain()
                layer_norm(L, 2, xr, lnb, S["xr_done"])
                phase(dve, L, 9)
                for t in range(NT):
                    modulate(L, NT + t, 1, hf2, t % 3, int(t < NS))
                phase(dve, L, 10)

                def hidden(i, b):
                    n = 12 * (NFF * L + i) + b
                    dve.wait_ge(S["r_done"], START + n + 1)
                    dve.tensor_tensor(fsq[:, b % 2], fr[:, b % 2], fr[:, b % 2], ALU.mult)
                    dve.drain()
                    r = (slice(None), b // 3, slice((b % 3) * GRP, (b % 3 + 1) * GRP))
                    dve.wait_ge(S["fhi_done"], n + 1)
                    dve.tensor_tensor(f_lo[r], fsq[:, b % 2], f_hi[r].bitcast(F32), ALU.subtract).then_inc(S["flo_done"], 1)

                def summed(i, b):
                    n = 18 * (NFF * L + i) + b
                    dve.wait_ge(S["f_ps"], START + n + 1)
                    a = acc[:, b // 2, (b % 2) * W:(b % 2 + 1) * W]
                    dve.tensor_tensor(a, a, ps[:, 3 + b % 3, :], ALU.add).then_inc(S["f_acc"], 1)

                dve.wait_ge(S["acc_zero"], L + 1)
                own(dve)
                with dve.Fori(0, NFF) as i:
                    for b in range(11):
                        hidden(i, b)
                    split_lo(dve, L, 2 * i + 8)
                    hidden(i, 11)
                    for b in range(17):
                        summed(i, b)
                    split_lo(dve, L, 2 * i + 9)
                    summed(i, 17)
                    dve.drain()
                phase(dve, L, 11)
                dve.wait_ge(S["ln_ld"], 16 * (13 * L + 13))
                own(dve)

                def residual2(n, k, u, g):
                    a = acc[:, n]
                    dve.tensor_tensor(a, a, gate2[:, g], ALU.mult)
                    dve.drain()
                    dve.wait_ge(x1_ld[u], 16 * (3 * L + k + 1))
                    dve.scalar_tensor_tensor(a, x1t[:, u], ALPHA, a, ALU.mult, ALU.add).then_inc(S["x1_used"], 1)

                with dve.Fori(0, 2) as i:
                    for u in range(3):
                        residual2(3 * i + u, i, u, 1)
                for u in range(3):
                    residual2(6 + u, 2, u, int(u < 2))
                dve.drain()
                layer_norm(L, 3, acc, lnb2, S["y_rdy"])
                phase(dve, L, 12)

        @block.tensor
        def _(pe):
            for n in ("mod_ps", "u_ps", "m_tp", "m_num", "z_ps", "f_ps", "h_ps", "o_out", "kd_ps", "s_ps", "pv_done", "ot_ps", "sm_ps", "w_used"):
                if n != "mod_ps":
                    pe.sem_inc(S[n], START)
            pe.wait_ge(S["const_ld"], 48)
            pe.wait_ge(S["mod_ready"], 1)
            own(pe)
            with pe.Fori(0, NL * 12 // 2) as i:
                for u in range(2):
                    pe.wait_ge(mod_w_ld[u], 16 * i + 16)
                    pe.wait_ge(S["mod_row"], START + 2 * i + u - 1)
                    for k in range(KT):
                        mm = pe.matmul(ps[0:2, u, :], sc[:, k, :], modw[:, u, k, :], start=(k == 0), stop=(k == KT - 1))
                    mm.then_inc(S["mod_ps"], 1)
            phase(pe, 0, -1)

            def product(out, a_hi, a_lo, b_hi, b_lo, first, last, used=None):
                mm = pe.matmul(out, a_hi, b_hi, start=first, stop=False)
                if used is not None:
                    mm.then_inc(used, 1)
                pe.matmul(out, a_hi, b_lo, start=False, stop=False)
                return pe.matmul(out, a_lo, b_hi, start=False, stop=last)

            def dense(L, g, t, bank, cols_, wait_w, last_tile, done):
                out = ps[:, bank, 0:cols_]
                a = slice(t * P, (t + 1) * P)
                for k in range(KT):
                    if wait_w:
                        pe.wait_ge(S["w_lo_done"], slot(L, g, k) + 1)
                    mm = product(out, hi[:, k, a], lo[:, k, a], w_hi[:, k, 0:cols_], w_lo[:, k, 0:cols_],
                                 k == 0, k == KT - 1, S["w_used"] if last_tile and k else None)
                mm.then_inc(done, 1)

            with pe.Fori(0, NL) as L:
                pe.wait_ge(S["mc_ld"], 32 * L + 32)
                own(pe)
                pe.transpose(ps[:, 7, 0:64], mod64[:, :], ident[0:64, 0:64]).then_inc(S["mc_ps"], 1)
                with pe.Fori(0, 3) as i:
                    for u in range(3):
                        pe.wait_ge(xt_ld[u], 16 * (3 * L + i + 1))
                        pe.wait_ge(S["hf_done"], START + 2 * NT * L + 3 * i + u - 2)
                        for k in range(KT):
                            mm = pe.transpose(ps[:, 2 * u + k // 4, (k % 4) * P:(k % 4 + 1) * P], xt[:, u, k * P:(k + 1) * P], ident[:])
                        mm.then_inc(S["xT_ps"], 1)
                phase(pe, L, 0)
                for g in range(3):
                    a = slice(g * GRP, (g + 1) * GRP)
                    for k in range(KT):
                        if g == 0:
                            pe.wait_ge(S["w_lo_done"], slot(L, 0, k) + 1)
                        mm = product(ps[:, 4 + g, 0:GRP], w_hi[:, k, 256:384], w_lo[:, k, 256:384], hi[:, k, a], lo[:, k, a],
                                     k == 0, k == KT - 1)
                    mm.then_inc(S["g_ps"], 1)
                for t in range(NT):
                    pe.wait_ge(S["z_done"], START + 45 * L + t - 2)
                    dense(L, 0, t, t % 3, 256, False, t == NT - 1, S["z_ps"])
                with pe.Fori(0, 4) as c:
                    for t in range(NT):
                        pe.wait_ge(S["z_done"], START + 45 * L + 9 * c + 9 + t - 2)
                        dense(L, c + 1, t, t % 3, W, t == 0, t == NT - 1, S["z_ps"])
                phase(pe, L, 1)
                pe.wait_ge(S["act_row"], 2 * L + 2)
                own(pe)
                for t in range(NT):
                    for q, r in enumerate((ri, rf, r_r, r_d)):
                        o = (t % 3) * 4 * ROWS + q * ROWS
                        pe.transpose(ps[:, t // 3, o:o + ROWS], r[:, t * P:(t + 1) * P], ident[0:ROWS, 0:ROWS])
                pe.wait_ge(S["ml_ld"], 48 * L + 48)
                for j in range(4):
                    mm = pe.matmul(ps[:, 3, j * NT:(j + 1) * NT], selc[0:ROWS, 8 + j], mrow[:, 4], start=True, stop=True)
                mm.then_inc(S["rt_ps"], 1)
                phase(pe, L, 2)

                def states(n):
                    pe.wait_ge(S["u_v"], NT * L + n + 1)
                    pe.wait_ge(S["u_kw"], NT * L + n + 1)
                    pe.wait_ge(S["u_done"], START + NT * L + n)
                    for d in range(2):
                        for p_ in range(2):
                            mm = pe.matmul(ps[:, d, p_ * PV:(p_ + 1) * PV], kw[:, d, p_ * P:(p_ + 1) * P],
                                           vext[:, 2 * p_:2 * p_ + 2, :].rearrange("p a b -> p (a b)"), start=True, stop=True)
                    mm.then_inc(S["u_ps"], 1)

                with pe.Fori(0, NS) as c:
                    states(c)
                states(NS)
                phase(pe, L, 3)

                def mlstm(c, n, s_f, s_b):
                    pe.wait_ge(S["m_w"], START + NT * L + n)
                    for d in range(2):
                        for h in range(MH):
                            pe.matmul(ps[:, 2 + d, h * P:(h + 1) * P], selc[0:ROWS, d * MH + h],
                                      r_m[:, bass.ds(c * P, P)], start=(h == 0), stop=False, skip_group_check=True)
                        mm = pe.matmul(ps[:, 2 + d, :], idr[:], mkr[:, d].unsqueeze(1).broadcast_to([P, MH, P]),
                                       start=False, stop=True, skip_group_check=True)
                    mm.then_inc(S["m_D"], 1)
                    pe.wait_ge(S["m_st"], NT * L + n + 1)
                    pe.wait_ge(S["m_qk"], START + NT * L + n)
                    for p_ in range(2):
                        pe.transpose(ps[:, 0, p_ * P:(p_ + 1) * P], qs[:, p_ * P:(p_ + 1) * P], ident[:])
                        mm = pe.transpose(ps[:, 0, (2 + p_) * P:(3 + p_) * P], ks[:, p_ * P:(p_ + 1) * P], ident[:])
                    mm.then_inc(S["m_tp"], 1)
                    pe.wait_ge(S["m_qk"], START + NT * L + n + 1)
                    pe.wait_ge(S["m_sw"], START + NT * L + n)
                    for p_ in range(2):
                        mm = pe.matmul(ps[:, 1, p_ * 256:(p_ + 1) * 256], kT[:, p_],
                                       qbd[:, p_].rearrange("p a b -> p (a b)"), start=True, stop=True)
                    mm.then_inc(S["m_S"], 1)
                    pe.wait_ge(S["m_fin"], START + NT * L + n)
                    for d, s_ in enumerate((s_f, s_b)):
                        for p_ in range(2):
                            pe.matmul(ps[:, 6 + d, p_ * PV:(p_ + 1) * PV], qT[:, p_], cs[:, s_, d, p_], start=True, stop=True)
                    pe.wait_ge(S["m_sw"], START + NT * L + n + 1)
                    for d in range(2):
                        for h in range(MH):
                            mm = pe.matmul(ps[:, 4 + d, h * VE:(h + 1) * VE], wt[:, d, h], vext[:, h], start=True, stop=True)
                    mm.then_inc(S["m_num"], 1)

                with pe.Fori(0, NS) as c:
                    mlstm(c, c, c, 7 - c)
                mlstm(NS, NS, 9, 9)
                phase(pe, L, 4)
                with pe.Fori(0, 3) as i:
                    for u in range(3):
                        pe.wait_ge(S["gm_vn"], START + 18 * L + 3 * i + u + 1)
                        for g in range(4):
                            mm = pe.matmul(ps[:, u, g * HD:(g + 1) * HD], wst[:, g], vn[:, 3 * i + u, g * HD:(g + 1) * HD],
                                           start=True, stop=True)
                        mm.then_inc(S["gm_ps"], 1)
                        if u == 2:
                            pe.wait_ge(S["gm_vn"], START + 18 * L + NT + 3 * i + 3)
                phase(pe, L, 5)

                def keys(n):
                    pe.wait_ge(S["kd_done"], START + 10 * L + n + 1)
                    pe.wait_ge(S["k_lo"], START + 10 * L + n)
                    for v in range(HKV):
                        mm = pe.transpose(ps[:, 0, v * P:(v + 1) * P], qd[:, v].rearrange("p a b -> p (a b)"), ident[:])
                    mm.then_inc(S["kd_ps"], 1)

                with pe.Fori(0, 10) as n:
                    keys(n)
                phase(pe, L, 6)

                def queries_T(G, g):
                    pe.wait_ge(S["qd_done"], G + 1)
                    pe.wait_ge(S["oy_done"], START + G - 2)
                    for h in range(HG):
                        mm = pe.transpose(ps[:, 7, h * P:(h + 1) * P], qd[:, g * HG + h].rearrange("p a b -> p (a b)"), ident[:])
                    mm.then_inc(S["q_ps"], 1)

                def scores(G, g, h, nk, pk):
                    pe.wait_ge(S["mx_done"], START + HG * G + h)
                    if h == 0:
                        pe.wait_ge(S["q_hi_done"], G + 1)
                        if pk:
                            pe.wait_ge(S["rv_done"], G - 1)
                    k0, w_ = (0, GRP) if nk == NT else (NT * P, P)
                    for b in range(3 if nk == NT else 1):
                        mm = pe.matmul(ps[:, b, 0:w_], q_hi[:, g, h], kst[:, g, k0 + b * w_:k0 + (b + 1) * w_], start=True, stop=True)
                    mm.then_inc(S["s_ps"], 1)

                def scores_T(G, E, g, j, nk, pk):
                    if j == 0:
                        pe.wait_ge(S["q_lo_done"], START + G + 1)
                        pe.wait_ge(S["dg_done"], HG * G + HG)
                    pe.wait_ge(S["ex_done"], START + (E + j if pk == 1 else E + j - 2))
                    key = kst[:, g, (j if nk == NT else NT) * P:(j + 1 if nk == NT else NT + 1) * P]
                    out = ps[:, 3 + j % 3, :]
                    pe.matmul(out, one_r[:], dg[:, g].rearrange("p a b -> p (a b)"), start=True, stop=False)
                    pe.matmul(out, key, q_hi[:, g].rearrange("p a b -> p (a b)"), start=False, stop=False)
                    pe.matmul(out, key, q_lo[:, g].rearrange("p a b -> p (a b)"), start=False, stop=True).then_inc(S["st_ps"], 1)

                def values(G, e, g, j, nk):
                    if j == 0:
                        pe.wait_ge(S["o_cp"], START + G)
                    pe.wait_ge(S["p_lo_done"], START + e + 1)
                    val = vst[:, g, j if nk == NT else NT]
                    pe.matmul(ps[:, 6, :], val, p_hi[:, j % 3], start=(j == 0), stop=False)
                    mm = pe.matmul(ps[:, 6, :], val, p_lo[:, j % 3], start=False, stop=(j == nk - 1))
                    mm.then_inc(S["pv_done"], 1)

                def sums(G, A, g, heads):
                    pe.wait_ge(S["mx_done"], START + heads)
                    pe.wait_ge(S["sum_done"], START + A)
                    for h in range(HG):
                        mm = pe.matmul(ps[:, 2, GRP + h:GRP + h + 1], psm[:, g, h * P:(h + 1) * P], ones[:, 0:1], start=True, stop=True)
                    mm.then_inc(S["sm_ps"], 1)

                def outputs_T(G, g):
                    pe.wait_ge(S["o_cp"], START + G + 1)
                    for h in range(HG):
                        mm = pe.transpose(ps[:, 7, h * P:(h + 1) * P], o_s[:, h * P:(h + 1) * P], ident[:])
                    mm.then_inc(S["ot_ps"], 1)

                def step(t, g, nk, pk, nn, prep):
                    G, E, A = counts(L, t, g)
                    last = [j for j in range(max(pk - 2, 0), pk)]
                    for j in range(nk):
                        scores_T(G, E, g, j, nk, pk)
                        if j > 1:
                            values(G, E + j - 2, g, j - 2, nk)
                        for k in last if nk == 1 else last[j:j + 1]:
                            values(G - 1, E - pk + k, 1 - g, k, pk)
                        if pk and j == min(1, nk - 1):
                            sums(G - 1, A, 1 - g, HG * (G + 1))
                        if nn and j == 0:
                            queries_T(G + 1, 1 - g)
                        for key, h in SCORES_AT.items():
                            if nn and j == min(key, nk - 1):
                                scores(G + 1, 1 - g, h, nn, pk)
                        if pk and j == min(5, nk - 1):
                            if nn:
                                pe.wait_ge(S["q_lo_done"], START + G + 2)
                            outputs_T(G - 1, 1 - g)

                queries_T(NG * L, 0)
                for h in range(HG):
                    scores(NG * L, 0, h, NT, 0)
                walk(pe, L, step)
                values(NG * (L + 1) - 1, N_E * (L + 1) - 1, 1, 0, 1)
                sums(NG * (L + 1) - 1, N_A * (L + 1), 1, HG * NG * (L + 1))
                outputs_T(NG * (L + 1) - 1, 1)
                phase(pe, L, 7)
                for t in range(NT):
                    pe.wait_ge(S["y_lo"], START + NT * L + t - 2)
                    for k in range(KT):
                        c = (ZQ + k * P) if k < 4 else (ZOM + (k - 4) * P) if k < 6 else (ZUG + (k - 6) * P)
                        mm = pe.transpose(ps[:, 2 * (t % 3) + k // 4, (k % 4) * P:(k % 4 + 1) * P], z[:, t, c:c + P], ident[:])
                    mm.then_inc(S["yT_ps"], 1)
                phase(pe, L, 8)
                with pe.Fori(0, 2) as n:
                    for t in range(NT):
                        pe.wait_ge(S["xr_half"], START + 18 * L + 9 * n + t - 2)
                        dense(L, n + 5, t, t % 3, W, t == 0, t == NT - 1, S["o_out"])
                phase(pe, L, 9)
                for t in range(NT):
                    pe.wait_ge(S["hf_done"], START + 2 * NT * L + NT + t - 2)
                    for k in range(KT):
                        mm = pe.transpose(ps[:, 2 * (t % 3) + k // 4, (k % 4) * P:(k % 4 + 1) * P], xr[:, t, k * P:(k + 1) * P], ident[:])
                    mm.then_inc(S["xT_ps"], 1)
                phase(pe, L, 10)
                with pe.Fori(0, NFF) as i:
                    for b in range(12):
                        n = 12 * (NFF * L + i) + b
                        m, g = b // 3, b % 3
                        a = slice(g * GRP, (g + 1) * GRP)
                        pe.wait_ge(S["r_done"], START + n - 2)
                        for k in range(KT):
                            if b == 0:
                                pe.wait_ge(S["w_lo_done"], slot(L, 2 * i + 7, k) + 1)
                            mm = product(ps[:, g, 0:GRP], w_hi[:, k, m * P:(m + 1) * P], w_lo[:, k, m * P:(m + 1) * P],
                                         hi[:, k, a], lo[:, k, a], k == 0, k == KT - 1, S["w_used"] if b == 11 and k else None)
                        mm.then_inc(S["h_ps"], 1)
                    for b in range(18):
                        n = 18 * (NFF * L + i) + b
                        t, hf_ = b // 2, b % 2
                        a = slice(t * P, (t + 1) * P)
                        if b in (0, 6, 12):
                            pe.wait_ge(S["flo_done"], START + 12 * (NFF * L + i) + 10 + b // 6)
                        pe.wait_ge(S["f_acc"], START + n - 2)
                        for m in range(4):
                            if t == 0:
                                pe.wait_ge(S["w_lo_done"], slot(L, 2 * i + 8, 4 * hf_ + m) + 1)
                            mm = product(ps[:, 3 + b % 3, :], f_hi[:, m, a], f_lo[:, m, a], w_hi[:, 4 * hf_ + m, :], w_lo[:, 4 * hf_ + m, :],
                                         m == 0, m == 3, S["w_used"] if t == NT - 1 and (m or hf_) else None)
                        mm.then_inc(S["f_ps"], 1)
                phase(pe, L, 11)
                phase(pe, L, 12)


_INS = ["x_in", "cond", "w_mod", "b_mod", "w_slots", "consts", "rope", "cache_k", "cache_v", "state0", "row_in",
        "qk_g", "gln", "ws_t", "bs_t", "ln_gb"]
_OUTS = [(NT, P, D), (NL, P, P), (NL, P, P), (NL, 2, MH, HD, HD), (NL, 2, MH, HD, 1), (NL, 2, MH, 1)]


def layout(x_prompt, x_sample, c, cache_attn_k, cache_attn_v, state_mlstm_C, state_mlstm_n, state_mlstm_m,
           c_ctx, w_mod, b_mod, w_in, q_norm_g, k_norm_g, mlstm_gate_b, gmlp_ln_g, gmlp_ln_b, gmlp_ws, gmlp_bs,
           w_out, ln1_g, ln1_b, w_ff1, w_ff2, ln2_g, ln2_b):
    f = np.float32
    a = {k: np.asarray(v) for k, v in locals().items() if k != "f"}
    out = {}
    out["x_in"] = np.concatenate([a["x_sample"].reshape(NS, P, D), a["x_prompt"].reshape(1, P, D)])
    out["cond"] = np.stack([a["c_ctx"].reshape(KT, P), a["c"].reshape(KT, P)], -1).transpose(1, 0, 2)
    out["w_mod"] = a["w_mod"].reshape(NL, KT, P, 12, W).transpose(0, 3, 2, 1, 4).reshape(NL * 12, P, KT, W)
    out["b_mod"] = np.broadcast_to(a["b_mod"].reshape(1, NL * 12, W), (2, NL * 12, W))
    o = np.cumsum([0, 512, 128, 128, 256, 256, 256, 256, 16, 256, 256])
    qa, ka, va, qm, km, vm, om, gm, ug, vg = (a["w_in"][:, :, o[i]:o[i + 1]] for i in range(10))
    first = np.zeros((NL, D, W), f)
    first[:, :, 0:256] = ug
    for kind, at in ((0, 256), (2, 256 + 32), (1, 256 + 64), (3, 256 + 96)):
        first[:, :, at:at + MH] = gm[:, :, kind * MH:(kind + 1) * MH]
    slots = np.zeros(((NL * GROUPS + 1) * SLOTS, P, W), f)
    for l in range(NL):
        groups = [first[l], np.concatenate([qm[l], km[l]], -1), np.concatenate([vm[l], om[l]], -1), qa[l],
                  np.concatenate([ka[l], va[l], vg[l]], -1), a["w_out"][l][:, :W], a["w_out"][l][:, W:]]
        groups = [g.reshape(KT, P, W) for g in groups]
        for i in range(NFF):
            groups.append(a["w_ff1"][l][:, i * HC:(i + 1) * HC].reshape(KT, P, W))
            w2 = a["w_ff2"][l][i * HC:(i + 1) * HC].reshape(HC // P, P, 2, W)
            groups.append(w2.transpose(2, 0, 1, 3).reshape(SLOTS, P, W))
        for g, v in enumerate(groups):
            s = (l * GROUPS + g) * SLOTS
            slots[s:s + SLOTS] = v
    out["w_slots"] = slots
    out["consts"] = constants()
    out["rope"] = rope_tables()
    out["cache_k"] = a["cache_attn_k"].reshape(NL, P, P)
    out["cache_v"] = a["cache_attn_v"].reshape(NL, P, P)
    s0 = np.zeros((NL, 2, HD, 2, 2, 2, VE), f)
    C, n = a["state_mlstm_C"][0], a["state_mlstm_n"][0]
    for h in range(MH):
        s0[:, h % 2, :, :, h // 2, h % 2, 0:HD] = C[:, :, h].transpose(0, 2, 1, 3)
        s0[:, h % 2, :, :, h // 2, h % 2, HD] = n[:, :, h].transpose(0, 2, 1)
    out["state0"] = s0.reshape(NL, P, 2, 2, PV)
    r = np.zeros((NL, ROWS, 3), f)
    gb, m = a["mlstm_gate_b"], a["state_mlstm_m"][0]
    for d in range(2):
        r[:, 32 * d:32 * d + MH, 0] = gb[:, 2 * d]
        r[:, 32 * d:32 * d + MH, 1] = gb[:, 2 * d + 1]
        r[:, 32 * d:32 * d + MH, 2] = m[:, d]
    out["row_in"] = r

    def rows(v):
        return np.broadcast_to(v[:, None], (NL, P, *v.shape[1:]))
    out["qk_g"] = rows(np.stack([a["q_norm_g"], a["k_norm_g"]], 1))
    out["gln"] = rows(np.stack([a["gmlp_ln_g"], a["gmlp_ln_b"]], 1))
    out["ws_t"] = a["gmlp_ws"].transpose(0, 3, 1, 2)
    out["bs_t"] = a["gmlp_bs"].transpose(0, 2, 1)
    out["ln_gb"] = np.stack([a["ln1_g"], a["ln1_b"], a["ln2_g"], a["ln2_b"]], 1)
    return {k: np.ascontiguousarray(out[k]) for k in _INS}


def program(nc, arrays):
    args = [nc.dram_tensor(f"in_{n}", v.shape, F32, kind="ExternalInput").ap() for n, v in arrays.items()]
    args += [nc.dram_tensor(f"out_{i}", s, F32, kind="ExternalOutput").ap() for i, s in enumerate(_OUTS)]
    build(nc, *args)


def kernel(**inputs):
    import concourse.bacc as bacc
    from concourse.bass_utils import run_bass_kernel_spmd
    arrays = layout(**inputs)
    nc = bacc.Bacc("TRN2", target_bir_lowering=False, num_devices=1)
    program(nc, arrays)
    r = run_bass_kernel_spmd(nc, [{f"in_{n}": v for n, v in arrays.items()}], core_ids=[0])
    y, k, v, c, n, m = (r.results[0][f"out_{i}"] for i in range(len(_OUTS)))
    return (y[NS:NT].reshape(1, SEQ, D), y[0:NS].reshape(1, DEC_SEQ, D),
            k.reshape(1, NL, SEQ, HKV, HD), v.reshape(1, NL, SEQ, HKV, HD),
            c.reshape(1, NL, 2, MH, HD, HD), n.reshape(1, NL, 2, MH, HD), m.reshape(1, NL, 2, MH))
```

```python
from contextlib import ExitStack

import numpy as np

import concourse.bass as bass
from concourse import mybir

ALU = mybir.AluOpType
ACT = mybir.ActivationFunctionType
AX = mybir.AxisListType
F32 = mybir.dt.float32
F32R = mybir.dt.float32r

P = 128
D = 1024
KT = D // P
SEQ = 128
DEC_SEQ = 1024
NS = DEC_SEQ // P
NT = NS + 1
TOK = NT * P
GRP = 3 * P
NL = 2
HD = 64
HQ, HKV = 8, 2
HG = HQ // HKV
MH = 4
FF = 4 * D
HC = 4 * P
NFF = FF // HC
W = 512
EPS = 1e-6
M_SCALE = HD ** -0.5
ALPHA = (2 * NL) ** 0.25
NEG = -1e30

ZQM, ZKM, ZVM, ZOM, ZQ, ZK, ZV, ZVG, ZUG = 0, 256, 512, 768, 1024, 1536, 1664, 1792, 2048
ZW = 2304
SLOTS = 8
G_IN, G_OUT, G_FF = 5, 2, 2 * NFF
GROUPS = G_IN + G_OUT + G_FF
RAW = 4

ROWS = 36
VE = HD + 1
PV = 2 * VE
NG = 2 * NT
N_E = 2 * (NS * NT + 1)
N_A = 2 * (NS * (NT - 1) + 1)
SCORES_AT = {3: 0, 4: 1, 5: 2, 6: 3}
LAG = 4


def ring(j):
    return j % LAG if j < 2 * LAG else LAG


START = 8
NSLOT = 11

C_ID, C_MF, C_MB, C_BM, C_SEL, C_SELP = 0, 128, 256, 384, 514, 514 + 8 * 128
NCONST = C_SELP + 4 * 128


def constants():
    k = np.zeros((P, NCONST), np.float32)
    k[:, C_ID:C_ID + P] = np.eye(P)
    s, t = np.arange(P)[:, None], np.arange(P)[None]
    k[:, C_MF:C_MF + P] = np.where(s <= t, 0.0, NEG)
    k[:, C_MB:C_MB + P] = np.where(s >= t, 0.0, NEG)
    k[:HD, C_BM:C_BM + VE] = 1.0
    k[HD:, C_BM + VE:C_BM + PV] = 1.0
    for d in range(2):
        for h in range(MH):
            r = 32 * d + h
            k[r, C_SEL + (d * MH + h) * P:C_SEL + (d * MH + h + 1) * P] = 1.0
            o = C_SELP + (d * 2 + h // 2) * P + (h % 2) * HD
            k[r, o:o + HD] = 1.0
    return k


def rope_tables():
    n = HD // 4
    inv = (10000.0 ** (-np.arange(n, dtype=np.float32) / n)).astype(np.float32)
    pos = np.arange(DEC_SEQ)
    out = np.zeros((DEC_SEQ, 2, HD), np.float32)
    for i, p in enumerate((pos // 64, pos % 64)):
        ang = (p.astype(np.float32)[:, None] * inv[None]).astype(np.float32)
        c, s = np.cos(ang), np.sin(ang)
        o = i * HD // 2
        out[:, 0, o:o + n], out[:, 0, o + n:o + 2 * n] = c, c
        out[:, 1, o:o + n], out[:, 1, o + n:o + 2 * n] = -s, s
    return out.reshape(NS, P, 2, HD).transpose(1, 0, 2, 3)



def build(nc, x_in, cond, w_mod, b_mod, w_slots, consts, rope, cache_k, cache_v, state0, row_in,
          qk_g, gln, ws_t, bs_t, ln_gb, y_out, k_out, v_out, c_out, n_out, m_out):
    x1_dram = nc.dram_tensor("x1_dram", (NT, P, D), F32, kind="Internal").ap()
    mod_dram = nc.dram_tensor("mod_dram", (NL * 12, 2, W), F32, kind="Internal").ap()

    with ExitStack() as ctx:
        a_w = 16512
        a_b = a_w + (2 * SLOTS + RAW) * W * 4
        a_a = a_b + NT * ZW * 4
        a_m = a_a + 2 * KT * TOK * 4
        a_end = 229344

        def region(start, end):
            free = [start]

            def place(name, shape, dt=F32, rows=P):
                t = nc.alloc_sbuf_tensor_at(name, [rows, *shape], dt, offset=free[0])
                free[0] += (int(np.prod(shape)) * 4 + 31) // 32 * 32
                assert free[0] <= end, (name, free[0] - end)
                return t
            return place

        put = region(a_w, a_b)
        w_hi = put("w_hi", [SLOTS, W], F32R)
        w_lo = put("w_lo", [SLOTS, W], F32R)
        w_raw = put("w_raw", [RAW, W])
        put = region(a_b, a_a)
        modw = put("modw", [2, KT, W])
        modb = put("modb", [NL * 12, W], rows=2)
        put = region(a_b, a_a)
        acc = put("acc", [NT, D])
        hf = put("hf", [3, D])
        put = region(a_b, a_a)
        z = put("z", [NT, ZW])
        put = region(a_b, a_a)
        xr = put("xr", [NT, D])
        hf2 = put("hf2", [3, D])
        lnb = put("lnb", [2, D])
        gate = put("gate", [2, D])
        lnt = put("lnt", [2, W])
        put = region(a_b + NT * D * 4, a_a)
        f_hi = put("f_hi", [HC // P, TOK], F32R)
        f_lo = put("f_lo", [HC // P, TOK], F32R)
        fr = put("fr", [2, GRP])
        fsq = put("fsq", [2, GRP])
        put = region(a_a, a_m)
        x1t = put("x1t", [NT, D])
        lnb2 = put("lnb2", [2, D])
        gate2 = put("gate2", [2, D])
        put = region(a_a, a_m)
        modr = put("modr", [NL * 12, W], rows=2)
        put = region(a_a, a_m)
        hi = put("hi", [KT, TOK], F32R)
        lo = put("lo", [KT, TOK], F32R)
        put = region(a_a, a_m)
        r_r = put("r_r", [TOK], rows=ROWS)
        r_d = put("r_d", [TOK], rows=ROWS)
        r_b = put("r_b", [TOK], rows=ROWS)
        r_m = put("r_m", [TOK], rows=ROWS)
        cs = put("cs", [NSLOT, 2, 2, PV])
        cols = put("cols", [NT, 4, ROWS])
        selc = put("selc", [12, P])
        bmask = put("bmask", [PV])
        kw = put("kw", [2, 256])
        vext = put("vext", [MH, VE])
        qs = put("qs", [256])
        ks = put("ks", [256])
        qT = put("qT", [2, P])
        kT = put("kT", [2, P])
        qbd = put("qbd", [2, 2, P])
        wt = put("wt", [2, MH, P])
        hn = put("hn", [2, MH, VE])
        hh = put("hh", [2, MH, HD])
        og = put("og", [256])
        dec = put("dec", [8, 2, 2])
        mrow = put("mrow", [5, NT], rows=ROWS)
        den = put("den", [2, 2, MH])
        put = region(a_a, a_a + 3 * TOK * 4)
        wt2 = put("wt2", [2, MH, P])
        vext2 = put("vext2", [MH, VE])
        qT2 = put("qT2", [2, P])
        og2 = put("og2", [256])
        kw2 = put("kw2", [2, 256])
        r_bd = put("r_bd", [2 * MH, P], rows=ROWS)
        wts, vexts, qTs, ogs, kws = (wt, wt2), (vext, vext2), (qT, qT2), (og, og2), (kw, kw2)
        put = region(a_a, a_m)
        wst = put("wst", [4, P])
        glnb = put("glnb", [2, 256])
        vn = put("vn", [NT, 256])
        gs = put("gs", [3, 256])
        bst = put("bst", [4])
        put = region(a_a, a_m)
        kst = put("kst", [HKV, 10 * P], F32R)
        vst = put("vst", [HKV, 10, P], F32R)
        q_hi = put("q_hi", [2, HG, P], F32R)
        q_lo = put("q_lo", [2, HG, P], F32R)
        pr = put("pr", [5, HG * P])
        p_hi = put("p_hi", [5, HG * P], F32R)
        p_lo = put("p_lo", [5, HG * P], F32R)
        psm = put("psm", [2, HG * P])
        dg = put("dg", [2, HG, P], F32R)
        o_s = put("o_s", [HG * P])
        rp = put("rp", [NS, 2, HD])
        put = region(a_a + (2 * HKV * 10 * P + 2 * 2 * HG * P) * 4, a_m)
        kn = put("kn", [NT, P])
        kd = put("kd", [10, HKV, 2, HD])
        sq = put("sq", [3, HQ * HD])
        put = region(a_m, a_end)
        ident = put("ident", [P])
        idr = put("idr", [P], F32R)
        mkr = put("mkr", [2, P], F32R)
        maskt = put("maskt", [2, P])
        ri = put("ri", [TOK], rows=ROWS)
        rf = put("rf", [TOK], rows=ROWS)
        modc = put("modc", [64])
        mod64 = put("mod64", [P], rows=64)
        sc = put("sc", [KT, 2])
        sce = put("sce", [KT, 2])
        condt = put("condt", [KT, 2])
        rcon = put("rcon", [3], rows=ROWS)
        st6 = put("st6", [NT, 2, 6])
        mv = put("mv", [NT, 2])
        rs = put("rs", [NT])
        nmean = put("nmean", [NT])
        nbias = put("nbias", [NT])
        half = put("half", [NT * 10])
        nm = put("nm", [2, HG])
        rinv = put("rinv", [HG])
        ss = put("ss", [NT, 10])
        put = region(a_m + 4 * 512, a_m + 6 * 512)
        one_r = put("one_r", [P], F32R)
        ones = put("ones", [P])
        put = region(a_m + 6 * 512, a_m + 6 * 512 + 2 * TOK * 4)
        qd = put("qd", [HQ, 2, HD])
        kvt = put("kvt", [2, P])
        gq = put("gq", [2, HD])
        qn = put("qn", [HQ * HD])
        ps = ctx.enter_context(nc.psum_tensor("ps", [P, 8, 512], F32))

        def sem(name):
            return ctx.enter_context(nc.semaphore(name))

        names = """passed x_copied const_ld mod_b_ld mod_st mod_ready silu_e mod_ps mod_row phase_end
            w_hi_done w_lo_done w_used
            mc_ld mc_ps xT_ps hf_done hi_done h_done row_ld
            z_ps z_done g_ps
            act_row dve_row abs_row pow_in pow_out rt_ps ml_ld ml_zero ml_one
            u_v u_kw u_ps u_done m_st m_tp m_qk m_bd m_D m_S m_w m_sw m_num m_og m_fin st_out
            gm_ld gm_x gm_vn gm_ps
            at_ld v_hi kd_done kd_ps k_hi k_lo kv_out
            qd_done q_ps q_hi_done q_lo_done s_ps mx_done dg_done st_ps ex_done p_hi_done p_lo_done sum_done pv_done
            o_cp ot_ps sm_ps rv_done ot_cp oy_done
            yT_ps y_hi y_lo o_out xr_half ln_ld xr_done x1_st
            h_ps r_done fhi_done flo_done f_ps f_acc acc_zero ln_in ln_rs ln_x ln_g y_rdy ln_st""".split()
        S = dict((n, sem(n)) for n in names)
        w_ld = [sem(f"w_ld{j}") for j in range(RAW)]
        x_ld = [sem(f"x_ld{j}") for j in range(3)]
        mod_w_ld = [sem(f"mod_w_ld{j}") for j in range(2)]
        x1_ld = [sem(f"x1_ld{j}") for j in range(3)]

        NB = 11

        def own(eng):
            eng.sem_inc(S["passed"], 1)

        def phase(eng, L, b):
            own(eng)
            eng.drain().then_inc(S["phase_end"], 1)
            eng.wait_ge(S["phase_end"], 4 * NB * L + 4 * (b + 2))
            own(eng)

        def counts(L, t, g):
            if isinstance(t, int) and t == NS:
                return NG * L + 2 * NS + g, N_E * L + 2 * NS * NT + g, N_A * L + 2 * NS * (NT - 1) + g
            return NG * L + 2 * t + g, N_E * L + 2 * NT * t + NT * g, N_A * L + 2 * (NT - 1) * t + (NT - 1) * g

        def walk(eng, L, step):
            step(0, 0, NT, 0, NT, 1)
            step(0, 1, NT, NT, NT, 1)
            with eng.Fori(1, NS - 1) as t:
                for g in range(2):
                    step(t, g, NT, NT, NT, t + 1)
            step(NS - 1, 0, NT, NT, NT, NS)
            step(NS - 1, 1, NT, NT, 1, NS)
            step(NS, 0, 1, NT, 1, None)
            step(NS, 1, 1, 1, 0, None)

        def slot(L, g, j):
            return L * (GROUPS * SLOTS) + g * SLOTS + j

        def split_hi(act, L, g, prev, js=range(SLOTS)):
            for j in js:
                act.wait_ge(w_ld[j % RAW], 16 * (L * (GROUPS * 2) + 2 * g + j // RAW + 1))
                if prev and j < SLOTS - 1:
                    act.wait_ge(S["w_used"], START + (SLOTS - 1) * (L * GROUPS + g - 1) + j + 1)
                elif prev:
                    act.wait_ge(*prev)
                act.copy(w_hi[:, j, :], w_raw[:, j % RAW, :]).then_inc(S["w_hi_done"], 1)

        def split_lo(dve, L, g, js=range(SLOTS)):
            for j in js:
                dve.wait_ge(S["w_hi_done"], slot(L, g, j) + 1)
                dve.tensor_tensor(w_lo[:, j, :], w_raw[:, j % RAW, :], w_hi[:, j, :].bitcast(F32),
                                  ALU.subtract).then_inc(S["w_lo_done"], 1)

        def col(L, which, kind, kt, g):
            c = which * 32 + (kind * 2 + kt // 4) * 8 + g * 4 + kt % 4
            return modc[:, c:c + 1]

        def spread(ap, n):
            return ap.unsqueeze(1).broadcast_to([ap.shape[0], n, *ap.shape[1:]])

        block = ctx.enter_context(nc.Block())

        @block.sync
        def _(sp):
            sp.dma_start(ident[:], consts[:, C_ID:C_ID + P]).then_inc(S["const_ld"], 16)
            sp.dma_start(maskt[:].rearrange("p a b -> p (a b)"), consts[:, C_MF:C_MF + 2 * P]).then_inc(S["const_ld"], 16)
            sp.dma_start(condt[:], cond).then_inc(S["const_ld"], 16)
            for n in range(2):
                sp.dma_start(modw[:, n], w_mod[n]).then_inc(mod_w_ld[n], 16)
            for j in range(RAW):
                sp.dma_start(w_raw[:, j, :], w_slots[j]).then_inc(w_ld[j], 16)
            sp.dma_start(y_out, x_in).then_inc(S["x_copied"], 16)
            with sp.Fori(0, NL * 12 // 2 - 1) as i:
                for u in range(2):
                    sp.wait_ge(S["mod_ps"], 2 * i + u + 1)
                    sp.dma_start(modw[:, u], w_mod[2 * i + u + 2]).then_inc(mod_w_ld[u], 16)
            sp.wait_ge(S["mod_row"], START + NL * 12)
            for j in range(3):
                sp.dma_start(acc[:, 3 * j:3 * j + 3], x_in[3 * j:3 * j + 3].rearrange("t p d -> p t d")).then_inc(x_ld[j], 16)
            with sp.Fori(0, (NL * GROUPS + 1) * SLOTS // RAW - 1) as i:
                for j in range(RAW):
                    sp.wait_ge(S["w_lo_done"], RAW * i + j + 1)
                    sp.dma_start(w_raw[:, j, :], w_slots[RAW * i + RAW + j]).then_inc(w_ld[j], 16)

        @block.gpsimd
        def _(pool):
            pool.memset(half[:], -0.5)
            pool.sem_inc(S["h_done"], START)
            pool.sem_inc(S["sum_done"], START)
            pool.dma_start(modb[:], b_mod).then_inc(S["mod_b_ld"], 16)
            pool.wait_ge(S["mod_row"], START + NL * 12)
            pool.dma_start(mod_dram.rearrange("n g f -> g n f"), modr[:]).then_inc(S["mod_st"], 16)
            pool.wait_ge(S["mod_st"], 16)
            pool.wait_ge(S["x_copied"], 16)
            phase(pool, 0, -1)

            pool.memset(ones[:], 1.0)

            def rstd(L, k, ap, n):
                pool.wait_ge(S["pow_in"], 3 * L + k + 1)
                return pool.tensor_tensor(ap, ap, half[:, 0:NT * n].rearrange("p (a b) -> p a b", b=n), ALU.pow)

            def norm_rows(L, w, x, gain, store):
                for t in range(NT + 2):
                    if t < NT:
                        n, r = NT * (2 * L + w) + t, rs[:, t:t + 1]
                        pool.wait_ge(S["ln_in"], n + 1)
                        pool.tensor_tensor(r, r, half[:, 0:1], ALU.pow)
                        pool.drain()
                        pool.tensor_tensor(nbias[:, t:t + 1], nmean[:, t:t + 1], r, ALU.mult).then_inc(S["ln_rs"], 1)
                    if 1 <= t <= NT:
                        pool.wait_ge(S["ln_x"], NT * (2 * L + w) + t)
                        pool.tensor_tensor(x[:, t - 1], x[:, t - 1], gain, ALU.mult).then_inc(S["ln_g"], 1)
                    if t > 1:
                        store(t - 2)

            def lo_of(t, src, count):
                pool.wait_ge(S["hi_done"], count + 1)
                pool.tensor_tensor(lo[:, :, bass.ds(t * P, P)], src.rearrange("p (k c) -> p k c", c=P),
                                   hi[:, :, bass.ds(t * P, P)].bitcast(F32), ALU.subtract).then_inc(S["h_done"], 1)

            with pool.Fori(0, NL) as L:
                for k in range(2):
                    pool.dma_start(mod64[32 * k:32 * k + 32, :],
                                   mod_dram[bass.ds(L * 12 + 6 * k, 4)].rearrange("n g (q f) -> (n g q) f", f=P)
                                   ).then_inc(S["mc_ld"], 16)
                pool.dma_start(rcon[:], row_in[L]).then_inc(S["row_ld"], 16)
                for t in range(NT):
                    lo_of(t, hf[:, t % 3], 2 * NT * L + t)
                phase(pool, L, 0)
                phase(pool, L, 1)
                pool.dma_start(selc[:], consts[:, C_SEL:C_SEL + 12 * P].rearrange("p (a b) -> p a b", b=P)).then_inc(S["ml_ld"], 16)
                pool.dma_start(bmask[:], consts[:, C_BM:C_BM + PV]).then_inc(S["ml_ld"], 16)
                pool.dma_start(cs[:, 0], state0[L]).then_inc(S["ml_ld"], 16)
                pool.memset(cs[:, 9], 0.0)
                pool.memset(qbd[:], 0.0)
                pool.memset(vext[:], 1.0).then_inc(S["ml_zero"], 1)
                pool.wait_ge(S["ml_ld"], 48 * L + 48)
                phase(pool, L, 2)
                pool.memset(vext2[:], 1.0).then_inc(S["ml_one"], 1)
                phase(pool, L, 3)
                with pool.Fori(0, NT) as n:
                    pool.wait_ge(S["m_D"], START + NT * L + n)
                    pool.tensor_tensor(r_bd[:], spread(r_m[:, bass.ds(n * P, P)], 2 * MH), selc[0:ROWS, 0:2 * MH],
                                       ALU.mult).then_inc(S["m_bd"], 1)
                for d in range(2):
                    for h in range(MH):
                        part, o = (h % 2) * HD, (h % 2) * VE
                        pool.dma_start(c_out[L, d, h], cs[part:part + HD, 10, d, h // 2, o:o + HD]).then_inc(S["st_out"], 16)
                        pool.dma_start(n_out[L, d, h], cs[part:part + HD, 10, d, h // 2, o + HD:o + VE]).then_inc(S["st_out"], 16)
                    pool.dma_start(m_out[L, d], mrow[32 * d:32 * d + MH, 3, NS:NT]).then_inc(S["st_out"], 16)
                pool.wait_ge(S["st_out"], 16 * 18 * (L + 1))
                phase(pool, L, 4)
                pool.dma_start(wst[:], ws_t[L]).then_inc(S["gm_ld"], 16)
                pool.dma_start(bst[:], bs_t[L]).then_inc(S["gm_ld"], 16)
                pool.dma_start(glnb[:], gln[L]).then_inc(S["gm_ld"], 16)
                rstd(L, 0, rs[:].unsqueeze(2), 1)
                pool.drain()
                pool.tensor_tensor(nbias[:], nmean[:], rs[:], ALU.mult).then_inc(S["pow_out"], 1)
                phase(pool, L, 5)
                pool.tensor_copy(one_r[:], ones[:])
                pool.dma_start(kvt[:, 0], cache_k[L]).then_inc(S["at_ld"], 16)
                pool.dma_start(kvt[:, 1], cache_v[L]).then_inc(S["at_ld"], 16)
                pool.dma_start(gq[:], qk_g[L]).then_inc(S["at_ld"], 16)
                pool.dma_start(rp[:], rope).then_inc(S["at_ld"], 16)
                rstd(L, 1, ss[:, :, HQ:HQ + HKV], HKV).then_inc(S["pow_out"], 1)
                rstd(L, 2, ss[:, :, 0:HQ], HQ).then_inc(S["pow_out"], 1)
                pool.wait_ge(S["kd_done"], L + 1)
                own(pool)
                pool.dma_start(k_out[L], kn[:, NS]).then_inc(S["kv_out"], 16)
                pool.dma_start(v_out[L], z[:, NS, ZV:ZV + P]).then_inc(S["kv_out"], 16)
                pool.wait_ge(S["kv_out"], 32 * L + 32)
                phase(pool, L, 6)
                def diagonal(G, g, h):
                    pool.wait_ge(S["mx_done"], START + HG * (G + 1) + h + 1)
                    n_ = 1 - g
                    pool.tensor_tensor(dg[:, n_, h], ident[:], nm[:, n_, h:h + 1].broadcast_to([P, P]),
                                       ALU.mult).then_inc(S["dg_done"], 1)

                def step(t, g, nk, pk, nn, prep):
                    G, E, A = counts(L, t, g)
                    pool.wait_ge(S["sm_ps"], START + G - 1)
                    if nk == 1:
                        pool.wait_ge(S["ex_done"], START + E + 1)
                        own(pool)
                        pool.tensor_copy(psm[:, g], pr[:, 0]).then_inc(S["sum_done"], 1)
                        for h in range(HG if nn else 0):
                            diagonal(G, g, h)
                    else:
                        for j in range(1, nk):
                            pool.wait_ge(S["ex_done"], START + E + j + 1)
                            if j > 1:
                                pool.wait_ge(S["sum_done"], START + A + j - 1)
                            pool.tensor_tensor(psm[:, g], pr[:, 0] if j == 1 else psm[:, g], pr[:, ring(j)],
                                               ALU.add).then_inc(S["sum_done"], 1)
                            if j - 1 in SCORES_AT:
                                diagonal(G, g, SCORES_AT[j - 1])

                for h in range(HG):
                    diagonal(NG * L - 1, 1, h)
                walk(pool, L, step)
                phase(pool, L, 7)
                phase(pool, L, 8)
                pool.dma_start(xr[:], y_out.rearrange("t p d -> p t d")).then_inc(S["ln_ld"], 16)
                for g in range(2):
                    for n in range(2):
                        pool.dma_start(gate[:, g, n * W:(n + 1) * W],
                                       mod_dram[L * 12 + 4 + n, g].partition_broadcast(P)).then_inc(S["ln_ld"], 16)
                for k in range(2):
                    pool.dma_start(lnb[:, k], ln_gb[L, k].partition_broadcast(P)).then_inc(S["ln_ld"], 16)

                def store1(t):
                    pool.wait_ge(S["xr_done"], NT * L + t + 1)
                    own(pool)
                    pool.dma_start(x1_dram[t], xr[:, t]).then_inc(S["x1_st"], 16)

                norm_rows(L, 0, xr, lnb[:, 0], store1)
                for t in range(NT):
                    lo_of(t, hf2[:, t % 3], 2 * NT * L + NT + t)
                pool.wait_ge(S["x1_st"], 16 * NT * (L + 1))
                phase(pool, L, 9)
                pool.memset(acc[:], 0.0).then_inc(S["acc_zero"], 1)
                pool.wait_ge(S["h_ps"], START + 12 * NFF * (L + 1))
                own(pool)
                for g in range(2):
                    for n in range(2):
                        pool.dma_start(gate2[:, g, n * W:(n + 1) * W],
                                       mod_dram[L * 12 + 10 + n, g].partition_broadcast(P)).then_inc(S["ln_ld"], 16)
                for u in range(3):
                    pool.dma_start(x1t[:, 3 * u:3 * u + 3], x1_dram[3 * u:3 * u + 3].rearrange("t p d -> p t d")).then_inc(x1_ld[u], 16)
                    if u == 0:
                        for k in range(2):
                            pool.dma_start(lnb2[:, k], ln_gb[L, 2 + k].partition_broadcast(P)).then_inc(S["ln_ld"], 16)

                def store2(t):
                    pool.wait_ge(S["y_rdy"], NT * L + t + 1)
                    own(pool)
                    pool.dma_start(y_out[t], acc[:, t]).then_inc(S["ln_st"], 16)

                pool.wait_ge(S["ln_ld"], 16 * (13 * L + 13))
                norm_rows(L, 1, acc, lnb2[:, 0], store2)
                pool.wait_ge(S["ln_st"], 16 * NT * (L + 1))
                phase(pool, L, 10)

        @block.scalar
        def _(act):
            for n in ("z_done", "ex_done", "r_done", "m_w", "o_cp"):
                act.sem_inc(S[n], START)
            act.wait_ge(S["const_ld"], 48)
            act.activation(sce[:], condt[:], ACT.Exp, scale=-1.0).then_inc(S["silu_e"], 1)
            act.copy(idr[:], ident[:])
            act.copy(mkr[:], maskt[:])
            split_hi(act, 0, 0, None)
            phase(act, 0, -1)

            def hi_of(t, src, count):
                act.wait_ge(S["hf_done"], START + count + 1)
                act.copy(hi[:, :, bass.ds(t * P, P)], src.rearrange("p (k c) -> p k c", c=P)).then_inc(S["hi_done"], 1)

            def norm_rows(L, w, x):
                for t in range(NT):
                    act.wait_ge(S["ln_rs"], NT * (2 * L + w) + t + 1)
                    act.activation(x[:, t], x[:, t], ACT.Identity, bias=nbias[:, t:t + 1],
                                   scale=rs[:, t:t + 1]).then_inc(S["ln_x"], 1)

            def z_tile(L, c, t, dst, src):
                act.wait_ge(S["z_ps"], START + 45 * L + 9 * c + t + 1)
                act.copy(dst, src).then_inc(S["z_done"], 1)

            def states_v(L, n, u):
                act.wait_ge(S["u_ps"], START + NT * L + n - 1)
                act.copy(vexts[u][:, :, 0:HD], z[:, n, ZVM:ZVM + 256].rearrange("p (h e) -> p h e", e=HD)).then_inc(S["u_v"], 1)

            def mlstm(L, n, u):
                N = NT * L + n
                act.wait_ge(S["m_tp"], START + N)
                act.copy(qs[:], z[:, n, ZQM:ZQM + 256])
                act.activation(ks[:], z[:, n, ZKM:ZKM + 256], ACT.Copy, scale=M_SCALE)
                act.wait_ge(S["m_num"], START + N - 1)
                act.copy(vexts[u][:, :, 0:HD], z[:, n, ZVM:ZVM + 256].rearrange("p (h e) -> p h e", e=HD)).then_inc(S["m_st"], 1)
                act.wait_ge(S["m_fin"], START + N - 1)
                act.activation(ogs[u][:], z[:, n, ZOM:ZOM + 256], ACT.Exp, scale=-1.0).then_inc(S["m_og"], 1)
                act.wait_ge(S["m_D"], START + N + 1)
                for d in range(2):
                    for h in range(MH):
                        ins = act.activation(wts[u][:, d, h], ps[:, 2 + d, h * P:(h + 1) * P], ACT.Exp,
                                             bias=cols[:, n, 0, 32 * d + h:32 * d + h + 1])
                ins.then_inc(S["m_w"], 1)

            with act.Fori(0, NL) as L:
                with act.Fori(0, 3) as i:
                    for u in range(3):
                        hi_of(3 * i + u, hf[:, u], 2 * NT * L + 3 * i + u)
                phase(act, L, 0)
                act.wait_ge(S["row_ld"], 16 * L + 16)
                for g in range(3):
                    act.wait_ge(S["g_ps"], 3 * L + g + 1)
                    act.activation(ri[:, g * GRP:(g + 1) * GRP], ps[0:ROWS, 4 + g, 0:GRP], ACT.Identity, bias=rcon[:, 0:1])
                    act.activation(rf[:, g * GRP:(g + 1) * GRP], ps[64:64 + ROWS, 4 + g, 0:GRP], ACT.Identity, bias=rcon[:, 1:2])
                for t in range(NT - 1):
                    z_tile(L, 0, t, z[:, t, ZUG:ZUG + 256], ps[:, t % 3, 0:256])
                split_hi(act, L, 1, (S["z_ps"], START + 45 * L + 9))
                z_tile(L, 0, NT - 1, z[:, NT - 1, ZUG:ZUG + 256], ps[:, 2, 0:256])
                with act.Fori(0, 4) as c:
                    for t in range(NT - 1):
                        z_tile(L, c + 1, t, z[:, t, bass.ds(c * W, W)], ps[:, t % 3, :])
                    split_hi(act, L, c + 2, (S["z_ps"], START + 45 * L + 9 * c + 18))
                    z_tile(L, c + 1, NT - 1, z[:, NT - 1, bass.ds(c * W, W)], ps[:, 2, :])
                phase(act, L, 1)
                act.wait_ge(S["abs_row"], L + 1)
                act.activation(r_b[:], r_b[:], ACT.Exp, scale=-1.0)
                act.drain()
                act.activation(r_b[:], r_b[:], ACT.Ln, bias=1.0).then_inc(S["act_row"], 1)
                act.wait_ge(S["dve_row"], L + 1)
                act.activation(rf[:], rf[:], ACT.Exp)
                act.activation(r_r[:], r_r[:], ACT.Exp)
                act.activation(r_d[:], r_d[:], ACT.Exp, scale=-1.0)
                act.activation(mrow[:, 4], mrow[:, 4], ACT.Exp).then_inc(S["act_row"], 1)
                phase(act, L, 2)
                act.wait_ge(S["ml_one"], L + 1)
                own(act)
                with act.Fori(0, NS // 2) as i:
                    for u in range(2):
                        states_v(L, 2 * i + u, u)
                states_v(L, NS, 0)
                phase(act, L, 3)
                with act.Fori(0, NS // 2) as i:
                    for u in range(2):
                        mlstm(L, 2 * i + u, u)
                mlstm(L, NS, 0)
                phase(act, L, 4)
                act.wait_ge(S["pow_out"], 3 * L + 1)
                own(act)
                for t in range(NT):
                    act.activation(vn[:, t], z[:, t, ZVG:ZVG + 256], ACT.Identity, bias=nbias[:, t:t + 1],
                                   scale=rs[:, t:t + 1]).then_inc(S["gm_x"], 1)
                phase(act, L, 5)
                act.wait_ge(S["at_ld"], 64 * L + 64)
                for v in range(HKV):
                    c = v * HD
                    act.copy(vst[:, v, 0:NS, 0:HD], z[:, 0:NS, ZV + c:ZV + c + HD])
                    act.copy(vst[:, v, 8, 0:HD], kvt[:, 1, c:c + HD])
                    ins = act.copy(vst[:, v, 9, 0:HD], z[:, NS, ZV + c:ZV + c + HD])
                ins.then_inc(S["v_hi"], 1)

                with act.Fori(0, 5) as i:
                    for u in range(2):
                        n = 10 * L + 2 * i + u
                        k2 = bass.ds((2 * i + u) * P, P)
                        act.wait_ge(S["kd_ps"], n + 1)
                        act.wait_ge(S["k_lo"], START + n - 1)
                        act.copy(kst[0:HD, :, k2], ps[0:HD, u, 0:2 * P].rearrange("p (a b) -> p a b", b=P))
                        act.copy(q_hi[HD:P, u, 0:2], ps[HD:P, u, 0:2 * P].rearrange("p (a b) -> p a b", b=P)).then_inc(S["k_hi"], 1)
                phase(act, L, 6)

                def queries_hi(G, g):
                    act.wait_ge(S["q_ps"], G + 1)
                    act.copy(q_hi[:, g], ps[:, 7, :].rearrange("p (a b) -> p a b", b=P)).then_inc(S["q_hi_done"], 1)

                def exp_(E, A, j, fresh):
                    act.wait_ge(S["st_ps"], E + j + 1)
                    act.wait_ge(S["p_lo_done"], START + (E + j if fresh else E + j + 1 - LAG))
                    act.wait_ge(S["sum_done"], START + A + (0 if fresh else j - LAG if j < LAG else max(j - LAG, 1)))
                    act.activation(pr[:, ring(j)], ps[:, 3 + j % 3, :], ACT.Exp).then_inc(S["ex_done"], 1)

                def hi_(e, j, fresh=False):
                    act.wait_ge(S["ex_done"], START + e + 1)
                    act.wait_ge(S["pv_done"], START + (e if fresh else e + 1 - LAG))
                    act.copy(p_hi[:, ring(j)], pr[:, ring(j)]).then_inc(S["p_hi_done"], 1)

                def sums_out(G, E):
                    act.wait_ge(S["oy_done"], START + G)
                    act.wait_ge(S["pv_done"], START + E)
                    act.copy(o_s[:], ps[:, 6, :]).then_inc(S["o_cp"], 1)

                def turned_out(G):
                    act.wait_ge(S["ot_ps"], START + G + 1)
                    act.copy(o_s[:, 0:256].rearrange("p (a b) -> p a b", b=HD),
                             ps[:, 7, :].rearrange("p (a b) -> p a b", b=P)[:, :, 0:HD]).then_inc(S["ot_cp"], 1)

                def step(t, g, nk, pk, nn, prep):
                    G, E, A = counts(L, t, g)
                    for j in range(nk):
                        if pk == 1:
                            hi_(E - 1, 0)
                        exp_(E, A, j, pk == 1)
                        if (j or pk) and pk != 1:
                            hi_(E + j - 1, (j or pk) - 1)
                        if nn and j == min(2, nk - 1):
                            queries_hi(G + 1, 1 - g)
                        if pk and j == min(3, nk - 1):
                            sums_out(G - 1, E)
                        if pk and j == min(7, nk - 1):
                            turned_out(G - 1)

                queries_hi(NG * L, 0)
                walk(act, L, step)
                hi_(N_E * (L + 1) - 1, 0, True)
                sums_out(NG * (L + 1) - 1, N_E * (L + 1))
                turned_out(NG * (L + 1) - 1)
                phase(act, L, 7)
                for t in range(NT):
                    act.wait_ge(S["yT_ps"], NT * L + t + 1)
                    for k in range(2):
                        ins = act.copy(hi[:, 4 * k:4 * k + 4, t * P:(t + 1) * P],
                                       ps[:, 2 * (t % 3) + k, :].rearrange("p (a b) -> p a b", b=P))
                    ins.then_inc(S["y_hi"], 1)
                phase(act, L, 8)
                split_hi(act, L, 6, (S["o_out"], START + 18 * L + 9))
                norm_rows(L, 0, xr)
                for half_, tiles in ((0, range(3)), (1, range(3, NT))):
                    split_hi(act, L, 7, (S["o_out"], START + 18 * L + 18), range(RAW * half_, RAW * half_ + RAW))
                    for t in tiles:
                        hi_of(t, hf2[:, t % 3], 2 * NT * L + NT + t)
                phase(act, L, 9)

                def hidden(i, b):
                    n = 12 * (NFF * L + i) + b
                    act.wait_ge(S["h_ps"], START + n + 1)
                    act.wait_ge(S["flo_done"], START + n - 1)
                    act.activation(fr[:, b % 2], ps[:, b % 3, 0:GRP], ACT.Relu).then_inc(S["r_done"], 1)
                    act.drain()
                    act.activation(f_hi[:, b // 3, (b % 3) * GRP:(b % 3 + 1) * GRP], fr[:, b % 2],
                                   ACT.Square).then_inc(S["fhi_done"], 1)

                def chunk(i):
                    for b in range(11):
                        hidden(i, b)
                    split_hi(act, L, 2 * i + 8, (S["h_ps"], START + 12 * (NFF * L + i) + 12))
                    hidden(i, 11)

                with act.Fori(0, NFF - 1) as i:
                    chunk(i)
                    split_hi(act, L, 2 * i + 9, (S["f_ps"], START + 18 * (NFF * L + i) + 18))
                chunk(NFF - 1)
                norm_rows(L, 1, acc)
                split_hi(act, L, 2 * NFF + 7, (S["f_ps"], START + 18 * NFF * (L + 1)))
                phase(act, L, 10)

        @block.vector
        def _(dve):
            for n in ("mod_row", "hf_done", "u_done", "m_qk", "m_sw", "m_fin", "gm_vn", "k_lo",
                      "mx_done", "p_lo_done", "oy_done", "q_lo_done", "y_lo", "xr_half", "flo_done", "f_acc"):
                dve.sem_inc(S[n], START)
            dve.wait_ge(S["silu_e"], 1)
            dve.tensor_scalar(sce[:], sce[:], 1.0, None, ALU.add)
            dve.drain()
            dve.reciprocal(sce[:], sce[:])
            dve.drain()
            dve.tensor_tensor(sc[:], sce[:], condt[:], ALU.mult).then_inc(S["mod_ready"], 1)
            dve.wait_ge(S["mod_b_ld"], 16)
            own(dve)
            with dve.Fori(0, NL * 12 // 2) as i:
                for u in range(2):
                    dve.wait_ge(S["mod_ps"], 2 * i + u + 1)
                    dve.tensor_tensor(modr[:, 2 * i + u], ps[0:2, u, :], modb[:, 2 * i + u], ALU.add).then_inc(S["mod_row"], 1)
            split_lo(dve, 0, 0)
            phase(dve, 0, -1)

            def modulate(L, n, which, dst, u, g):
                dve.wait_ge(S["xT_ps"], 2 * NT * L + n + 1)
                dve.wait_ge(S["h_done"], START + 2 * NT * L + n - 2)
                for kt in range(KT):
                    ins = dve.tensor_scalar(dst[:, u, kt * P:(kt + 1) * P],
                                            ps[:, 2 * u + kt // 4, (kt % 4) * P:(kt % 4 + 1) * P],
                                            col(L, which, 1, kt, g), col(L, which, 0, kt, g), ALU.mult, ALU.add)
                ins.then_inc(S["hf_done"], 1)

            def b2(ap, n):
                return ap.unsqueeze(len(ap.shape)).broadcast_to([*ap.shape, n])

            def statistics(x, t):
                dve.drain()
                for j in range(2):
                    dve.bn_stats(st6[:, t, j], x[:, t, j * W:(j + 1) * W])
                dve.drain()
                dve.bn_aggr(mv[:, t], st6[:, t].rearrange("p a b -> p (a b)"))
                dve.drain()
                dve.tensor_scalar(nmean[:, t:t + 1], mv[:, t, 0:1], -1.0, None, ALU.mult)
                dve.tensor_scalar(rs[:, t:t + 1], mv[:, t, 1:2], EPS, None, ALU.add).then_inc(S["ln_in"], 1)

            def offset(L, w, x, t, bias, done):
                dve.wait_ge(S["ln_g"], NT * (2 * L + w) + t + 1)
                dve.tensor_tensor(x[:, t], x[:, t], bias, ALU.add).then_inc(done, 1)

            with dve.Fori(0, NL) as L:
                dve.wait_ge(S["mc_ps"], L + 1)
                for k in range(2):
                    dve.tensor_copy(modc[:, 32 * k:32 * k + 16], ps[:, 7, 32 * k:32 * k + 16])
                    dve.tensor_scalar(modc[:, 32 * k + 16:32 * k + 32], ps[:, 7, 32 * k + 16:32 * k + 32], 1.0, None, ALU.add)
                dve.drain()
                with dve.Fori(0, 2) as i:
                    for u in range(3):
                        modulate(L, 3 * i + u, 0, hf, u, 1)
                for u in range(3):
                    modulate(L, 6 + u, 0, hf, u, int(u < 2))
                phase(dve, L, 0)
                with dve.Fori(0, 5) as c:
                    split_lo(dve, L, c + 1)
                phase(dve, L, 1)
                dve.scalar_tensor_tensor(r_b[:], rf[:], -1.0, rf[:], ALU.mult, ALU.max).then_inc(S["abs_row"], 1)
                dve.memset(r_r[:], 1.0)
                dve.memset(r_d[:], 0.0)
                dve.memset(r_m[:], 0.0)
                dve.memset(mrow[:], 0.0)
                dve.drain()
                dve.memset(r_r[:, 0:TOK:P], 0.0)
                dve.wait_ge(S["act_row"], 2 * L + 1)
                dve.scalar_tensor_tensor(rf[:], rf[:], 0.0, r_b[:], ALU.min, ALU.subtract)
                dve.drain()
                F, Bk = slice(0, MH), slice(32, 32 + MH)
                dve.tensor_tensor_scan(r_b[F], r_r[F], rf[F], 0.0, ALU.mult, ALU.add)
                dve.tensor_tensor_scan(r_b[Bk, ::-1], r_r[Bk], rf[Bk, ::-1], 0.0, ALU.mult, ALU.add)
                dve.drain()
                dve.tensor_copy(r_d[F, P:DEC_SEQ:P], r_b[F, P - 1:DEC_SEQ - P:P])
                dve.tensor_copy(r_d[Bk, P - 1:DEC_SEQ - P:P], r_b[Bk, P:DEC_SEQ:P])
                dve.tensor_tensor(ri[:], ri[:], r_b[:], ALU.subtract)
                dve.drain()
                N = DEC_SEQ
                dve.tensor_tensor_scan(r_m[F, 0:N], r_d[F, 0:N], ri[F, 0:N], rcon[F, 2:3], ALU.add, ALU.max)
                dve.tensor_tensor_scan(r_m[F, N:TOK], r_d[F, N:TOK], ri[F, N:TOK], 0.0, ALU.add, ALU.max)
                dve.tensor_tensor_scan(r_m[Bk, N - 1::-1], r_d[Bk, N - 1::-1], ri[Bk, N - 1::-1], rcon[Bk, 2:3], ALU.add, ALU.max)
                dve.tensor_tensor_scan(r_m[Bk, TOK - 1:N - 1:-1], r_d[Bk, TOK - 1:N - 1:-1], ri[Bk, TOK - 1:N - 1:-1],
                                       0.0, ALU.add, ALU.max)
                dve.drain()
                dve.tensor_copy(mrow[F, 0], r_b[F, P - 1:TOK:P])
                dve.tensor_copy(mrow[Bk, 0], r_b[Bk, 0:TOK:P])
                dve.tensor_copy(mrow[F, 1], r_m[F, P - 1:TOK:P])
                dve.tensor_copy(mrow[Bk, 1], r_m[Bk, 0:TOK:P])
                dve.tensor_copy(mrow[F, 2, 0:1], rcon[F, 2:3])
                dve.tensor_copy(mrow[Bk, 2, NS - 1:NS], rcon[Bk, 2:3])
                dve.drain()
                dve.tensor_tensor(mrow[:, 3], mrow[:, 0], mrow[:, 1], ALU.add)
                dve.drain()
                dve.tensor_copy(mrow[F, 2, 1:NS], mrow[F, 3, 0:NS - 1])
                dve.tensor_copy(mrow[Bk, 2, 0:NS - 1], mrow[Bk, 3, 1:NS])
                dve.drain()
                dve.tensor_tensor(mrow[:, 4], mrow[:, 2], mrow[:, 1], ALU.subtract)
                v3 = lambda r: r[:].rearrange("p (c t) -> p c t", t=P)
                dve.tensor_tensor(v3(rf), v3(ri), b2(mrow[:, 1], P), ALU.subtract)
                dve.tensor_tensor(v3(r_r), b2(mrow[:, 2], P), v3(r_m), ALU.subtract)
                dve.tensor_tensor(r_d[:], r_b[:], r_m[:], ALU.add).then_inc(S["dve_row"], 1)
                dve.drain()
                dve.tensor_scalar(r_m[:], r_m[:], -1.0, None, ALU.mult)
                dve.wait_ge(S["rt_ps"], L + 1)
                dve.tensor_copy(cols[:].rearrange("p (a b) c d -> p a (b c d)", b=3), ps[:, 0:3, 0:12 * ROWS])
                for p_ in range(2):
                    dve.tensor_copy(dec[:, :, 0, p_], ps[:, 3, p_ * NT:p_ * NT + NS])
                    dve.tensor_copy(dec[:, :, 1, p_], ps[:, 3, (2 + p_) * NT:(2 + p_) * NT + NS][:, ::-1])
                phase(dve, L, 2)

                def keys_w(n, u):
                    dve.wait_ge(S["u_ps"], START + NT * L + n - 1)
                    for d in range(2):
                        ins = dve.scalar_tensor_tensor(kws[u][:, d].rearrange("p (h e) -> p h e", e=HD),
                                                       z[:, n, ZKM:ZKM + 256].rearrange("p (h e) -> p h e", e=HD), M_SCALE,
                                                       b2(cols[:, n, 1, 32 * d:32 * d + MH], HD), ALU.mult, ALU.mult)
                    ins.then_inc(S["u_kw"], 1)

                def states(n, u, s_f, s_b):
                    dve.wait_ge(S["u_ps"], START + NT * L + n + 1)
                    for d, s_ in enumerate((s_f, s_b)):
                        ins = dve.tensor_tensor(cs[:, s_, d], ps[:, 2 * u + d, 0:2 * PV].rearrange("p (a b) -> p a b", b=PV),
                                                spread(bmask[:], 2), ALU.mult)
                    ins.then_inc(S["u_done"], 1)

                keys_w(0, 0)
                with dve.Fori(0, NS // 2) as i:
                    for u in range(2):
                        n = 2 * i + u
                        keys_w(n + 1, 1 - u)
                        states(n, u, n + 1, 8 - n)
                states(NS, 0, 10, 10)
                dve.drain()
                tmp = hn[:].rearrange("p a b c -> p (a b c)")
                flat = lambda ap: ap.rearrange("p a b c -> p (a b) c")
                with dve.Fori(0, NS) as i:
                    dve.tensor_tensor(tmp.rearrange("p (a b) -> p a b", b=PV), flat(cs[:, i]),
                                      b2(dec[:, i].rearrange("p a b -> p (a b)"), PV), ALU.mult)
                    dve.drain()
                    dve.tensor_tensor(flat(cs[:, i + 1]), flat(cs[:, i + 1]), tmp.rearrange("p (a b) -> p a b", b=PV), ALU.add)
                    dve.drain()
                phase(dve, L, 3)

                def turned(n, u):
                    N = NT * L + n
                    dve.wait_ge(S["m_tp"], START + N + 1)
                    dve.wait_ge(S["m_S"], START + N)
                    dve.wait_ge(S["m_num"], START + N - 1)
                    for p_ in range(2):
                        a = slice(HD * p_, HD * p_ + HD)
                        dve.tensor_copy(qbd[a, :, p_, :], ps[a, 0, 0:2 * P].rearrange("p (a b) -> p a b", b=P))
                    dve.tensor_copy(qTs[u][:], ps[:, 0, 0:2 * P].rearrange("p (a b) -> p a b", b=P))
                    dve.tensor_copy(kT[:], ps[:, 0, 2 * P:4 * P].rearrange("p (a b) -> p a b", b=P)).then_inc(S["m_qk"], 1)

                def weighted(n, u):
                    N = NT * L + n
                    og_, wt_ = ogs[u], wts[u]
                    dve.wait_ge(S["m_S"], START + N + 1)
                    dve.wait_ge(S["m_w"], START + N + 1)
                    for d in range(2):
                        ins = dve.tensor_tensor(wt_[:, d].rearrange("p a b -> p (a b)"), ps[:, 1, :],
                                                wt_[:, d].rearrange("p a b -> p (a b)"), ALU.mult)
                    ins.then_inc(S["m_sw"], 1)
                    dve.wait_ge(S["m_og"], N + 1)
                    dve.tensor_scalar(og_[:], og_[:], 1.0, None, ALU.add)
                    dve.drain()
                    dve.reciprocal(og_[:], og_[:])

                def outputs_m(n, u):
                    N = NT * L + n
                    dve.wait_ge(S["m_num"], START + N + 1)
                    v = lambda b: ps[:, b, 0:2 * PV].rearrange("p (a b) -> p a b", b=VE)
                    for d in range(2):
                        dve.tensor_tensor(hn[:, d], v(6 + d), b2(cols[:, n, 2, 32 * d:32 * d + MH], VE), ALU.mult)
                    dve.drain()
                    for d in range(2):
                        dve.tensor_tensor(hn[:, d], hn[:, d], v(4 + d), ALU.add)
                    dve.drain()
                    dve.scalar_tensor_tensor(den[:, 0], hn[:, :, :, HD], -1.0, hn[:, :, :, HD], ALU.mult, ALU.max)
                    dve.drain()
                    for d in range(2):
                        dve.tensor_tensor(den[:, 0, d], den[:, 0, d], cols[:, n, 3, 32 * d:32 * d + MH], ALU.max)
                    dve.drain()
                    dve.reciprocal(den[:, 1], den[:, 0])
                    dve.drain()
                    for d in range(2):
                        dve.tensor_tensor(hh[:, d], hn[:, d, :, 0:HD], b2(den[:, 1, d], HD), ALU.mult)
                    dve.drain()
                    dve.tensor_tensor(hh[:, 0], hh[:, 0], hh[:, 1], ALU.add)
                    dve.drain()
                    dve.tensor_tensor(z[:, n, ZOM:ZOM + 256], hh[:, 0].rearrange("p a b -> p (a b)"), ogs[u][:],
                                      ALU.mult).then_inc(S["m_fin"], 1)

                turned(0, 0)
                with dve.Fori(0, NS // 2) as i:
                    for u in range(2):
                        n = 2 * i + u
                        turned(n + 1, 1 - u)
                        weighted(n, u)
                        outputs_m(n, u)
                weighted(NS, 0)
                outputs_m(NS, 0)
                phase(dve, L, 4)
                for t in range(NT):
                    dve.bn_stats(st6[:, t, 0], z[:, t, ZVG:ZVG + 256])
                dve.drain()
                for t in range(NT):
                    dve.bn_aggr(mv[:, t], st6[:, t, 0])
                dve.drain()
                dve.tensor_scalar(nmean[:], mv[:, :, 0], -1.0, None, ALU.mult)
                dve.tensor_scalar(rs[:], mv[:, :, 1], EPS, None, ALU.add).then_inc(S["pow_in"], 1)
                dve.wait_ge(S["gm_ld"], 48 * L + 48)

                def normed_v(i):
                    v3 = vn[:, 3 * i:3 * i + 3]
                    dve.wait_ge(S["gm_x"], NT * L + 3 * i + 3)
                    dve.tensor_tensor(v3, v3, spread(glnb[:, 0], 3), ALU.mult)
                    dve.drain()
                    dve.tensor_tensor(v3, v3, spread(glnb[:, 1], 3), ALU.add).then_inc(S["gm_vn"], 1)

                def gated(i):
                    ug = z[:, 3 * i:3 * i + 3, ZUG:ZUG + 256]
                    dve.wait_ge(S["gm_ps"], 3 * L + i + 1)
                    for u in range(3):
                        dve.tensor_tensor(gs[:, u].rearrange("p (a b) -> p a b", b=HD),
                                          ps[:, 3 * (i % 2) + u, 0:256].rearrange("p (a b) -> p a b", b=HD),
                                          b2(bst[:], HD), ALU.add)
                    dve.drain()
                    dve.tensor_tensor(ug, ug, gs[:], ALU.mult).then_inc(S["gm_vn"], 1)

                normed_v(0)
                normed_v(1)
                gated(0)
                normed_v(2)
                dve.drain()
                gated(1)
                dve.drain()
                gated(2)
                phase(dve, L, 5)

                sk = sq[:].rearrange("p a b -> p (a b)")[:, 0:NT * P]
                k3 = z[:, :, ZK:ZK + P]
                dve.tensor_tensor(sk.rearrange("p (a b) -> p a b", b=P), k3, k3, ALU.mult)
                dve.drain()
                dve.tensor_reduce(ss[:, :, HQ:HQ + HKV], sk.rearrange("p (a b c) -> p a b c", b=HKV, c=HD), AX.X, ALU.add)
                dve.drain()
                k3 = ss[:, :, HQ:HQ + HKV]
                dve.tensor_scalar(k3, k3, 1.0 / HD, EPS, ALU.mult, ALU.add).then_inc(S["pow_in"], 1)
                for i in range(3):
                    q3 = z[:, 3 * i:3 * i + 3, ZQ:ZQ + HQ * HD]
                    dve.tensor_tensor(sq[:], q3, q3, ALU.mult)
                    dve.drain()
                    dve.tensor_reduce(ss[:, 3 * i:3 * i + 3, 0:HQ], sq[:].rearrange("p a (b c) -> p a b c", c=HD), AX.X, ALU.add)
                    dve.drain()
                q3 = ss[:, :, 0:HQ]
                dve.tensor_scalar(q3, q3, 1.0 / HD, EPS, ALU.mult, ALU.add).then_inc(S["pow_in"], 1)
                dve.wait_ge(S["at_ld"], 64 * L + 64)
                dve.wait_ge(S["v_hi"], L + 1)
                for v in range(HKV):
                    c = v * HD
                    for o_, i_ in ((vst[:, v, 0:NS], z[:, 0:NS, ZV + c:ZV + c + HD]), (vst[:, v, 8], kvt[:, 1, c:c + HD]),
                                   (vst[:, v, 9], z[:, NS, ZV + c:ZV + c + HD])):
                        o_h, o_l = (o_[:, :, 0:HD], o_[:, :, HD:P]) if len(o_.shape) == 3 else (o_[:, 0:HD], o_[:, HD:P])
                        dve.tensor_tensor(o_l, i_, o_h.bitcast(F32), ALU.subtract)
                dve.wait_ge(S["pow_out"], 3 * L + 2)
                own(dve)

                def normed(t, nh, c0, k0, which, extra):
                    o_ = qn[:, 0:nh * HD].rearrange("p (a b) -> p a b", b=HD)
                    dve.tensor_tensor(o_, z[:, t, c0:c0 + nh * HD].rearrange("p (a b) -> p a b", b=HD),
                                      b2(ss[:, t, k0:k0 + nh], HD), ALU.mult)
                    dve.drain()
                    dve.scalar_tensor_tensor(o_, o_, extra, spread(gq[:, which], nh), ALU.mult, ALU.mult)
                    dve.drain()

                def rotated(t, nh, a):
                    o_ = qn[:, 0:nh * HD].rearrange("p (a b) -> p a b", b=HD)
                    dve.tensor_tensor(qd[:, a:a + nh, 0], o_, spread(rp[:, t, 0], nh), ALU.mult)
                    for r in range(2):
                        h_ = HD // 2
                        q4 = o_[:, :, r * h_:(r + 1) * h_].rearrange("p a (b c) -> p a b c", b=2)
                        d4 = qd[:, a:a + nh, 1, r * h_:(r + 1) * h_].rearrange("p a (b c) -> p a b c", b=2)
                        s4 = rp[:, t, 1, r * h_:(r + 1) * h_].rearrange("p (b c) -> p b c", b=2)
                        dve.tensor_tensor(d4, q4[:, :, ::-1, :], spread(s4, nh), ALU.mult)
                    dve.drain()
                    dve.tensor_tensor(qd[:, a:a + nh, 0], qd[:, a:a + nh, 0], qd[:, a:a + nh, 1], ALU.add)
                    dve.drain()
                    return dve.tensor_copy(qd[:, a:a + nh, 1], qd[:, a:a + nh, 0])

                flat2 = lambda ap: ap.rearrange("p a b -> p (a b)").rearrange("p (a b) -> p a b", b=HD)
                kn4 = kn[:].rearrange("p a (b c) -> p a b c", c=HD)
                dve.tensor_tensor(kn4, z[:, :, ZK:ZK + P].rearrange("p a (b c) -> p a b c", c=HD),
                                  b2(ss[:, :, HQ:HQ + HKV], HD), ALU.mult)
                dve.drain()
                dve.tensor_tensor(flat2(kn[:]), flat2(kn[:]), spread(gq[:, 1], NT * HKV), ALU.mult)
                dve.drain()
                for v in range(HKV):
                    kv_ = kn4[:, 0:NS, v]
                    dve.tensor_tensor(kd[:, 0:NS, v, 0], kv_, rp[:, :, 0], ALU.mult)
                    for r in range(2):
                        h_ = slice(r * HD // 2, (r + 1) * HD // 2)
                        k4, d4, s4 = (ap[:, :, h_].rearrange("p a (b c) -> p a b c", b=2)
                                      for ap in (kv_, kd[:, 0:NS, v, 1], rp[:, :, 1]))
                        dve.tensor_tensor(d4, k4[:, :, ::-1, :], s4, ALU.mult)
                dve.drain()
                for v in range(HKV):
                    dve.tensor_tensor(kd[:, 0:NS, v, 0], kd[:, 0:NS, v, 0], kd[:, 0:NS, v, 1], ALU.add)
                for tile, src in ((NS, kvt[:, 0]), (NT, kn[:, NS])):
                    dve.tensor_copy(kd[:, tile], src.rearrange("p (a b) -> p a b", b=HD).unsqueeze(2)
                                    .broadcast_to([P, HKV, 2, HD]))
                dve.drain()
                for v in range(HKV):
                    ins = dve.tensor_copy(kd[:, 0:NS, v, 1], kd[:, 0:NS, v, 0])
                ins.then_inc(S["kd_done"], 1)
                with dve.Fori(0, 5) as i:
                    for u in range(2):
                        n = 2 * i + u
                        dve.wait_ge(S["k_hi"], 10 * L + n + 1)
                        dve.tensor_tensor(kst[HD:P, :, bass.ds(n * P, P)], ps[HD:P, u, 0:2 * P].rearrange("p (a b) -> p a b", b=P),
                                          q_hi[HD:P, u, 0:2].bitcast(F32), ALU.subtract).then_inc(S["k_lo"], 1)
                phase(dve, L, 6)

                def queries(t, g, part=2):
                    o = g * HG
                    if part != 1:
                        normed(t, HG, ZQ + o * HD, o, 0, HD ** -0.5)
                    if part and isinstance(t, int) and t == NS:
                        dve.tensor_copy(qd[:, o:o + HG], qn[:, 0:HG * HD].rearrange("p (a b) -> p a b", b=HD).unsqueeze(2)
                                        .broadcast_to([P, HG, 2, HD])).then_inc(S["qd_done"], 1)
                    elif part:
                        rotated(t, HG, o).then_inc(S["qd_done"], 1)

                def queries_lo(G, g):
                    dve.wait_ge(S["q_hi_done"], G + 1)
                    dve.tensor_tensor(q_lo[:, g], ps[:, 7, :].rearrange("p (a b) -> p a b", b=P),
                                      q_hi[:, g].bitcast(F32), ALU.subtract).then_inc(S["q_lo_done"], 1)

                def maximum(G, g, h, nk):
                    dve.wait_ge(S["s_ps"], START + HG * G + h + 1)
                    i_ = ps[:, 0:3, 0:GRP] if nk == NT else ps[:, 0:1, 0:P]
                    dve.tensor_reduce(nm[:, g, h:h + 1], i_, AX.XY, ALU.max, negate=True).then_inc(S["mx_done"], 1)

                def lo_(e, j):
                    dve.wait_ge(S["p_hi_done"], e + 1)
                    dve.tensor_tensor(p_lo[:, ring(j)], pr[:, ring(j)], p_hi[:, ring(j)].bitcast(F32),
                                      ALU.subtract).then_inc(S["p_lo_done"], 1)

                def reciprocals(G):
                    dve.wait_ge(S["sm_ps"], START + G + 1)
                    dve.reciprocal(rinv[:], ps[:, 2, GRP:GRP + HG]).then_inc(S["rv_done"], 1)

                def outputs(t, g, G):
                    dve.wait_ge(S["ot_cp"], G + 1)
                    o3 = z[:, t, ZQ + g * 256:ZQ + g * 256 + 256].rearrange("p (a b) -> p a b", b=HD)
                    dve.tensor_tensor(o3, o_s[:, 0:256].rearrange("p (a b) -> p a b", b=HD),
                                      ps[:, 7, :].rearrange("p (a b) -> p a b", b=P)[:, :, HD:P], ALU.add)
                    dve.drain()
                    dve.tensor_tensor(o3, o3, b2(rinv[:], HD), ALU.mult).then_inc(S["oy_done"], 1)

                def step(t, g, nk, pk, nn, prep):
                    G, E, A = counts(L, t, g)
                    for j in range(nk):
                        for key, h in SCORES_AT.items():
                            if nn and nk == NT and j == key - (h > 0):
                                maximum(G + 1, 1 - g, h, nn)
                        if j or pk:
                            lo_(E + j - 1, (j or pk) - 1)
                        if pk and j == min(1, nk - 1):
                            reciprocals(G - 1)
                        if nn and j == min(2, nk - 1):
                            queries_lo(G + 1, 1 - g)
                        if prep is not None and j in (0, 6):
                            queries(prep, g, j // 6)
                        if nn and nk == 1:
                            for h in range(HG):
                                maximum(G + 1, 1 - g, h, nn)
                        if pk and j == nk - 1:
                            outputs(t if g else t - 1, 1 - g, G - 1)

                for g in range(2):
                    queries(0, g)
                queries_lo(NG * L, 0)
                for h in range(HG):
                    maximum(NG * L, 0, h, NT)
                walk(dve, L, step)
                lo_(N_E * (L + 1) - 1, 0)
                reciprocals(NG * (L + 1) - 1)
                outputs(NS, 1, NG * (L + 1) - 1)
                phase(dve, L, 7)
                for t in range(NT):
                    dve.wait_ge(S["y_hi"], NT * L + t + 1)
                    for k in range(2):
                        r = (slice(None), slice(4 * k, 4 * k + 4), slice(t * P, (t + 1) * P))
                        ins = dve.tensor_tensor(lo[r], ps[:, 2 * (t % 3) + k, :].rearrange("p (a b) -> p a b", b=P),
                                                hi[r].bitcast(F32), ALU.subtract)
                    ins.then_inc(S["y_lo"], 1)
                phase(dve, L, 8)

                def residual(n, t):
                    k = 18 * L + 9 * n + t
                    g = int(t < NS)
                    dve.wait_ge(S["o_out"], START + k + 1)
                    dve.tensor_tensor(lnt[:, (n + t) % 2], ps[:, t % 3, :], gate[:, g, bass.ds(n * W, W)], ALU.mult)
                    dve.drain()
                    r = xr[:, t, bass.ds(n * W, W)]
                    dve.scalar_tensor_tensor(r, r, ALPHA, lnt[:, (n + t) % 2], ALU.mult, ALU.add).then_inc(S["xr_half"], 1)

                dve.wait_ge(S["ln_ld"], 16 * (13 * L + 7))
                own(dve)
                for t in range(NT - 1):
                    residual(0, t)
                split_lo(dve, L, 6)
                residual(0, NT - 1)
                for t in range(NT + 2):
                    if t < NT:
                        residual(1, t)
                        statistics(xr, t)
                    if t > 1:
                        offset(L, 0, xr, t - 2, lnb[:, 1], S["xr_done"])
                    if t >= NT - 1:
                        modulate(L, t + 1, 1, hf2, t - (NT - 1), 1)
                split_lo(dve, L, 7, range(RAW))
                for t in range(3, NT):
                    if t == 6:
                        split_lo(dve, L, 7, range(RAW, SLOTS))
                    modulate(L, NT + t, 1, hf2, t % 3, int(t < NS))
                phase(dve, L, 9)

                def hidden(i, b):
                    n = 12 * (NFF * L + i) + b
                    dve.wait_ge(S["r_done"], START + n + 1)
                    dve.tensor_tensor(fsq[:, b % 2], fr[:, b % 2], fr[:, b % 2], ALU.mult)
                    dve.drain()
                    r = (slice(None), b // 3, slice((b % 3) * GRP, (b % 3 + 1) * GRP))
                    dve.wait_ge(S["fhi_done"], n + 1)
                    dve.tensor_tensor(f_lo[r], fsq[:, b % 2], f_hi[r].bitcast(F32), ALU.subtract).then_inc(S["flo_done"], 1)

                def summed(i, b):
                    n = 18 * (NFF * L + i) + b
                    dve.wait_ge(S["f_ps"], START + n + 1)
                    a = acc[:, b // 2, (b % 2) * W:(b % 2 + 1) * W]
                    dve.tensor_tensor(a, a, ps[:, 3 + b % 3, :], ALU.add).then_inc(S["f_acc"], 1)

                dve.wait_ge(S["acc_zero"], L + 1)
                own(dve)
                def chunk(i):
                    for b in range(11):
                        hidden(i, b)
                    split_lo(dve, L, 2 * i + 8)
                    hidden(i, 11)

                with dve.Fori(0, NFF - 1) as i:
                    chunk(i)
                    for b in range(17):
                        summed(i, b)
                    split_lo(dve, L, 2 * i + 9)
                    summed(i, 17)
                    dve.drain()
                chunk(NFF - 1)
                for t in range(NT + 2):
                    if t < NT:
                        a = acc[:, t]
                        for n in range(2):
                            summed(NFF - 1, 2 * t + n)
                        dve.drain()
                        if t == 0:
                            dve.wait_ge(S["ln_ld"], 16 * (13 * L + 13))
                        dve.tensor_tensor(a, a, gate2[:, int(t < NS)], ALU.mult)
                        dve.drain()
                        dve.wait_ge(x1_ld[t // 3], 16 * (L + 1))
                        dve.scalar_tensor_tensor(a, x1t[:, t], ALPHA, a, ALU.mult, ALU.add)
                        statistics(acc, t)
                    if t > 1:
                        offset(L, 1, acc, t - 2, lnb2[:, 1], S["y_rdy"])
                split_lo(dve, L, 2 * NFF + 7)
                phase(dve, L, 10)

        @block.tensor
        def _(pe):
            for n in ("mod_ps", "u_ps", "m_tp", "m_D", "m_S", "m_num", "z_ps", "f_ps", "h_ps", "o_out", "s_ps", "pv_done", "ot_ps", "sm_ps", "w_used"):
                if n != "mod_ps":
                    pe.sem_inc(S[n], START)
            pe.wait_ge(S["const_ld"], 48)
            pe.wait_ge(S["mod_ready"], 1)
            own(pe)
            with pe.Fori(0, NL * 12 // 2) as i:
                for u in range(2):
                    pe.wait_ge(mod_w_ld[u], 16 * i + 16)
                    pe.wait_ge(S["mod_row"], START + 2 * i + u - 1)
                    for k in range(KT):
                        mm = pe.matmul(ps[0:2, u, :], sc[:, k, :], modw[:, u, k, :], start=(k == 0), stop=(k == KT - 1))
                    mm.then_inc(S["mod_ps"], 1)
            phase(pe, 0, -1)

            def product(out, a_hi, a_lo, b_hi, b_lo, first, last, used=None):
                mm = pe.matmul(out, a_hi, b_hi, start=first, stop=False)
                if used is not None:
                    mm.then_inc(used, 1)
                pe.matmul(out, a_hi, b_lo, start=False, stop=False)
                return pe.matmul(out, a_lo, b_hi, start=False, stop=last)

            def dense(L, g, t, bank, cols_, wait_w, last_tile, done):
                out = ps[:, bank, 0:cols_]
                a = slice(t * P, (t + 1) * P)
                for k in range(KT):
                    if wait_w:
                        pe.wait_ge(S["w_lo_done"], slot(L, g, k) + 1)
                    mm = product(out, hi[:, k, a], lo[:, k, a], w_hi[:, k, 0:cols_], w_lo[:, k, 0:cols_],
                                 k == 0, k == KT - 1, S["w_used"] if last_tile and k else None)
                mm.then_inc(done, 1)

            with pe.Fori(0, NL) as L:
                pe.wait_ge(S["mc_ld"], 32 * L + 32)
                own(pe)
                pe.transpose(ps[:, 7, 0:64], mod64[:, :], ident[0:64, 0:64]).then_inc(S["mc_ps"], 1)
                for t in range(NT):
                    if t % 3 == 0:
                        pe.wait_ge(x_ld[t // 3], 16)
                    pe.wait_ge(S["hf_done"], START + 2 * NT * L + t - 2)
                    for k in range(KT):
                        mm = pe.transpose(ps[:, 2 * (t % 3) + k // 4, (k % 4) * P:(k % 4 + 1) * P], acc[:, t, k * P:(k + 1) * P], ident[:])
                    mm.then_inc(S["xT_ps"], 1)
                phase(pe, L, 0)
                for g in range(3):
                    a = slice(g * GRP, (g + 1) * GRP)
                    for k in range(KT):
                        if g == 0:
                            pe.wait_ge(S["w_lo_done"], slot(L, 0, k) + 1)
                        mm = product(ps[:, 4 + g, 0:GRP], w_hi[:, k, 256:384], w_lo[:, k, 256:384], hi[:, k, a], lo[:, k, a],
                                     k == 0, k == KT - 1)
                    mm.then_inc(S["g_ps"], 1)
                for t in range(NT):
                    pe.wait_ge(S["z_done"], START + 45 * L + t - 2)
                    dense(L, 0, t, t % 3, 256, False, t == NT - 1, S["z_ps"])
                with pe.Fori(0, 4) as c:
                    for t in range(NT):
                        pe.wait_ge(S["z_done"], START + 45 * L + 9 * c + 9 + t - 2)
                        dense(L, c + 1, t, t % 3, W, t == 0, t == NT - 1, S["z_ps"])
                phase(pe, L, 1)
                pe.wait_ge(S["act_row"], 2 * L + 2)
                own(pe)
                for t in range(NT):
                    for q, r in enumerate((ri, rf, r_r, r_d)):
                        o = (t % 3) * 4 * ROWS + q * ROWS
                        pe.transpose(ps[:, t // 3, o:o + ROWS], r[:, t * P:(t + 1) * P], ident[0:ROWS, 0:ROWS])
                pe.wait_ge(S["ml_ld"], 48 * L + 48)
                for j in range(4):
                    mm = pe.matmul(ps[:, 3, j * NT:(j + 1) * NT], selc[0:ROWS, 8 + j], mrow[:, 4], start=True, stop=True)
                mm.then_inc(S["rt_ps"], 1)
                phase(pe, L, 2)

                def states(n, u):
                    pe.wait_ge(S["u_v"], NT * L + n + 1)
                    pe.wait_ge(S["u_kw"], NT * L + n + 1)
                    pe.wait_ge(S["u_done"], START + NT * L + n - 1)
                    for d in range(2):
                        for p_ in range(2):
                            mm = pe.matmul(ps[:, 2 * u + d, p_ * PV:(p_ + 1) * PV], kws[u][:, d, p_ * P:(p_ + 1) * P],
                                           vexts[u][:, 2 * p_:2 * p_ + 2, :].rearrange("p a b -> p (a b)"), start=True, stop=True)
                    mm.then_inc(S["u_ps"], 1)

                with pe.Fori(0, NS // 2) as i:
                    for u in range(2):
                        states(2 * i + u, u)
                states(NS, 0)
                phase(pe, L, 3)

                def weights_m(n):
                    N = NT * L + n
                    pe.wait_ge(S["m_w"], START + N)
                    pe.wait_ge(S["m_bd"], N + 1)
                    for d in range(2):
                        pe.matmul(ps[:, 2 + d, :], ones[0:ROWS], r_bd[:, d * MH:(d + 1) * MH].rearrange("p a b -> p (a b)"),
                                  start=True, stop=False)
                        mm = pe.matmul(ps[:, 2 + d, :], idr[:], mkr[:, d].unsqueeze(1).broadcast_to([P, MH, P]),
                                       start=False, stop=True)
                    mm.then_inc(S["m_D"], 1)
                    pe.wait_ge(S["m_st"], N + 1)
                    pe.wait_ge(S["m_qk"], START + N)
                    for p_ in range(2):
                        pe.transpose(ps[:, 0, p_ * P:(p_ + 1) * P], qs[:, p_ * P:(p_ + 1) * P], ident[:])
                        mm = pe.transpose(ps[:, 0, (2 + p_) * P:(3 + p_) * P], ks[:, p_ * P:(p_ + 1) * P], ident[:])
                    mm.then_inc(S["m_tp"], 1)

                def scores_m(n):
                    N = NT * L + n
                    pe.wait_ge(S["m_qk"], START + N + 1)
                    pe.wait_ge(S["m_sw"], START + N)
                    for p_ in range(2):
                        mm = pe.matmul(ps[:, 1, p_ * 256:(p_ + 1) * 256], kT[:, p_],
                                       qbd[:, p_].rearrange("p a b -> p (a b)"), start=True, stop=True)
                    mm.then_inc(S["m_S"], 1)

                def before_m(n, u, s_f, s_b):
                    pe.wait_ge(S["m_qk"], START + NT * L + n + 1)
                    pe.wait_ge(S["m_fin"], START + NT * L + n)
                    for d, s_ in enumerate((s_f, s_b)):
                        for p_ in range(2):
                            pe.matmul(ps[:, 6 + d, p_ * PV:(p_ + 1) * PV], qTs[u][:, p_], cs[:, s_, d, p_], start=True, stop=True)

                def within_m(n, u):
                    pe.wait_ge(S["m_sw"], START + NT * L + n + 1)
                    for d in range(2):
                        for h in range(MH):
                            mm = pe.matmul(ps[:, 4 + d, h * VE:(h + 1) * VE], wts[u][:, d, h], vexts[u][:, h], start=True, stop=True)
                    mm.then_inc(S["m_num"], 1)

                weights_m(0)
                scores_m(0)
                with pe.Fori(0, NS // 2) as i:
                    for u in range(2):
                        n = 2 * i + u
                        weights_m(n + 1)
                        before_m(n, u, n, NS - 1 - n)
                        scores_m(n + 1)
                        within_m(n, u)
                before_m(NS, 0, NT, NT)
                within_m(NS, 0)
                phase(pe, L, 4)
                for i in range(3):
                    pe.wait_ge(S["gm_vn"], START + 6 * L + (1, 2, 4)[i])
                    for u in range(3):
                        for g in range(4):
                            mm = pe.matmul(ps[:, 3 * (i % 2) + u, g * HD:(g + 1) * HD], wst[:, g],
                                           vn[:, 3 * i + u, g * HD:(g + 1) * HD], start=True, stop=True)
                    mm.then_inc(S["gm_ps"], 1)
                phase(pe, L, 5)

                pe.wait_ge(S["kd_done"], L + 1)
                own(pe)
                for n in range(10):
                    pe.wait_ge(S["k_lo"], START + 10 * L + n - 1)
                    for v in range(HKV):
                        mm = pe.transpose(ps[:, n % 2, v * P:(v + 1) * P], kd[:, n, v].rearrange("p a b -> p (a b)"), ident[:])
                    mm.then_inc(S["kd_ps"], 1)
                phase(pe, L, 6)

                def queries_T(G, g):
                    pe.wait_ge(S["qd_done"], G + 1)
                    pe.wait_ge(S["oy_done"], START + G - 2)
                    for h in range(HG):
                        mm = pe.transpose(ps[:, 7, h * P:(h + 1) * P], qd[:, g * HG + h].rearrange("p a b -> p (a b)"), ident[:])
                    mm.then_inc(S["q_ps"], 1)

                def scores(G, g, h, nk, pk):
                    pe.wait_ge(S["mx_done"], START + HG * G + h)
                    if h == 0:
                        pe.wait_ge(S["q_hi_done"], G + 1)
                        if pk:
                            pe.wait_ge(S["rv_done"], G - 1)
                    k0, w_ = (0, GRP) if nk == NT else (NT * P, P)
                    for b in range(3 if nk == NT else 1):
                        mm = pe.matmul(ps[:, b, 0:w_], q_hi[:, g, h], kst[:, g, k0 + b * w_:k0 + (b + 1) * w_], start=True, stop=True)
                    mm.then_inc(S["s_ps"], 1)

                def scores_T(G, E, g, j, nk, pk):
                    if j == 0:
                        pe.wait_ge(S["q_lo_done"], START + G + 1)
                        pe.wait_ge(S["dg_done"], HG * G + HG)
                    pe.wait_ge(S["ex_done"], START + (E + j if pk == 1 else E + j - 2))
                    key = kst[:, g, (j if nk == NT else NT) * P:(j + 1 if nk == NT else NT + 1) * P]
                    out = ps[:, 3 + j % 3, :]
                    pe.matmul(out, one_r[:], dg[:, g].rearrange("p a b -> p (a b)"), start=True, stop=False)
                    pe.matmul(out, key, q_hi[:, g].rearrange("p a b -> p (a b)"), start=False, stop=False)
                    pe.matmul(out, key, q_lo[:, g].rearrange("p a b -> p (a b)"), start=False, stop=True).then_inc(S["st_ps"], 1)

                def values(G, e, g, j, nk):
                    if j == 0:
                        pe.wait_ge(S["o_cp"], START + G)
                    pe.wait_ge(S["p_lo_done"], START + e + 1)
                    val = vst[:, g, j if nk == NT else NT]
                    pe.matmul(ps[:, 6, :], val, p_hi[:, ring(j)], start=(j == 0), stop=False)
                    mm = pe.matmul(ps[:, 6, :], val, p_lo[:, ring(j)], start=False, stop=(j == nk - 1))
                    mm.then_inc(S["pv_done"], 1)

                def sums(G, A, g, heads):
                    pe.wait_ge(S["mx_done"], START + heads)
                    pe.wait_ge(S["sum_done"], START + A)
                    for h in range(HG):
                        mm = pe.matmul(ps[:, 2, GRP + h:GRP + h + 1], psm[:, g, h * P:(h + 1) * P], ones[:, 0:1], start=True, stop=True)
                    mm.then_inc(S["sm_ps"], 1)

                def outputs_T(G, g):
                    pe.wait_ge(S["o_cp"], START + G + 1)
                    for h in range(HG):
                        mm = pe.transpose(ps[:, 7, h * P:(h + 1) * P], o_s[:, h * P:(h + 1) * P], ident[:])
                    mm.then_inc(S["ot_ps"], 1)

                def step(t, g, nk, pk, nn, prep):
                    G, E, A = counts(L, t, g)
                    last = list(range(max(pk - LAG, 0), pk))
                    for j in range(nk):
                        scores_T(G, E, g, j, nk, pk)
                        for k in (0, 1) if j == LAG + 1 else (j - LAG,) if j > LAG + 1 else ():
                            values(G, E + k, g, k, nk)
                        for k in last if nk == 1 else last[j:j + 1]:
                            values(G - 1, E - pk + k, 1 - g, k, pk)
                        if pk and j == min(1, nk - 1):
                            sums(G - 1, A, 1 - g, HG * (G + 1))
                        if nn and j == min(1, nk - 1):
                            queries_T(G + 1, 1 - g)
                        for key, h in SCORES_AT.items():
                            if nn and j == min(key, nk - 1):
                                scores(G + 1, 1 - g, h, nn, pk)
                        if pk and j == min(5, nk - 1):
                            if nn:
                                pe.wait_ge(S["q_lo_done"], START + G + 2)
                            outputs_T(G - 1, 1 - g)

                queries_T(NG * L, 0)
                for h in range(HG):
                    scores(NG * L, 0, h, NT, 0)
                walk(pe, L, step)
                values(NG * (L + 1) - 1, N_E * (L + 1) - 1, 1, 0, 1)
                sums(NG * (L + 1) - 1, N_A * (L + 1), 1, HG * NG * (L + 1))
                outputs_T(NG * (L + 1) - 1, 1)
                phase(pe, L, 7)
                for t in range(NT):
                    pe.wait_ge(S["y_lo"], START + NT * L + t - 2)
                    for k in range(KT):
                        c = (ZQ + k * P) if k < 4 else (ZOM + (k - 4) * P) if k < 6 else (ZUG + (k - 6) * P)
                        mm = pe.transpose(ps[:, 2 * (t % 3) + k // 4, (k % 4) * P:(k % 4 + 1) * P], z[:, t, c:c + P], ident[:])
                    mm.then_inc(S["yT_ps"], 1)
                phase(pe, L, 8)
                with pe.Fori(0, 2) as n:
                    for t in range(NT):
                        pe.wait_ge(S["xr_half"], START + 18 * L + 9 * n + t - 2)
                        dense(L, n + 5, t, t % 3, W, t == 0, t == NT - 1, S["o_out"])
                pe.wait_ge(S["xr_half"], START + 18 * (L + 1))
                for t in range(NT):
                    pe.wait_ge(S["xr_done"], NT * L + t + 1)
                    pe.wait_ge(S["hf_done"], START + 2 * NT * L + NT + t - 2)
                    for k in range(KT):
                        mm = pe.transpose(ps[:, 2 * (t % 3) + k // 4, (k % 4) * P:(k % 4 + 1) * P], xr[:, t, k * P:(k + 1) * P], ident[:])
                    mm.then_inc(S["xT_ps"], 1)
                phase(pe, L, 9)
                with pe.Fori(0, NFF) as i:
                    for b in range(12):
                        n = 12 * (NFF * L + i) + b
                        m, g = b // 3, b % 3
                        a = slice(g * GRP, (g + 1) * GRP)
                        pe.wait_ge(S["r_done"], START + n - 2)
                        for k in range(KT):
                            if b == 0:
                                pe.wait_ge(S["w_lo_done"], slot(L, 2 * i + 7, k) + 1)
                            mm = product(ps[:, g, 0:GRP], w_hi[:, k, m * P:(m + 1) * P], w_lo[:, k, m * P:(m + 1) * P],
                                         hi[:, k, a], lo[:, k, a], k == 0, k == KT - 1, S["w_used"] if b == 11 and k else None)
                        mm.then_inc(S["h_ps"], 1)
                    for b in range(18):
                        n = 18 * (NFF * L + i) + b
                        t, hf_ = b // 2, b % 2
                        a = slice(t * P, (t + 1) * P)
                        if b in (0, 6, 12):
                            pe.wait_ge(S["flo_done"], START + 12 * (NFF * L + i) + 10 + b // 6)
                        pe.wait_ge(S["f_acc"], START + n - 2)
                        for m in range(4):
                            if t == 0:
                                pe.wait_ge(S["w_lo_done"], slot(L, 2 * i + 8, 4 * hf_ + m) + 1)
                            mm = product(ps[:, 3 + b % 3, :], f_hi[:, m, a], f_lo[:, m, a], w_hi[:, 4 * hf_ + m, :], w_lo[:, 4 * hf_ + m, :],
                                         m == 0, m == 3, S["w_used"] if t == NT - 1 and (m or hf_) else None)
                        mm.then_inc(S["f_ps"], 1)
                phase(pe, L, 10)


_INS = ["x_in", "cond", "w_mod", "b_mod", "w_slots", "consts", "rope", "cache_k", "cache_v", "state0", "row_in",
        "qk_g", "gln", "ws_t", "bs_t", "ln_gb"]
_OUTS = [(NT, P, D), (NL, P, P), (NL, P, P), (NL, 2, MH, HD, HD), (NL, 2, MH, HD, 1), (NL, 2, MH, 1)]


def layout(x_prompt, x_sample, c, cache_attn_k, cache_attn_v, state_mlstm_C, state_mlstm_n, state_mlstm_m,
           c_ctx, w_mod, b_mod, w_in, q_norm_g, k_norm_g, mlstm_gate_b, gmlp_ln_g, gmlp_ln_b, gmlp_ws, gmlp_bs,
           w_out, ln1_g, ln1_b, w_ff1, w_ff2, ln2_g, ln2_b):
    f = np.float32
    a = {k: np.asarray(v) for k, v in locals().items() if k != "f"}
    out = {}
    out["x_in"] = np.concatenate([a["x_sample"].reshape(NS, P, D), a["x_prompt"].reshape(1, P, D)])
    out["cond"] = np.stack([a["c_ctx"].reshape(KT, P), a["c"].reshape(KT, P)], -1).transpose(1, 0, 2)
    out["w_mod"] = a["w_mod"].reshape(NL, KT, P, 12, W).transpose(0, 3, 2, 1, 4).reshape(NL * 12, P, KT, W)
    out["b_mod"] = np.broadcast_to(a["b_mod"].reshape(1, NL * 12, W), (2, NL * 12, W))
    o = np.cumsum([0, 512, 128, 128, 256, 256, 256, 256, 16, 256, 256])
    qa, ka, va, qm, km, vm, om, gm, ug, vg = (a["w_in"][:, :, o[i]:o[i + 1]] for i in range(10))
    first = np.zeros((NL, D, W), f)
    first[:, :, 0:256] = ug
    for kind, at in ((0, 256), (2, 256 + 32), (1, 256 + 64), (3, 256 + 96)):
        first[:, :, at:at + MH] = gm[:, :, kind * MH:(kind + 1) * MH]
    slots = np.zeros(((NL * GROUPS + 1) * SLOTS, P, W), f)
    for l in range(NL):
        groups = [first[l], np.concatenate([qm[l], km[l]], -1), np.concatenate([vm[l], om[l]], -1), qa[l],
                  np.concatenate([ka[l], va[l], vg[l]], -1), a["w_out"][l][:, :W], a["w_out"][l][:, W:]]
        groups = [g.reshape(KT, P, W) for g in groups]
        for i in range(NFF):
            groups.append(a["w_ff1"][l][:, i * HC:(i + 1) * HC].reshape(KT, P, W))
            w2 = a["w_ff2"][l][i * HC:(i + 1) * HC].reshape(HC // P, P, 2, W)
            groups.append(w2.transpose(2, 0, 1, 3).reshape(SLOTS, P, W))
        for g, v in enumerate(groups):
            s = (l * GROUPS + g) * SLOTS
            slots[s:s + SLOTS] = v
    out["w_slots"] = slots
    out["consts"] = constants()
    out["rope"] = rope_tables()
    out["cache_k"] = a["cache_attn_k"].reshape(NL, P, P)
    out["cache_v"] = a["cache_attn_v"].reshape(NL, P, P)
    s0 = np.zeros((NL, 2, HD, 2, 2, 2, VE), f)
    C, n = a["state_mlstm_C"][0], a["state_mlstm_n"][0]
    for h in range(MH):
        s0[:, h % 2, :, :, h // 2, h % 2, 0:HD] = C[:, :, h].transpose(0, 2, 1, 3)
        s0[:, h % 2, :, :, h // 2, h % 2, HD] = n[:, :, h].transpose(0, 2, 1)
    out["state0"] = s0.reshape(NL, P, 2, 2, PV)
    r = np.zeros((NL, ROWS, 3), f)
    gb, m = a["mlstm_gate_b"], a["state_mlstm_m"][0]
    for d in range(2):
        r[:, 32 * d:32 * d + MH, 0] = gb[:, 2 * d]
        r[:, 32 * d:32 * d + MH, 1] = gb[:, 2 * d + 1]
        r[:, 32 * d:32 * d + MH, 2] = m[:, d]
    out["row_in"] = r

    def rows(v):
        return np.broadcast_to(v[:, None], (NL, P, *v.shape[1:]))
    out["qk_g"] = rows(np.stack([a["q_norm_g"], a["k_norm_g"]], 1))
    out["gln"] = rows(np.stack([a["gmlp_ln_g"], a["gmlp_ln_b"]], 1))
    out["ws_t"] = a["gmlp_ws"].transpose(0, 3, 1, 2)
    out["bs_t"] = a["gmlp_bs"].transpose(0, 2, 1)
    out["ln_gb"] = np.stack([a["ln1_g"], a["ln1_b"], a["ln2_g"], a["ln2_b"]], 1)
    return {k: np.ascontiguousarray(out[k]) for k in _INS}


def program(nc, arrays):
    args = [nc.dram_tensor(f"in_{n}", v.shape, F32, kind="ExternalInput").ap() for n, v in arrays.items()]
    args += [nc.dram_tensor(f"out_{i}", s, F32, kind="ExternalOutput").ap() for i, s in enumerate(_OUTS)]
    build(nc, *args)


def kernel(**inputs):
    import concourse.bacc as bacc
    from concourse.bass_utils import run_bass_kernel_spmd
    arrays = layout(**inputs)
    nc = bacc.Bacc("TRN2", target_bir_lowering=False, num_devices=1)
    program(nc, arrays)
    r = run_bass_kernel_spmd(nc, [{f"in_{n}": v for n, v in arrays.items()}], core_ids=[0])
    y, k, v, c, n, m = (r.results[0][f"out_{i}"] for i in range(len(_OUTS)))
    return (y[NS:NT].reshape(1, SEQ, D), y[0:NS].reshape(1, DEC_SEQ, D),
            k.reshape(1, NL, SEQ, HKV, HD), v.reshape(1, NL, SEQ, HKV, HD),
            c.reshape(1, NL, 2, MH, HD, HD), n.reshape(1, NL, 2, MH, HD), m.reshape(1, NL, 2, MH))
```
